# Optimizing a Trainium2 kernel written in Bass

```python
import jax
import jax.numpy as jnp
from jax import lax
import numpy as np
import math
import jax, jax.numpy as jnp

D_MODEL = 1024
BATCH = 1
SEQ = 256
DEPTH = 2

GRID_W = 64
CTX_LEN = 256

N_HEADS = 8
N_KV_HEADS = 2
HEAD_DIM = 128
Q_PER_KV = N_HEADS // N_KV_HEADS
ROPE_THETA = 10000.0
Q_BLOCK = 128

GLA_HEADS = 4
GLA_DK = D_MODEL // 2 // GLA_HEADS
GLA_DV = D_MODEL // GLA_HEADS
GLA_RANK = 16
GLA_TAU = 16.0
GLA_CHUNK = 64

CONV_CH = D_MODEL
CONV_WIDTH = 31

D_FF = -(-8 * D_MODEL // (3 * 256)) * 256

ALPHA = (2.0 * DEPTH) ** 0.25
BETA = (8.0 * DEPTH) ** -0.25
NORM_EPS = 1e-6

ATT_Q = N_HEADS * HEAD_DIM
ATT_KV = N_KV_HEADS * HEAD_DIM
GLA_K = GLA_HEADS * GLA_DK
GLA_V = GLA_HEADS * GLA_DV
N_BRANCH = 3
MEM_SPLITS = (ATT_KV, ATT_KV, GLA_K, GLA_V, 2 * GLA_RANK)
REST_SPLITS = (ATT_Q, GLA_K, GLA_V, 2 * CONV_CH, N_BRANCH * D_MODEL)
MEM_COLS = sum(MEM_SPLITS)
IN_COLS = MEM_COLS + sum(REST_SPLITS)


def _split(a, sizes):
    return jnp.split(a, np.cumsum(sizes)[:-1].tolist(), axis=-1)

def _layernorm(x, g=None, b=None):
    xf = x.astype(jnp.float32)
    xc = xf - jnp.mean(xf, -1, keepdims=True)
    y = xc * lax.rsqrt(jnp.mean(xc * xc, -1, keepdims=True) + NORM_EPS)
    if g is not None:
        y = y * g.astype(jnp.float32) + b.astype(jnp.float32)
    return y.astype(x.dtype)

def _rmsnorm(x, g):
    xf = x.astype(jnp.float32)
    y = xf * lax.rsqrt(jnp.mean(xf * xf, -1, keepdims=True) + NORM_EPS)
    return (y * g.astype(jnp.float32)).astype(x.dtype)

def _modulate(x, shift, scale):
    return _layernorm(x) * (1.0 + scale) + shift

def _post(x, f, gate, g, b):
    return _layernorm(ALPHA * x + gate * f, g, b)

def _heads(a, n):
    B, L, _ = a.shape
    return a.reshape(B, L, n, -1).transpose(0, 2, 1, 3)

def _flip(a):
    return a[:, :, ::-1]

def _axial_rope(rows):
    t = jnp.arange(rows * GRID_W)
    row = (t // GRID_W).astype(jnp.float32)
    col = (t % GRID_W).astype(jnp.float32)
    half = HEAD_DIM // 2
    inv = ROPE_THETA ** (-jnp.arange(0, half, 2, dtype=jnp.float32) / half)
    ang = jnp.concatenate([row[:, None] * inv, col[:, None] * inv], axis=-1)
    return jnp.cos(ang), jnp.sin(ang)

def _apply_rope(x, cos, sin):
    xf = x.astype(jnp.float32)
    x1, x2 = xf[..., 0::2], xf[..., 1::2]
    y = jnp.stack([x1 * cos - x2 * sin, x1 * sin + x2 * cos], axis=-1)
    return y.reshape(x.shape).astype(x.dtype)

def _sdpa(q, k, v):
    s = jnp.einsum('bkgqd,bkld->bkgql', q, k, preferred_element_type=jnp.float32) * (HEAD_DIM ** -0.5)
    p = jax.nn.softmax(s, axis=-1)
    return jnp.einsum('bkgql,bkld->bkgqd', p.astype(v.dtype), v)

def _attend_blocks(q, k_all, v_all):
    B, Hk, G, S, Dh = q.shape
    nb = S // Q_BLOCK
    qb = jnp.moveaxis(q.reshape(B, Hk, G, nb, Q_BLOCK, Dh), 3, 0)
    o = lax.map(lambda blk: _sdpa(blk, k_all, v_all), qb)
    return jnp.moveaxis(o, 0, 3).reshape(B, Hk, G, S, Dh)

def _gla_log_gates(glr, w_a2, b_a):
    B, L, _ = glr.shape
    z = jnp.einsum('blnr,nrk->nblk', glr.reshape(B, L, 2, GLA_RANK), w_a2) + b_a[:, None, None, :]
    lg = jax.nn.log_sigmoid(z.astype(jnp.float32)) / GLA_TAU
    lg = lg.reshape(2, B, L, GLA_HEADS, GLA_DK).transpose(0, 1, 3, 2, 4)
    return lg[0], lg[1]

def _gla_scan(q, k, v, logg, s0):
    B, H, L, dk = q.shape
    dv = v.shape[-1]
    n = L // GLA_CHUNK

    def chunks(a):
        a = a.astype(jnp.float32)
        return a.reshape(B, H, n, GLA_CHUNK, a.shape[-1]).transpose(2, 0, 1, 3, 4)

    lower = jnp.tril(jnp.ones((GLA_CHUNK, GLA_CHUNK), dtype=bool))[:, :, None]

    def step(s, inp):
        qc, kc, vc, gc = inp
        b = jnp.cumsum(gc, axis=2)
        rel = jnp.where(lower, b[:, :, :, None, :] - b[:, :, None, :, :], -jnp.inf)
        a = jnp.einsum('bhid,bhjd,bhijd->bhij', qc, kc, jnp.exp(rel))
        o = jnp.einsum('bhid,bhde->bhie', qc * jnp.exp(b), s) + jnp.einsum('bhij,bhje->bhie', a, vc)
        b_end = b[:, :, -1:, :]
        s = jnp.exp(b_end[:, :, 0, :, None]) * s + jnp.einsum('bhjd,bhje->bhde', kc * jnp.exp(b_end - b), vc)
        return s, o

    s_end, o = lax.scan(step, s0, (chunks(q), chunks(k), chunks(v), chunks(logg)))
    return o.transpose(1, 2, 0, 3, 4).reshape(B, H, L, dv).astype(v.dtype), s_end

def _gla_final_state(k, v, logg):
    b = jnp.cumsum(logg, axis=2)
    w = jnp.exp(b[:, :, -1:, :] - b)
    return jnp.einsum('bhld,bhle->bhde', k.astype(jnp.float32) * w, v.astype(jnp.float32))

def _gla_bidir(qg, kg, vg, gf, gb, s_f, s_b):
    o_f, s_f_end = _gla_scan(qg, kg, vg, gf, s_f)
    o_b, s_b_end = _gla_scan(_flip(qg), _flip(kg), _flip(vg), _flip(gb), s_b)
    return o_f + _flip(o_b), s_f_end, s_b_end

def _mem_parts(pm, p):
    k, v, kg, vg, glr = _split(pm, MEM_SPLITS)
    k = _rmsnorm(_heads(k, N_KV_HEADS), p['k_norm'])
    v = _heads(v, N_KV_HEADS)
    gf, gb = _gla_log_gates(glr, p['gla_w_a2'], p['gla_b_a'])
    return k, v, _heads(kg, GLA_HEADS), _heads(vg, GLA_HEADS), gf, gb

def _rest_parts(pr, p):
    q, qg, r, glu, gates = _split(pr, REST_SPLITS)
    B, L, _ = q.shape
    q = _rmsnorm(q.reshape(B, L, N_KV_HEADS, Q_PER_KV, HEAD_DIM), p['q_norm']).transpose(0, 2, 3, 1, 4)
    qg = _heads(qg, GLA_HEADS) * (GLA_DK ** -0.5)
    return q, qg, r, glu, gates

def _conv_module(glu, p):
    a, g = jnp.split(glu, 2, axis=-1)
    y = a * jax.nn.sigmoid(g)
    pad = CONV_WIDTH // 2
    y = lax.conv_general_dilated(y, p['conv_w_dw'].astype(y.dtype), (1,), [(pad, pad)],
                                 dimension_numbers=('NWC', 'WIO', 'NWC'),
                                 feature_group_count=CONV_CH) + p['conv_b_dw']
    y = jax.nn.silu(_layernorm(y, p['conv_ln_g'], p['conv_ln_b']))
    return y @ p['w_conv_o']

def _merge(o_att, o_gla, r, glu, gates, p):
    B, L, _ = r.shape
    y_att = o_att.transpose(0, 3, 1, 2, 4).reshape(B, L, ATT_Q) @ p['w_att_o']
    o_gla = _rmsnorm(o_gla, p['gla_norm']).transpose(0, 2, 1, 3).reshape(B, L, GLA_V)
    y_gla = (o_gla * jax.nn.silu(r)) @ p['w_gla_o']
    y_conv = _conv_module(glu, p)
    g_att, g_gla, g_conv = jnp.split(jax.nn.sigmoid(gates), N_BRANCH, axis=-1)
    return (g_att * y_att + g_gla * y_gla + g_conv * y_conv) @ p['w_out']

def _context_mixer(h, p):
    proj = h @ p['w_in']
    k, v, kg, vg, gf, gb = _mem_parts(proj[..., :MEM_COLS], p)
    q, qg, r, glu, gates = _rest_parts(proj[..., MEM_COLS:], p)
    o_att = _sdpa(q, k, v)
    zero = jnp.zeros(kg.shape[:2] + (GLA_DK, GLA_DV), jnp.float32)
    o_gla, s_f, s_b = _gla_bidir(qg, kg, vg, gf, gb, zero, zero)
    return _merge(o_att, o_gla, r, glu, gates, p), (k, v, s_f, s_b)

def _context_memory(h, p):
    k, v, kg, vg, gf, gb = _mem_parts(h @ p['w_in'][:, :MEM_COLS], p)
    s_f = _gla_final_state(kg, vg, gf)
    s_b = _gla_final_state(_flip(kg), _flip(vg), _flip(gb))
    return k, v, s_f, s_b

def _latent_mixer(h, mem, cos, sin, p):
    proj = h @ p['w_in']
    k, v, kg, vg, gf, gb = _mem_parts(proj[..., :MEM_COLS], p)
    q, qg, r, glu, gates = _rest_parts(proj[..., MEM_COLS:], p)
    k_ctx, v_ctx, s_f, s_b = mem
    k_all = jnp.concatenate([_apply_rope(k, cos, sin), k_ctx], axis=2)
    v_all = jnp.concatenate([v, v_ctx], axis=2)
    o_att = _attend_blocks(_apply_rope(q, cos, sin), k_all, v_all)
    o_gla, _, _ = _gla_bidir(qg, kg, vg, gf, gb, s_f, s_b)
    return _merge(o_att, o_gla, r, glu, gates, p)

def _ffn(h, p):
    return (jax.nn.silu(h @ p['w_ff_gate']) * (h @ p['w_ff_up'])) @ p['w_ff_down']

def first_inputs(seed: int = 0) -> dict:
    key = jax.random.key(seed)
    ks = jax.random.split(key, 27)

    def nrm(i, shape, scale):
        return jax.random.normal(ks[i], shape, jnp.float32) * scale

    D = D_MODEL
    L = DEPTH
    return {
        'x': nrm(0, (BATCH, SEQ, D), 1.0),
        'c': nrm(1, (BATCH, D), 1.0),
        'ctx': nrm(2, (BATCH, CTX_LEN, D), 1.0),
        'c_ctx': nrm(3, (D,), 1.0),
        'w_ada': nrm(4, (L, D, 6 * D), 0.3 * D ** -0.5),
        'b_ada': nrm(5, (L, 6 * D), 0.02),
        'w_in': nrm(6, (L, D, IN_COLS), D ** -0.5),
        'q_norm': 1.0 + nrm(7, (L, HEAD_DIM), 0.02),
        'k_norm': 1.0 + nrm(8, (L, HEAD_DIM), 0.02),
        'w_att_o': nrm(9, (L, ATT_Q, D), ATT_Q ** -0.5),
        'gla_w_a2': nrm(10, (L, 2, GLA_RANK, GLA_K), GLA_RANK ** -0.5),
        'gla_b_a': nrm(11, (L, 2, GLA_K), 0.5),
        'gla_norm': 1.0 + nrm(12, (L, GLA_DV), 0.02),
        'w_gla_o': nrm(13, (L, GLA_V, D), GLA_V ** -0.5),
        'conv_w_dw': nrm(14, (L, CONV_WIDTH, 1, CONV_CH), CONV_WIDTH ** -0.5),
        'conv_b_dw': nrm(15, (L, CONV_CH), 0.02),
        'conv_ln_g': 1.0 + nrm(16, (L, CONV_CH), 0.02),
        'conv_ln_b': nrm(17, (L, CONV_CH), 0.02),
        'w_conv_o': nrm(18, (L, CONV_CH, D), CONV_CH ** -0.5),
        'w_out': nrm(19, (L, D, D), BETA * D ** -0.5),
        'ln1_g': 1.0 + nrm(20, (L, D), 0.02),
        'ln1_b': nrm(21, (L, D), 0.02),
        'w_ff_gate': nrm(22, (L, D, D_FF), D ** -0.5),
        'w_ff_up': nrm(23, (L, D, D_FF), D ** -0.5),
        'w_ff_down': nrm(24, (L, D_FF, D), BETA * D_FF ** -0.5),
        'ln2_g': 1.0 + nrm(25, (L, D), 0.02),
        'ln2_b': nrm(26, (L, D), 0.02),
    }

def first_block(x, c, ctx, c_ctx, w_ada, b_ada, w_in, q_norm, k_norm, w_att_o, gla_w_a2, gla_b_a,
              gla_norm, w_gla_o, conv_w_dw, conv_b_dw, conv_ln_g, conv_ln_b, w_conv_o, w_out,
              ln1_g, ln1_b, w_ff_gate, w_ff_up, w_ff_down, ln2_g, ln2_b):
    rows = x.shape[1] // GRID_W
    cos, sin = _axial_rope(rows)
    silu_c = jax.nn.silu(c)
    silu_cc = jax.nn.silu(c_ctx)
    xc = ctx
    for l in range(DEPTH):
        p = {'w_in': w_in[l], 'q_norm': q_norm[l], 'k_norm': k_norm[l], 'w_att_o': w_att_o[l],
             'gla_w_a2': gla_w_a2[l], 'gla_b_a': gla_b_a[l], 'gla_norm': gla_norm[l],
             'w_gla_o': w_gla_o[l], 'conv_w_dw': conv_w_dw[l], 'conv_b_dw': conv_b_dw[l],
             'conv_ln_g': conv_ln_g[l], 'conv_ln_b': conv_ln_b[l], 'w_conv_o': w_conv_o[l],
             'w_out': w_out[l], 'w_ff_gate': w_ff_gate[l], 'w_ff_up': w_ff_up[l],
             'w_ff_down': w_ff_down[l]}
        last = l == DEPTH - 1
        mod = (silu_c @ w_ada[l] + b_ada[l])[:, None, :]
        sh1, sc1, g1, sh2, sc2, g2 = jnp.split(mod, 6, axis=-1)
        n_cm = 2 if last else 6
        mod_c = jnp.split(silu_cc @ w_ada[l][:, :n_cm * D_MODEL] + b_ada[l][:n_cm * D_MODEL], n_cm)
        hc = _modulate(xc, mod_c[0], mod_c[1])
        if last:
            mem = _context_memory(hc, p)
        else:
            yc, mem = _context_mixer(hc, p)
            xc = _post(xc, yc, mod_c[2], ln1_g[l], ln1_b[l])
            xc = _post(xc, _ffn(_modulate(xc, mod_c[3], mod_c[4]), p), mod_c[5], ln2_g[l], ln2_b[l])
        x = _post(x, _latent_mixer(_modulate(x, sh1, sc1), mem, cos, sin, p), g1, ln1_g[l], ln1_b[l])
        x = _post(x, _ffn(_modulate(x, sh2, sc2), p), g2, ln2_g[l], ln2_b[l])
    return x


D_MIX = D_MODEL
N_MIXERS = 4
D_GROUP = D_MIX // N_MIXERS

MLA_HEADS = 4
MLA_Q_RANK = D_MODEL // 4
MLA_KV_RANK = D_MODEL // 8
MLA_NOPE = 64
MLA_ROPE = 32
MLA_V = D_GROUP // MLA_HEADS

CONV_WIDTH_2 = 3
CONV_CH_2 = D_GROUP

POOL_WINDOWS = (2, 4, 8, 16)
POOL_GROUPS = len(POOL_WINDOWS)
POOL_CH = D_GROUP // POOL_GROUPS

SWA_HEADS = 4
SWA_KV_HEADS = 2
SWA_HEAD_DIM = D_GROUP // SWA_HEADS
SWA_WINDOW = 128

BLOCK = 128

D_FF_2 = -(-8 * D_MODEL // (3 * 256)) * 256

RMS_EPS = 1e-6

IN_SPLITS = (MLA_Q_RANK, MLA_KV_RANK, MLA_ROPE,
             CONV_CH_2, CONV_CH_2, CONV_CH_2,
             D_GROUP,
             SWA_HEADS * SWA_HEAD_DIM,
             SWA_KV_HEADS * SWA_HEAD_DIM,
             SWA_KV_HEADS * SWA_HEAD_DIM)
D_IN = sum(IN_SPLITS)


def _split_points():
    pts, acc = [], 0
    for w in IN_SPLITS[:-1]:
        acc += w
        pts.append(acc)
    return pts

def _alibi_slopes(n):
    return np.asarray([2.0 ** (-8.0 * (i + 1) / n) for i in range(n)], dtype=np.float32)

def rmsnorm(x, g):
    xf = x.astype(jnp.float32)
    y = xf * lax.rsqrt(jnp.mean(xf * xf, axis=-1, keepdims=True) + RMS_EPS)
    return (y * g.astype(jnp.float32)).astype(x.dtype)

def rope_tables(seq, dim, dtype):
    inv = 1.0 / (ROPE_THETA ** (jnp.arange(0, dim, 2, dtype=jnp.float32) / dim))
    ang = jnp.arange(seq, dtype=jnp.float32)[:, None] * inv[None, :]
    return jnp.cos(ang).astype(dtype), jnp.sin(ang).astype(dtype)

def apply_rope(x, cos, sin):
    x1, x2 = jnp.split(x, 2, axis=-1)
    c = cos[:, None, :]
    s = sin[:, None, :]
    return jnp.concatenate([x1 * c - x2 * s, x1 * s + x2 * c], axis=-1)

def mla_attention(c_q, c_kv, k_r, q_norm_g, kv_norm_g, w_uq, w_ukv, cos, sin):
    b, s, _ = c_q.shape
    dqk = MLA_NOPE + MLA_ROPE
    q = (rmsnorm(c_q, q_norm_g) @ w_uq).reshape(b, s, MLA_HEADS, dqk)
    q_nope, q_rot = q[..., :MLA_NOPE], q[..., MLA_NOPE:]
    q_rot = apply_rope(q_rot, cos, sin)
    kv = (rmsnorm(c_kv, kv_norm_g) @ w_ukv).reshape(b, s, MLA_HEADS, MLA_NOPE + MLA_V)
    k_nope, v = kv[..., :MLA_NOPE], kv[..., MLA_NOPE:]
    k_rot = apply_rope(k_r[:, :, None, :], cos, sin)
    k = jnp.concatenate([k_nope, jnp.broadcast_to(k_rot, (b, s, MLA_HEADS, MLA_ROPE))], axis=-1)
    q = jnp.concatenate([q_nope, q_rot], axis=-1) * (1.0 / math.sqrt(dqk))
    nb = s // BLOCK
    qb = q.reshape(b, nb, BLOCK, MLA_HEADS, dqk).transpose(1, 0, 2, 3, 4)
    key_pos = jnp.arange(s)

    def one_block(args):
        q_blk, i = args
        sc = jnp.einsum('bqhd,bkhd->bhqk', q_blk, k).astype(jnp.float32)
        q_pos = i * BLOCK + jnp.arange(BLOCK)
        causal = key_pos[None, :] <= q_pos[:, None]
        sc = jnp.where(causal[None, None], sc, -jnp.inf)
        p = jax.nn.softmax(sc, axis=-1).astype(v.dtype)
        return jnp.einsum('bhqk,bkhd->bqhd', p, v)

    out = lax.map(one_block, (qb, jnp.arange(nb)))
    return out.transpose(1, 0, 2, 3, 4).reshape(b, s, MLA_HEADS * MLA_V)

def short_gated_conv(gate_b, gate_c, u, conv_w):
    z = gate_c * u
    y = lax.conv_general_dilated(
        z, conv_w[:, None, :].astype(z.dtype), window_strides=(1,),
        padding=[(CONV_WIDTH_2 - 1, 0)], dimension_numbers=('NWC', 'WIO', 'NWC'),
        feature_group_count=CONV_CH_2)
    return gate_b * y

def multiscale_pool(u, pool_w, pool_scale):
    b, s, _ = u.shape
    uf = u.astype(jnp.float32)
    cs = jnp.cumsum(uf, axis=1)
    pos = jnp.arange(s)
    outs = []
    for g, w in enumerate(POOL_WINDOWS):
        cs_g = cs[:, :, g * POOL_CH:(g + 1) * POOL_CH]
        lag = jnp.pad(cs_g, ((0, 0), (w, 0), (0, 0)))[:, :s]
        count = jnp.minimum(pos + 1, w).astype(jnp.float32)[None, :, None]
        outs.append((cs_g - lag) / count)
    pooled = jnp.stack(outs, axis=2) - uf.reshape(b, s, POOL_GROUPS, POOL_CH)
    mixed = jnp.einsum('bsgc,gcd->bsgd', pooled.astype(u.dtype), pool_w)
    return mixed.reshape(b, s, D_GROUP) * pool_scale

def swa_sink_attention(q, k, v, sinks, slopes):
    b, s, _, hd = q.shape
    grp = SWA_HEADS // SWA_KV_HEADS
    nb = s // BLOCK
    qb = q.reshape(b, nb, BLOCK, SWA_KV_HEADS, grp, hd)
    kb = k.reshape(b, nb, BLOCK, SWA_KV_HEADS, hd)
    vb = v.reshape(b, nb, BLOCK, SWA_KV_HEADS, hd)

    def with_prev(t):
        prev = jnp.pad(t, ((0, 0), (1, 0), (0, 0), (0, 0), (0, 0)))[:, :nb]
        return jnp.concatenate([prev, t], axis=2)

    kk, vv = with_prev(kb), with_prev(vb)
    sc = jnp.einsum('bnqkgd,bnskd->bnkgqs', qb, kk).astype(jnp.float32) * (1.0 / math.sqrt(hd))
    blk = jnp.arange(nb)[:, None] * BLOCK
    q_pos = blk + jnp.arange(BLOCK)[None, :]
    k_pos = blk - BLOCK + jnp.arange(2 * BLOCK)[None, :]
    dist = q_pos[:, :, None] - k_pos[:, None, :]
    valid = (dist >= 0) & (dist < SWA_WINDOW) & (k_pos[:, None, :] >= 0)
    sl = jnp.asarray(slopes).reshape(SWA_KV_HEADS, grp)
    bias = -sl[None, None, :, :, None, None] * dist.astype(jnp.float32)[None, :, None, None, :, :]
    sc = jnp.where(valid[None, :, None, None], sc + bias, -jnp.inf)
    sink = jnp.broadcast_to(
        sinks.astype(jnp.float32).reshape(SWA_KV_HEADS, grp)[None, None, :, :, None, None],
        sc.shape[:-1] + (1,))
    p = jax.nn.softmax(jnp.concatenate([sc, sink], axis=-1), axis=-1)[..., :-1].astype(v.dtype)
    out = jnp.einsum('bnkgqs,bnskd->bnqkgd', p, vv)
    return out.reshape(b, s, SWA_HEADS * hd)

def second_inputs(seed: int = 0) -> dict:
    key = jax.random.key(seed)
    ks = jax.random.split(key, 17)
    f32 = jnp.float32

    def dense(k, shape, fan_in):
        return jax.random.normal(k, shape, f32) * fan_in ** -0.5

    def gain(k, shape):
        return 1.0 + 0.05 * jax.random.normal(k, shape, f32)

    return {
        "x": jax.random.normal(ks[0], (BATCH, SEQ, D_MODEL), f32),
        "attn_norm": gain(ks[1], (DEPTH, D_MODEL)),
        "w_in": dense(ks[2], (DEPTH, D_MODEL, D_IN), D_MODEL),
        "mla_q_norm": gain(ks[3], (DEPTH, MLA_Q_RANK)),
        "w_uq": dense(ks[4], (DEPTH, MLA_Q_RANK, MLA_HEADS * (MLA_NOPE + MLA_ROPE)), MLA_Q_RANK),
        "mla_kv_norm": gain(ks[5], (DEPTH, MLA_KV_RANK)),
        "w_ukv": dense(ks[6], (DEPTH, MLA_KV_RANK, MLA_HEADS * (MLA_NOPE + MLA_V)), MLA_KV_RANK),
        "conv_w": dense(ks[7], (DEPTH, CONV_WIDTH_2, CONV_CH_2), CONV_WIDTH_2),
        "pool_w": dense(ks[8], (DEPTH, POOL_GROUPS, POOL_CH, POOL_CH), POOL_CH),
        "pool_scale": gain(ks[9], (DEPTH, D_GROUP)),
        "swa_sinks": 0.5 * jax.random.normal(ks[10], (DEPTH, SWA_HEADS), f32),
        "mix_norm": gain(ks[11], (DEPTH, D_MIX)),
        "w_o": dense(ks[12], (DEPTH, D_MIX, D_MODEL), D_MIX),
        "ffn_norm": gain(ks[13], (DEPTH, D_MODEL)),
        "w_gate_up": dense(ks[14], (DEPTH, D_MODEL, 2 * D_FF_2), D_MODEL),
        "w_down": dense(ks[15], (DEPTH, D_FF_2, D_MODEL), D_FF_2),
        "final_norm": gain(ks[16], (D_MODEL,)),
    }

def second_block(x, attn_norm, w_in, mla_q_norm, w_uq, mla_kv_norm, w_ukv, conv_w, pool_w,
              pool_scale, swa_sinks, mix_norm, w_o, ffn_norm, w_gate_up, w_down, final_norm):
    b, s, _ = x.shape
    cos, sin = rope_tables(s, MLA_ROPE, x.dtype)
    slopes = _alibi_slopes(SWA_HEADS)
    pts = _split_points()
    for l in range(DEPTH):
        h = rmsnorm(x, attn_norm[l])
        proj = h @ w_in[l]
        (c_q, c_kv, k_r, g_b, g_c, u_conv, u_pool,
         q_sw, k_sw, v_sw) = jnp.split(proj, pts, axis=-1)
        y_a = mla_attention(c_q, c_kv, k_r, mla_q_norm[l], mla_kv_norm[l],
                            w_uq[l], w_ukv[l], cos, sin)
        y_b = short_gated_conv(g_b, g_c, u_conv, conv_w[l])
        y_c = multiscale_pool(u_pool, pool_w[l], pool_scale[l])
        y_d = swa_sink_attention(q_sw.reshape(b, s, SWA_HEADS, SWA_HEAD_DIM),
                                 k_sw.reshape(b, s, SWA_KV_HEADS, SWA_HEAD_DIM),
                                 v_sw.reshape(b, s, SWA_KV_HEADS, SWA_HEAD_DIM),
                                 swa_sinks[l], slopes)
        groups = jnp.stack([y_a, y_b, y_c, y_d], axis=2)
        gf = groups.astype(jnp.float32)
        gf = gf * lax.rsqrt(jnp.mean(gf * gf, axis=-1, keepdims=True) + RMS_EPS)
        mixed = (gf.reshape(b, s, D_MIX) * mix_norm[l].astype(jnp.float32)).astype(x.dtype)
        x = x + mixed @ w_o[l]
        h2 = rmsnorm(x, ffn_norm[l])
        gate, up = jnp.split(h2 @ w_gate_up[l], 2, axis=-1)
        x = x + (jax.nn.silu(gate) * up) @ w_down[l]
    return rmsnorm(x, final_norm)


def setup_inputs(seed=0):
    out = dict(first_inputs(seed))
    for name, value in second_inputs(seed + 1).items():
        if name != "x":
            out[name + "_2"] = value
    return out


def reference(
    x, c, ctx, c_ctx, w_ada, b_ada, w_in, q_norm, k_norm, w_att_o, gla_w_a2, gla_b_a, gla_norm,
    w_gla_o, conv_w_dw, conv_b_dw, conv_ln_g, conv_ln_b, w_conv_o, w_out, ln1_g, ln1_b,
    w_ff_gate, w_ff_up, w_ff_down, ln2_g, ln2_b, attn_norm_2, w_in_2, mla_q_norm_2, w_uq_2,
    mla_kv_norm_2, w_ukv_2, conv_w_2, pool_w_2, pool_scale_2, swa_sinks_2, mix_norm_2, w_o_2,
    ffn_norm_2, w_gate_up_2, w_down_2, final_norm_2,
):
    x = first_block(
        x, c, ctx, c_ctx, w_ada, b_ada, w_in, q_norm, k_norm, w_att_o, gla_w_a2, gla_b_a,
        gla_norm, w_gla_o, conv_w_dw, conv_b_dw, conv_ln_g, conv_ln_b, w_conv_o, w_out, ln1_g,
        ln1_b, w_ff_gate, w_ff_up, w_ff_down, ln2_g, ln2_b,
    )
    return second_block(
        x, attn_norm_2, w_in_2, mla_q_norm_2, w_uq_2, mla_kv_norm_2, w_ukv_2, conv_w_2,
        pool_w_2, pool_scale_2, swa_sinks_2, mix_norm_2, w_o_2, ffn_norm_2, w_gate_up_2,
        w_down_2, final_norm_2,
    )


_drawn_inputs = setup_inputs


def setup_inputs(seed=0):
    import zlib

    import numpy as np

    out = dict(_drawn_inputs(seed))
    spreads = {}
    factors = {'ctx': 4.276,
     'c_ctx': 3.286,
     'b_ada': 3.908,
     'q_norm': 38.585,
     'k_norm': 40.969,
     'gla_w_a2': 8.0,
     'gla_b_a': 5.518,
     'gla_norm': 58.639,
     'conv_b_dw': 8.0,
     'conv_ln_g': 35.425,
     'conv_ln_b': 30.262,
     'mla_q_norm_2': 3.652}
    for name, (base, spread) in spreads.items():
        noise = np.random.default_rng([zlib.crc32(name.encode()), seed]).standard_normal(out[name].shape)
        drawn = base * np.exp(spread * noise) if base else spread * noise
        out[name] = jnp.asarray(drawn.astype(out[name].dtype))
    for name, factor in factors.items():
        out[name] = (out[name] * factor).astype(out[name].dtype)
    return out
```

```python
import concourse.bass as bass
import numpy as np
from concourse import mybir
from concourse.alu_op_type import AluOpType as ALU
from contextlib import ExitStack

P = 128
D = 1024
KC = D // P
S = 256
T = 2 * S
CTX, LAT = 0, 1
DEPTH = 2
EPS = 1e-6
ALPHA = (2.0 * DEPTH) ** 0.25
HEADS, KVH, DH = 8, 2, 128
GH, GDK, GDV, RANK, TAU = 4, 128, 256, 16, 16.0
TAPS = 31
PAD = TAPS // 2
FF = 2816
FC = FF // P
QT = S // P
LEVELS = (128, 64, 32, 16, 8, 4, 2, 1)
MH, NOPE, ROPE, MV = 4, 64, 32, 64
QK = NOPE + ROPE
SH, SHD = 4, 64
WINDOW = 128
POOLS = (2, 4, 8, 16)
NEG = -1e30
TILES = 16
SLOTS = 4
LAYER1_TILES = 48 * KC + 16 * KC + (2 + 8 + 2 + 8 + 4 + 4) * KC + 3 * 16 * KC + 8 * KC + 8 * KC + 2 * FC * KC + 8 * FC
LAYER2_TILES = 16 * KC + 8 * KC + 2 * FC * KC + 8 * FC
LOADS = DEPTH * (LAYER1_TILES + LAYER2_TILES) // TILES
VEC1 = {}
for _name, _n in (("b_ada", 48), ("q_norm", 1), ("k_norm", 1), ("gla_b_a", 8), ("gla_norm", 2), ("conv_b", 8),
                  ("conv_ln_g", 8), ("conv_ln_b", 8), ("ln1_g", 8), ("ln1_b", 8), ("ln2_g", 8), ("ln2_b", 8),
                  ("conv_w", 8 * TAPS)):
    VEC1[_name] = sum(n for _, n in VEC1.values()), _n
N_VEC1 = sum(n for _, n in VEC1.values())
VEC2 = {}
for _name, _n in (("attn_norm", 8), ("q_norm", 2), ("kv_norm", 1), ("conv_w", 6), ("pool_scale", 2), ("mix_norm", 8),
                  ("ffn_norm", 8), ("sinks", 4)):
    VEC2[_name] = sum(n for _, n in VEC2.values()), _n
N_VEC2 = sum(n for _, n in VEC2.values())
CONST1 = {}
for _name, _n in (("ident", P), ("mean1024", P), ("mean256", P), ("mean128", P), ("rot", P), ("cos", S), ("sin", S)):
    CONST1[_name] = sum(n for _, n in CONST1.values()), _n
N_CONST1 = sum(n for _, n in CONST1.values())
CONST2 = {}
for _name, _n in (("rot", P), ("cos", S), ("sin", S), ("inv_count", 2 * S), ("causal", QT * S), ("window", SH * QT * S)):
    CONST2[_name] = sum(n for _, n in CONST2.values()), _n
N_CONST2 = sum(n for _, n in CONST2.values())
N_SMALL2 = 2 * MH * QK + MH * (NOPE + MV) + 2 * P
N_MASK = 2 * (len(LEVELS) - 1) + 1


class Tally:

    def __init__(self):
        self.of = {}

    def up(self, name, k=1):
        self.of[name] = self.of.get(name, 0) + k
        return self.of[name]

    def at(self, name):
        return self.of.get(name, 0)


def program(nc, stream, xt_in, cvec_in, vec1_in, vec2_in, glr_in, a2_in, const1_in, const2_in, small2_in, mask_in, out):
    F32 = mybir.dt.float32
    U8 = mybir.dt.uint8
    ACT = mybir.ActivationFunctionType
    AXX = mybir.AxisListType.X
    with ExitStack() as ctx:
        def sb(name, shape, dt=F32):
            return ctx.enter_context(nc.sbuf_tensor(name, shape, dt))

        def sem(name):
            return ctx.enter_context(nc.semaphore(name))

        ring = sb("ring", [P, SLOTS, TILES * P])
        X = sb("X", [P, KC, T])
        H = sb("H", [P, KC, T])
        M = sb("M", [P, KC, T])
        arena1 = sb("arena1", [P, 14336])
        arena2 = sb("arena2", [P, 8 * 2 * (S + 2 * PAD) + KC * T])
        gate_buf = sb("gate_buf", [P, 2, T])
        y_buf = sb("y_buf", [P, 2, T])
        std = sb("std", [P, 2, S * 2])
        rstd = sb("rstd", [P, T])
        tmp = sb("tmp", [P, T])
        vec1 = sb("vec1", [P, DEPTH, N_VEC1])
        vec2 = sb("vec2", [P, DEPTH * N_VEC2 + KC])
        cvec = sb("cvec", [P, KC, 2])
        silu_c = sb("silu_c", [P, KC, 2])
        mod = sb("mod", [P, 48, 2])
        wglr = sb("wglr", [P, DEPTH, KC * 2 * RANK])
        wa2 = sb("wa2", [RANK, DEPTH, 2 * GH * GDK])
        const1 = sb("const1", [P, N_CONST1])
        masks = sb("masks", [P, N_MASK, P], U8)
        small = sb("small", [P, 2, 8])

        def view(t, at, *shape):
            n = int(np.prod(shape))
            v = t[:, at:at + n]
            if len(shape) == 2:
                return v.rearrange("p (a b) -> p a b", a=shape[0])
            if len(shape) == 3:
                return v.rearrange("p (a b c) -> p a b c", a=shape[0], b=shape[1])
            if len(shape) == 4:
                return v.rearrange("p (a b c d) -> p a b c d", a=shape[0], b=shape[1], c=shape[2])
            return v

        Q = view(arena1, 0, HEADS, T)
        K = view(arena1, 4096, KVH, T)
        V = view(arena1, 5120, T // P, KVH * DH)
        KG = view(arena1, 6144, 2, GH, S)
        QG = view(arena1, 8192, 2, GH, S)
        VG = view(arena1, 10240, T // P, GH * GDV)
        state = view(arena1, 4096, 2, GH, GDV)
        HID = view(arena1, 0, FC, T)
        YP = view(arena2, 0, KC, 2, S + 2 * PAD)
        CV = view(arena2, 8 * 2 * (S + 2 * PAD), KC, T)
        probs = view(arena2, 0, 2, T)
        probsT = view(arena2, 2 * T, 2, T // P, P)
        Z = view(arena2, 0, 2 * GH, S)
        DL = view(arena2, 0, 2, GH, S)
        B = view(arena2, 2048, 2 * GH, S)
        A = view(arena2, 4096, GH, QT, S)
        KT = view(arena2, 6144, 2, QT, GH, P)
        OSQ = view(arena2, 0, KC, T)
        a = 0
        w2 = {}
        for name, shape in (("cq", (2, S)), ("ckv", (1, S)), ("kr", (1, S)), ("qh", (MH, S)), ("kh", (MH, S)),
                            ("vm", (QT, MH * MV)), ("gb", (2, S)), ("gc", (2, S)), ("uc", (2, S)), ("zp", (2, S + 2)),
                            ("up", (2, S + 16)), ("qs", (2, S)), ("ks", (1, S)), ("vs", (QT, P))):
            w2[name] = view(arena1, a, *shape)
            a += int(np.prod(shape))
        HID2 = view(arena1, 0, FC, S)
        at_c2 = 14336 - N_CONST2 - DEPTH * N_SMALL2
        assert a <= at_c2 and FC * S <= at_c2
        const2 = arena1[:, at_c2:at_c2 + N_CONST2]
        small2 = view(arena1, at_c2 + N_CONST2, DEPTH, N_SMALL2)
        a = 0
        for name, shape in (("mx", (8, S)), ("probs", (2, S)), ("probsT", (2, QT, P)), ("scores", (2, S)),
                            ("p2", (2, S + 16)), ("p4", (2, S + 16)), ("p8", (2, S + 16)), ("p16", (2, S + 16)),
                            ("pooled", (2, S)), ("yb", (2, S))):
            w2[name] = view(arena2, a, *shape)
            a += int(np.prod(shape))
        assert a <= 8 * 2 * (S + 2 * PAD) + KC * T

        def c1(name):
            at, n = CONST1[name]
            return const1[:, at:at + n]

        def c2(name):
            at, n = CONST2[name]
            return const2[:, at:at + n]

        def v1(l, name, c=0, n=1):
            at = VEC1[name][0] + c
            return vec1[:, l, at:at + n]

        def v2(l, name, c=0):
            at = l * N_VEC2 + VEC2[name][0] + c
            return vec2[:, at:at + 1]

        lin = [ctx.enter_context(nc.psum_tensor(f"lin{i}", [P, T], F32)) for i in range(4)]
        aux = [ctx.enter_context(nc.psum_tensor(f"aux{i}", [P, T], F32)) for i in range(4)]

        landed = [sem(f"landed{i}") for i in range(SLOTS)]
        NAMES = ("w_used",
                 "lin_done",
                 "lin_evac",
                 "params", "x_landed", "b2_landed", "stored",
                 "silu_ready", "mod_ready", "x_ready", "h_ready", "mean_done", "xc_ready", "sq_ready",
                 "var_done", "std_ready", "pads_ready", "y_ready", "conv_done", "cn_ready", "cv_ready",
                 "m_ready", "qk_normed", "rot_done", "qk_ready", "s_done", "nb_ready", "p_ready",
                 "pn_ready", "pt_done", "pt_ready", "o_done", "o_ready", "ln_ready", "diff_ready",
                 "lev_exp", "lev_ready", "gram_done", "a_copied", "hat_diff", "hat_exp", "hat_ready",
                 "og_ready", "hid_ready", "r_ready", "dve_step", "act_step", "kr_done", "pooled_ready", "pool_done",
                 "pool_ready", "yb_ready", "sm_ready", "es_ready", "b2_free", "fin_ready")
        sems = {name: sem(name) for name in NAMES}
        block = ctx.enter_context(nc.Block())

        def val(base, i, per):
            return base if i is None else base + i * per

        @block.sync
        def _(sp):
            sp.dma_start(cvec[:, :, :], cvec_in).then_inc(sems["params"], 16)
            sp.dma_start(X[:, :, :], xt_in).then_inc(sems["x_landed"], 16)
            sp.dma_start(vec1[:, :, :], vec1_in).then_inc(sems["params"], 16)
            sp.dma_start(const1[:, :], const1_in).then_inc(sems["params"], 16)
            for s in range(SLOTS):
                sp.dma_start(ring[:, s, :], stream[s]).then_inc(landed[s], 16)
            sp.dma_start(vec2[:, :], vec2_in).then_inc(sems["params"], 16)
            sp.dma_start(wglr[:, :, :], glr_in).then_inc(sems["params"], 16)
            sp.dma_start(wa2[:, :, :], a2_in).then_inc(sems["params"], 16)
            sp.dma_start(view(arena2, 0, N_MASK, P), mask_in).then_inc(sems["params"], 16)
            with sp.Fori(1, LOADS // SLOTS) as i:
                for s in range(SLOTS):
                    sp.wait_ge(sems["w_used"], i * SLOTS + (s + 1 - SLOTS))
                    sp.dma_start(ring[:, s, :], stream[bass.ds(i * SLOTS + s, 1)].rearrange("a p n -> p (a n)")
                                 ).then_inc(landed[s], 16)
            sp.wait_ge(sems["fin_ready"], 1)
            sp.dma_start(out, H[:, :, S:T]).then_inc(sems["stored"], 16)
            sp.wait_ge(sems["stored"], 16)

        PARAMS = 16 * 7

        @block.gpsimd
        def _(pool):
            n = Tally()
            for l in range(DEPTH):
                pool.wait_ge(sems["h_ready"], 2 * l + 1)
                pool.memset(YP[:, :, :, 0:PAD], 0.0)
                pool.memset(YP[:, :, :, PAD + S:2 * PAD + S], 0.0).then_inc(sems["pads_ready"], 1)
            pool.wait_ge(sems["x_ready"], 2 * DEPTH)
            pool.dma_start(const2, const2_in).then_inc(sems["b2_landed"], 16)
            pool.dma_start(small2, small2_in).then_inc(sems["b2_landed"], 16)

        @block.tensor
        def _(pe):
            n = Tally()
            place = [0]

            def wait(name, k=1):
                pe.wait_ge(sems[name], n.up(name, k))

            def weight(i=None):
                t = place[0]
                place[0] += 1
                load = t // TILES
                slot = load % SLOTS
                if t % TILES == 0:
                    pe.wait_ge(landed[slot], val(16 * (load // SLOTS + 1), i, 16))
                return ring[:, slot, t % TILES * P:(t % TILES + 1) * P], t % TILES == 0 and load > 0

            def bank(i=None, per=0):
                c = n.up("lin_done") - 1
                if c >= 4:
                    pe.wait_ge(sems["lin_evac"], val(c - 3, i, per))
                return lin[c % 4]

            def done(mm):
                mm.then_inc(sems["lin_done"], 1)

            def dense(rhs, i=None, per=0, rows=P, at=0):
                o = bank(i, per)
                w = rhs[0].free_size()
                for k, r in enumerate(rhs):
                    tile, first = weight(i)
                    mm = pe.matmul(o[at:at + rows, 0:w], tile[:, 0:rows], r, start=k == 0, stop=k == len(rhs) - 1)
                    if first:
                        mm.then_inc(sems["w_used"], 1)
                done(mm)

            def token_major(tts, width):
                t = place[0]
                load = t // TILES
                slot = load % SLOTS
                off = t % TILES * P
                if off == 0:
                    pe.wait_ge(landed[slot], 16 * (load // SLOTS + 1))
                place[0] += KC * width // P
                first = off == 0
                per = min(2, len(tts))
                for c in range(0, len(tts), per):
                    o = bank()
                    for j, tt in enumerate(tts[c:c + per]):
                        for k in range(KC):
                            mm = pe.matmul(o[:, j * width:(j + 1) * width], H[:, k, tt * P:(tt + 1) * P],
                                           ring[:, slot, off + k * width:off + (k + 1) * width],
                                           start=k == 0, stop=k == KC - 1)
                            if first:
                                mm.then_inc(sems["w_used"], 1)
                                first = False
                    done(mm)

            def cols(t, rng):
                return [t[:, k, rng[0]:rng[1]] for k in range(t.shape[1])]

            def mean_of(src, rng):
                for k in range(KC):
                    mm = pe.matmul(aux[0][:, 0:rng[1] - rng[0]], c1("mean1024"), src[:, k, rng[0]:rng[1]],
                                   start=k == 0, stop=k == KC - 1)
                mm.then_inc(sems["mean_done"], 1)

            def var_of(b, weights, squares):
                wait("sq_ready")
                for k, r in enumerate(squares):
                    mm = pe.matmul(b[:, 0:r.free_size()], weights, r, start=k == 0, stop=k == len(squares) - 1)
                mm.then_inc(sems["var_done"], 1)

            def layernorm(src, rng):
                mean_of(src, rng)
                var_of(aux[1], c1("mean1024"), cols(M, rng))

            def merge(src, rng):
                for c in range(KC):
                    dense(cols(H, rng))
                    dense(cols(src, rng))

            def attention(items):
                def scores(j):
                    if j >= 2:
                        pe.wait_ge(sems["p_ready"], n.at("s_done") - 1)
                    q, k, _, _, w = items[j]
                    pe.matmul(aux[j % 2][:, 0:w], q, k, start=True, stop=True).then_inc(sems["s_done"], 1)
                    n.up("s_done")

                def values(j):
                    q, _, v, rows, w = items[j]
                    wait("pn_ready")
                    for kt in range(w // P):
                        mm = pe.transpose(aux[2][:, kt * P:(kt + 1) * P], p_tile[:, j % 2, kt * P:(kt + 1) * P], c1("ident"))
                    mm.then_inc(sems["pt_done"], 1)
                    wait("pt_ready")
                    if j >= 1:
                        wait("o_ready")
                    for kt in range(w // P):
                        mm = pe.matmul(aux[3][rows[0]:rows[1], 0:P], v[kt], pt_tile[:, j % 2, kt, :],
                                       start=kt == 0, stop=kt == w // P - 1)
                    mm.then_inc(sems["o_done"], 1)
                for j in range(len(items)):
                    scores(j)
                    if j >= 1:
                        values(j - 1)
                values(len(items) - 1)
                wait("o_ready")

            def gla(l, s):
                sl = slice(s * S, (s + 1) * S)
                full = l == 0 or s == LAT
                for j in range(4):
                    o = bank()
                    for k in range(2):
                        d, h = divmod(2 * j + k, GH)
                        mm = pe.matmul(o[:, k * S:(k + 1) * S], wa2[:, l, (d * GH + h) * GDK:(d * GH + h + 1) * GDK],
                                       gate_buf[0:RANK, d, sl], start=True, stop=True)
                    done(mm)
                if full:
                    for j in range(2 * len(LEVELS)):
                        half, d = LEVELS[j // 2], j % 2
                        wait("lev_ready")
                        pair = [aux[2 * (j % 2)], aux[2 * (j % 2) + 1]]
                        if n.of.get("grams", 0) >= 2:
                            pe.wait_ge(sems["a_copied"], n.at("grams") - 1)
                        n.up("grams")
                        if half == P:
                            ks, qs = (0, P) if d == 0 else (P, 0)
                            for h in range(GH):
                                mm = pe.matmul(pair[0][:, h * P:(h + 1) * P], DL[:, j % 2, h, ks:ks + P],
                                               DL[:, j % 2, h, qs:qs + P], start=True, stop=True)
                        else:
                            for kt in range(QT):
                                for h in range(GH):
                                    part = DL[:, j % 2, h, kt * P:(kt + 1) * P]
                                    mm = pe.matmul(pair[kt][:, h * P:(h + 1) * P], part, part, start=True, stop=True)
                        mm.then_inc(sems["gram_done"], 1)
                    j = 2 * len(LEVELS)
                    pe.wait_ge(sems["a_copied"], n.at("grams") - 1)
                    n.up("grams")
                    for kt in range(QT):
                        for h in range(GH):
                            at = kt * P
                            for rep in range(2):
                                mm = pe.matmul(aux[kt][:, h * P:(h + 1) * P], KG[:, s, h, at:at + P], QG[:, s, h, at:at + P],
                                               start=rep == 0, stop=rep == 1)
                    mm.then_inc(sems["gram_done"], 1)
                wait("hat_ready")
                if s == CTX:
                    for d in range(2):
                        for kt in range(QT):
                            o = bank()
                            for h in range(GH):
                                mm = pe.transpose(o[:, h * P:(h + 1) * P], DL[:, d, h, kt * P:(kt + 1) * P], c1("ident"))
                            done(mm)
                    pe.wait_ge(sems["lin_evac"], n.at("lin_done"))
                    for j in range(4):
                        o = bank()
                        for k in range(2):
                            d, h = divmod(2 * j + k, GH)
                            for kt in range(QT):
                                mm = pe.matmul(o[:, k * GDV:(k + 1) * GDV], KT[:, d, kt, h, :],
                                               VG[:, kt, h * GDV:(h + 1) * GDV], start=kt == 0, stop=kt == QT - 1)
                        done(mm)
                if full:
                    pe.wait_ge(sems["a_copied"], n.at("grams"))
                    if s == LAT:
                        pe.wait_ge(sems["lin_evac"], n.at("lin_done"))
                    for h in range(GH):
                        o = bank()
                        for c in range(2):
                            at = h * GDV + c * P
                            for kt in range(QT):
                                mm = pe.matmul(o[:, c * S:(c + 1) * S], VG[:, s * QT + kt, at:at + P], A[:, h, kt, :],
                                               start=kt == 0, stop=kt == QT - 1 and s == CTX)
                            if s == LAT:
                                for d in range(2):
                                    mm = pe.matmul(o[:, c * S:(c + 1) * S], state[:, d, h, c * P:(c + 1) * P],
                                                   DL[:, d, h, :], start=False, stop=d == 1)
                        done(mm)

            def ff(rng):
                def turn(i, loads, per):
                    for _ in range(2 * loads):
                        dense(cols(H, rng), i, per)
                turns = 2 * FC * KC // (SLOTS * TILES)
                with pe.Fori(0, turns) as i:
                    turn(i, SLOTS, 2 * SLOTS)
                n.up("lin_done", 2 * SLOTS * (turns - 1))
                place[0] += SLOTS * TILES * (turns - 1)
                turn(None, FC - SLOTS * turns, 0)

            pe.wait_ge(sems["params"], PARAMS)
            for l in range(DEPTH):
                rest = (0, T) if l == 0 else (S, T)
                if l == 0:
                    wait("silu_ready")

                def ada(i, per):
                    for _ in range(SLOTS):
                        o = bank(i, per)
                        for c in range(2):
                            for k in range(KC):
                                tile, first = weight(i)
                                mm = pe.matmul(o[:, 2 * c:2 * c + 2], tile, silu_c[:, k, :], start=k == 0, stop=k == KC - 1)
                                if first:
                                    mm.then_inc(sems["w_used"], 1)
                        done(mm)
                ada(None, 0)
                turns = 48 * KC // (SLOTS * TILES) - 1
                with pe.Fori(0, turns) as i:
                    ada(i, SLOTS)
                n.up("lin_done", SLOTS * (turns - 1))
                place[0] += SLOTS * TILES * (turns - 1)

                if l == 0:
                    pe.wait_ge(sems["x_landed"], 16)
                layernorm(X, (0, T))
                wait("h_ready")
                for c in range(16):
                    dense(cols(H, rest))
                for c in range(KVH):
                    dense(cols(H, (0, T)))
                for c in range(HEADS):
                    dense(cols(H, rest))
                token_major(range(4), KVH * DH)
                for c in range(4):
                    token_major(range(4), 2 * P)
                for c in range(GH):
                    dense(cols(H, (0, T)))
                for c in range(GH):
                    dense(cols(H, rest))
                wait("conv_done")
                layernorm(CV, rest)
                wait("cv_ready")
                merge(CV, rest)
                w = rest[1] - rest[0]
                heads = [(K, c, (0, T)) for c in range(KVH)] + [(Q, c, rest) for c in range(HEADS)]

                def rotate(j):
                    t, c, rng = heads[j]
                    wait("qk_normed")
                    if j >= 2:
                        pe.wait_ge(sems["qk_ready"], n.at("qk_ready") + j - 1)
                    pe.matmul(aux[2 + j % 2][:, 0:S], c1("rot"), t[:, c, S:T], start=True, stop=True
                              ).then_inc(sems["rot_done"], 1)
                for j, (t, c, rng) in enumerate(heads):
                    var_of(aux[j % 2], c1("mean128"), [gate_buf[:, j % 2, 0:rng[1] - rng[0]]])
                    if j >= 1:
                        rotate(j - 1)
                rotate(len(heads) - 1)
                wait("qk_ready", len(heads))
                p_tile, pt_tile = probs, probsT
                items = []
                for s in ((CTX, LAT) if l == 0 else (LAT,)):
                    keys = S if s == CTX else T
                    for h in range(HEADS):
                        g = h // (HEADS // KVH)
                        for qt in range(QT):
                            at = s * S + qt * P
                            items.append((Q[:, h, at:at + P], K[:, g, 0:keys],
                                          [V[:, kt, g * DH:(g + 1) * DH] for kt in range(keys // P)], (0, P), keys))
                attention(items)
                merge(Q, rest)
                for d in range(2):
                    o = bank()
                    for k in range(KC):
                        at = k * 2 * RANK + d * RANK
                        mm = pe.matmul(o[0:RANK, :], wglr[:, l, at:at + RANK], H[:, k, :], start=k == 0, stop=k == KC - 1)
                    done(mm)
                pe.wait_ge(sems["lin_evac"], n.at("lin_done"))
                gla(l, CTX)
                gla(l, LAT)
                for h in range(GH):
                    if h >= 2:
                        pe.wait_ge(sems["og_ready"], n.at("og_ready") + h - 1)
                    var_of(aux[h % 2], c1("mean256"), [OSQ[:, 2 * h + c, rest[0]:rest[1]] for c in range(2)])
                n.up("og_ready", GH)
                for c in range(KC):
                    dense(cols(H, rest))
                wait("y_ready", 2 * KC)
                merge(Q, rest)
                wait("m_ready", 3 * KC)
                for c in range(KC):
                    dense(cols(M, rest))
                wait("r_ready", KC)
                layernorm(X, rest)
                wait("x_ready")
                layernorm(X, rest)
                wait("h_ready")
                ff(rest)
                wait("hid_ready", FC)
                for c in range(KC):
                    dense(cols(HID[:, :, 0:w], (0, w)))
                wait("r_ready", KC)
                layernorm(X, rest)
                wait("x_ready")

            lat = (S, T)
            pe.wait_ge(sems["b2_landed"], 32)
            for l in range(DEPTH):
                var_of(aux[1], c1("mean1024"), cols(M, lat))
                wait("h_ready")
                for c in range(3):
                    dense(cols(H, lat))
                dense(cols(H, lat), rows=ROPE, at=NOPE)
                for c in range(11):
                    dense(cols(H, lat))
                token_major(range(2, 4), P)
                var_of(aux[0], c1("mean256"), [gate_buf[:, 0, c * S:(c + 1) * S] for c in range(2)])
                var_of(aux[1], c1("mean128"), [gate_buf[:, 1, 0:S]])
                wait("qk_normed", 2)
                wuq = small2[:, l, 0:2 * MH * QK]
                wukv = small2[:, l, 2 * MH * QK:2 * MH * QK + MH * (NOPE + MV)]
                wpool = small2[:, l, 2 * MH * QK + MH * (NOPE + MV):N_SMALL2]
                for h in range(MH):
                    o = bank()
                    for k in range(2):
                        at = (k * MH + h) * QK
                        mm = pe.matmul(o[0:QK, 0:S], wuq[:, at:at + QK], w2["cq"][:, k, :], start=k == 0, stop=k == 1)
                    done(mm)
                for h in range(MH):
                    o = bank()
                    at = h * (NOPE + MV)
                    done(pe.matmul(o[0:NOPE, 0:S], wukv[:, at:at + NOPE], w2["ckv"][:, 0, :], start=True, stop=True))
                o = bank()
                vcols = wukv.rearrange("p (h e) -> p h e", h=MH)[:, :, NOPE:]
                for tt in range(QT):
                    mm = pe.matmul(o[:, tt * MH * MV:(tt + 1) * MH * MV], w2["ckv"][:, 0, tt * P:(tt + 1) * P], vcols,
                                   start=True, stop=True)
                done(mm)
                rot = c2("rot")
                pe.wait_ge(sems["lin_evac"], n.at("lin_done"))
                pe.matmul(aux[2][NOPE:QK, 0:S], rot[NOPE:QK, NOPE:QK], w2["kr"][NOPE:QK, 0, :], start=True, stop=True
                          ).then_inc(sems["rot_done"], 1)
                for h in range(MH):
                    if h >= 1:
                        pe.wait_ge(sems["qk_ready"], n.at("qk_ready") + h)
                    pe.matmul(aux[2 + (h + 1) % 2][0:QK, 0:S], rot[0:QK, 0:QK], w2["qh"][0:QK, h, :], start=True, stop=True
                              ).then_inc(sems["rot_done"], 1)
                wait("qk_ready", MH + 1)
                wait("pooled_ready")
                for c in range(2):
                    o = bank()
                    done(pe.matmul(o[:, 0:S], wpool[:, c * P:(c + 1) * P], w2["pooled"][:, c, :], start=True, stop=True))
                p_tile, pt_tile = w2["probs"], w2["probsT"]
                items = []
                for h in range(MH):
                    for qt in range(QT):
                        items.append((w2["qh"][0:QK, h, qt * P:(qt + 1) * P], w2["kh"][0:QK, h, :],
                                      [w2["vm"][:, kt, h * MV:(h + 1) * MV] for kt in range(QT)],
                                      (64 * (h % 2), 64 * (h % 2) + 64), S))
                for h in range(SH):
                    g, j = divmod(h, 2)
                    for qt in range(QT):
                        items.append((w2["qs"][64 * g:64 * g + 64, j, qt * P:(qt + 1) * P], w2["ks"][64 * g:64 * g + 64, 0, :],
                                      [w2["vs"][:, kt, g * SHD:(g + 1) * SHD] for kt in range(QT)],
                                      (64 * (h % 2), 64 * (h % 2) + 64), S))
                attention(items)
                for g in range(4):
                    if g >= 2:
                        pe.wait_ge(sems["og_ready"], n.at("og_ready") + g - 1)
                    var_of(aux[g % 2], c1("mean256"), [M[:, 2 * g + c, S:T] for c in range(2)])
                wait("og_ready", 4)
                for c in range(KC):
                    dense(cols(w2["mx"], (0, S)))
                wait("r_ready", KC)
                var_of(aux[1], c1("mean1024"), cols(M, lat))
                wait("h_ready")
                ff(lat)
                wait("hid_ready", FC)
                for c in range(KC):
                    dense(cols(HID2, (0, S)))
                wait("r_ready", KC)
            var_of(aux[1], c1("mean1024"), cols(M, lat))

        @block.scalar
        def _(act):
            n = Tally()

            def wait(name, k=1):
                act.wait_ge(sems[name], n.up(name, k))

            def arrived(i=None, per=0):
                c = n.up("lin_done") - 1
                act.wait_ge(sems["lin_done"], val(c + 1, i, per))
                n.up("lin_evac")
                return lin[c % 4]

            def moved(ins):
                ins.then_inc(sems["lin_evac"], 1)

            def step(ins):
                ins.then_inc(sems["act_step"], 1)
                act.wait_ge(sems["act_step"], n.up("act_step"))

            def square(out, in_):
                act.activation(out, in_, ACT.Square).then_inc(sems["sq_ready"], 1)
                n.up("sq_ready")

            def root(b, w, slot=0):
                wait("var_done")
                act.activation(std[:, slot, 0:w], b[:, 0:w], ACT.Sqrt, bias=EPS).then_inc(sems["std_ready"], 1)

            def layernorm(src, rng):
                wait("xc_ready")
                square(M[:, :, rng[0]:rng[1]], src[:, :, rng[0]:rng[1]])
                root(aux[1], rng[1] - rng[0])

            def merge(w):
                for c in range(KC):
                    o = arrived()
                    if c >= 2:
                        act.wait_ge(sems["m_ready"], n.at("m_ready") + c - 1)
                    moved(act.activation(gate_buf[:, c % 2, 0:w], o[:, 0:w], ACT.Sigmoid))
                    o = arrived()
                    moved(act.activation(y_buf[:, c % 2, 0:w], o[:, 0:w], ACT.Copy))
                n.up("m_ready", KC)

            def residual(w, l, gate):
                for c in range(KC):
                    o = arrived()
                    if c >= 2:
                        act.wait_ge(sems["r_ready"], n.at("r_ready") + c - 1)
                    if gate is None:
                        moved(act.activation(gate_buf[:, c % 2, 0:w], o[:, 0:w], ACT.Copy))
                    elif w == S:
                        moved(act.activation(gate_buf[:, c % 2, 0:S], o[:, 0:S], ACT.Copy, scale=mod[:, gate + c, LAT:LAT + 1]))
                    else:
                        act.activation(gate_buf[:, c % 2, 0:S], o[:, 0:S], ACT.Copy, scale=mod[:, gate + c, CTX:CTX + 1])
                        moved(act.activation(gate_buf[:, c % 2, S:T], o[:, S:T], ACT.Copy, scale=mod[:, gate + c, LAT:LAT + 1]))
                n.up("r_ready", KC)

            def ff(w):
                def turn(i, loads, per_i, base):
                    for c in range(loads):
                        o = arrived(i, 2 * per_i)
                        if base + c >= 2:
                            act.wait_ge(sems["hid_ready"], val(n.at("hid_ready") + base + c - 1, i, per_i))
                        moved(act.activation(gate_buf[:, c % 2, 0:w], o[:, 0:w], ACT.Silu))
                        o = arrived(i, 2 * per_i)
                        moved(act.activation(y_buf[:, c % 2, 0:w], o[:, 0:w], ACT.Copy))
                turns = 2 * FC * KC // (SLOTS * TILES)
                turn(None, SLOTS, 0, 0)
                with act.Fori(0, turns - 1) as i:
                    turn(i, SLOTS, SLOTS, SLOTS)
                n.up("lin_done", 2 * SLOTS * (turns - 2))
                n.up("lin_evac", 2 * SLOTS * (turns - 2))
                turn(None, FC - SLOTS * turns, 0, SLOTS * turns)
                n.up("hid_ready", FC)

            def attention(items, scale):
                p_tile, pt_tile = (probs, probsT) if scale is not None else (w2["probs"], w2["probsT"])

                def soft(j):
                    w, _, sink, _ = items[j]
                    wait("nb_ready")
                    if scale is not None:
                        act.activation(p_tile[:, j % 2, 0:w], aux[j % 2][:, 0:w], ACT.Exp, scale=scale, bias=small[:, j % 2, 1:2],
                                       accum_out=small[:, j % 2, 2:3]).then_inc(sems["p_ready"], 1)
                    else:
                        if sink is not None:
                            act.activation(small[:, j % 2, 4:5], sink, ACT.Exp, bias=small[:, j % 2, 1:2])
                        act.activation(p_tile[:, j % 2, 0:w], w2["scores"][:, j % 2, 0:w], ACT.Exp, bias=small[:, j % 2, 1:2],
                                       accum_out=small[:, j % 2, 2:3]).then_inc(sems["p_ready"], 1)

                def move(j):
                    w, place, _, rows = items[j]
                    wait("pt_done")
                    act.activation(pt_tile[:, j % 2, 0:w // P, :], aux[2][:, 0:w].rearrange("p (a b) -> p a b", b=P), ACT.Copy
                                   ).then_inc(sems["pt_ready"], 1)
                    wait("o_done")
                    act.activation(place, aux[3][rows[0]:rows[1], 0:P], ACT.Copy).then_inc(sems["o_ready"], 1)
                    n.up("o_ready")
                for j in range(len(items)):
                    soft(j)
                    if j >= 1:
                        move(j - 1)
                move(len(items) - 1)

            def gla(l, s):
                sl = slice(s * S, (s + 1) * S)
                full = l == 0 or s == LAT
                for j in range(4):
                    o = arrived()
                    for k in range(2):
                        ins = act.activation(Z[:, 2 * j + k, :], o[:, k * S:(k + 1) * S], ACT.Identity,
                                             bias=v1(l, "gla_b_a", 2 * j + k))
                    moved(ins)
                act.wait_ge(sems["lin_evac"], n.at("lin_evac"))
                step(act.activation(B[:, :, :], Z[:, :, :], ACT.Abs))
                step(act.activation(B[:, :, :], B[:, :, :], ACT.Exp, scale=-1.0))
                act.activation(B[:, :, :], B[:, :, :], ACT.Ln, bias=1.0).then_inc(sems["ln_ready"], 1)
                if full:
                    for j in range(2 * len(LEVELS)):
                        wait("diff_ready")
                        act.activation(DL[:, j % 2], DL[:, j % 2], ACT.Exp, scale=1.0 / TAU).then_inc(sems["lev_exp"], 1)
                wait("hat_diff")
                src = DL if s == CTX else B[:, :, :].rearrange("p (d h) t -> p d h t", d=2)
                act.activation(DL[:, :, :, :], src[:, :, :, :], ACT.Exp, scale=1.0 / TAU).then_inc(sems["hat_exp"], 1)
                if s == CTX:
                    for d in range(2):
                        for kt in range(QT):
                            o = arrived()
                            moved(act.activation(KT[:, d, kt, :, :], o[:, :].rearrange("p (h k) -> p h k", h=GH), ACT.Copy))
                    for j in range(4):
                        o = arrived()
                        d, h = divmod(2 * j, GH)
                        moved(act.activation(state[:, d, h:h + 2, :], o[:, :].rearrange("p (h e) -> p h e", h=2), ACT.Copy))
                if full:
                    for h in range(GH):
                        o = arrived()
                        moved(act.activation(Q[:, 2 * h:2 * h + 2, sl], o[:, :].rearrange("p (c t) -> p c t", c=2), ACT.Copy))

            act.wait_ge(sems["params"], PARAMS)
            act.activation(silu_c[:, :, :], cvec[:, :, :], ACT.Silu).then_inc(sems["silu_ready"], 1)
            for l in range(DEPTH):
                rest = (0, T) if l == 0 else (S, T)
                w = rest[1] - rest[0]
                pairs = mod[:, :, :].rearrange("p (n c) s -> p n (c s)", c=2)

                def ada(i, first, per):
                    for c in range(SLOTS):
                        o = arrived(i, per)
                        dst = pairs[:, first + c, :] if i is None else pairs[:, bass.ds(i * SLOTS + (first + c), 1), :].rearrange("p a c -> p (a c)")
                        moved(act.activation(dst, o[:, 0:4], ACT.Copy))
                ada(None, 0, 0)
                turns = 48 * KC // (SLOTS * TILES) - 1
                with act.Fori(0, turns) as i:
                    ada(i, SLOTS, SLOTS)
                n.up("lin_done", SLOTS * (turns - 1))
                n.up("lin_evac", SLOTS * (turns - 1))
                layernorm(H, (0, T))
                streams = slice(0, 2) if l == 0 else slice(1, 2)
                y0 = n.at("y_ready")
                for c in range(KC):
                    o = arrived()
                    moved(act.activation(YP[:, c, streams, PAD:PAD + S], o[:, 0:w].rearrange("p (s t) -> p s t", t=S), ACT.Copy))
                    o = arrived()
                    if c >= 2:
                        act.wait_ge(sems["y_ready"], y0 + c - 1)
                    moved(act.activation(gate_buf[:, c % 2, 0:w], o[:, 0:w], ACT.Sigmoid))
                n.up("y_ready", KC)
                for c in range(KVH):
                    moved(act.activation(K[:, c, :], arrived()[:, :], ACT.Copy))
                for c in range(HEADS):
                    moved(act.activation(Q[:, c, rest[0]:rest[1]], arrived()[:, 0:w], ACT.Copy))
                for c in range(2):
                    moved(act.activation(V[:, 2 * c:2 * c + 2, :], arrived()[:, :].rearrange("p (a b) -> p a b", a=2), ACT.Copy))
                for j in range(4):
                    for c in range(2):
                        moved(act.activation(VG[:, 2 * c:2 * c + 2, 2 * P * j:2 * P * (j + 1)],
                                             arrived()[:, :].rearrange("p (a b) -> p a b", a=2), ACT.Copy))
                for c in range(GH):
                    moved(act.activation(KG[:, :, c, :], arrived()[:, :].rearrange("p (s t) -> p s t", t=S), ACT.Copy))
                for c in range(GH):
                    moved(act.activation(QG[:, streams, c, :], arrived()[:, 0:w].rearrange("p (s t) -> p s t", t=S), ACT.Copy,
                                         scale=float(GDK) ** -0.5))
                layernorm(CV, rest)
                wait("cn_ready")
                act.activation(CV[:, :, rest[0]:rest[1]], CV[:, :, rest[0]:rest[1]], ACT.Silu).then_inc(sems["cv_ready"], 1)
                merge(w)
                heads = [(K, c, (0, T)) for c in range(KVH)] + [(Q, c, rest) for c in range(HEADS)]
                act.wait_ge(sems["m_ready"], n.at("m_ready"))
                v0 = n.at("var_done")

                def head_square(j):
                    t, c, rng = heads[j]
                    if j >= 2:
                        act.wait_ge(sems["var_done"], v0 + j - 1)
                    square(gate_buf[:, j % 2, 0:rng[1] - rng[0]], t[:, c, rng[0]:rng[1]])
                head_square(0)
                for j, (t, c, rng) in enumerate(heads):
                    if j + 1 < len(heads):
                        head_square(j + 1)
                    if j >= 2:
                        act.wait_ge(sems["qk_normed"], n.at("qk_normed") + j - 1)
                    root(aux[j % 2], rng[1] - rng[0], j % 2)
                n.up("qk_normed", len(heads))
                items = []
                for s in ((CTX, LAT) if l == 0 else (LAT,)):
                    for h in range(HEADS):
                        for qt in range(QT):
                            at = s * S + qt * P
                            items.append((S if s == CTX else T, Q[:, h, at:at + P], None, (0, P)))
                attention(items, float(DH) ** -0.5)
                merge(w)
                act.wait_ge(sems["m_ready"], n.at("m_ready"))
                for d in range(2):
                    moved(act.activation(gate_buf[0:RANK, d, :], arrived()[0:RANK, :], ACT.Copy))
                gla(l, CTX)
                gla(l, LAT)
                act.wait_ge(sems["lin_evac"], n.at("lin_evac"))
                for h in range(GH):
                    square(OSQ[:, 2 * h:2 * h + 2, rest[0]:rest[1]], Q[:, 2 * h:2 * h + 2, rest[0]:rest[1]])
                for h in range(GH):
                    if h >= 2:
                        act.wait_ge(sems["og_ready"], n.at("og_ready") + h - 1)
                    root(aux[h % 2], w, h % 2)
                n.up("og_ready", GH)
                for c in range(KC):
                    o = arrived()
                    if c >= 2:
                        act.wait_ge(sems["y_ready"], n.at("y_ready") + c - 1)
                    moved(act.activation(gate_buf[:, c % 2, 0:w], o[:, 0:w], ACT.Silu))
                n.up("y_ready", KC)
                act.wait_ge(sems["y_ready"], n.at("y_ready"))
                merge(w)
                act.wait_ge(sems["m_ready"], n.at("m_ready"))
                residual(w, l, 16)
                layernorm(X, rest)
                wait("x_ready")
                layernorm(H, rest)
                ff(w)
                act.wait_ge(sems["hid_ready"], n.at("hid_ready"))
                residual(w, l, 40)
                layernorm(X, rest)
                wait("x_ready")

            def rms(w):
                square(M[:, :, S:T], X[:, :, S:T])
                root(aux[1], S)

            act.wait_ge(sems["b2_landed"], 32)
            for l in range(DEPTH):
                rms(S)

                def move(dst, rows=(0, P), scale=1.0):
                    o = arrived()
                    src = o[rows[0]:rows[1], 0:dst.free_size()]
                    if len(dst.shape) == 3:
                        src = src.rearrange("p (a b) -> p a b", a=dst.shape[1])
                    moved(act.activation(dst, src, ACT.Copy, scale=scale))
                for c in range(2):
                    move(w2["cq"][:, c, :])
                move(w2["ckv"][:, 0, :])
                move(w2["kr"][NOPE:QK, 0, :], (NOPE, QK))
                for name in ("gb", "gc", "uc"):
                    for c in range(2):
                        move(w2[name][:, c, :])
                for c in range(2):
                    move(w2["up"][:, c, 16:])
                for c in range(2):
                    move(w2["qs"][:, c, :])
                move(w2["ks"][:, 0, :])
                move(w2["vs"][:, :, :])
                act.wait_ge(sems["lin_evac"], n.at("lin_evac"))
                square(gate_buf[:, 0, :], w2["cq"][:, :, :].rearrange("p a b -> p (a b)"))
                square(gate_buf[:, 1, 0:S], w2["ckv"][:, 0, :])
                root(aux[0], S, 0)
                root(aux[1], S, 1)
                for h in range(MH):
                    move(w2["qh"][0:QK, h, :], (0, QK))
                for h in range(MH):
                    move(w2["kh"][0:NOPE, h, :], (0, NOPE))
                move(w2["vm"][:, :, :])
                for c in range(2):
                    move(w2["mx"][:, 4 + c, :], scale=v2(l, "pool_scale", c))
                items = []
                for h in range(MH):
                    for qt in range(QT):
                        r = 64 * (h % 2)
                        items.append((S, w2["mx"][r:r + 64, h // 2, qt * P:(qt + 1) * P], None, (r, r + 64)))
                for h in range(SH):
                    for qt in range(QT):
                        r = 64 * (h % 2)
                        items.append((S, w2["mx"][r:r + 64, 6 + h // 2, qt * P:(qt + 1) * P], v2(l, "sinks", h), (r, r + 64)))
                attention(items, None)
                act.wait_ge(sems["yb_ready"], l + 1)
                act.wait_ge(sems["o_ready"], n.at("o_ready"))
                for g in range(4):
                    square(M[:, 2 * g:2 * g + 2, S:T], w2["mx"][:, 2 * g:2 * g + 2, :])
                for g in range(4):
                    if g >= 2:
                        act.wait_ge(sems["og_ready"], n.at("og_ready") + g - 1)
                    root(aux[g % 2], S, g % 2)
                n.up("og_ready", 4)
                act.wait_ge(sems["og_ready"], n.at("og_ready"))
                residual(S, l, None)
                act.wait_ge(sems["r_ready"], n.at("r_ready"))
                rms(S)
                ff(S)
                act.wait_ge(sems["hid_ready"], n.at("hid_ready"))
                residual(S, l, None)
                act.wait_ge(sems["r_ready"], n.at("r_ready"))
            rms(S)

        @block.vector
        def _(dve):
            n = Tally()

            def wait(name, k=1):
                dve.wait_ge(sems[name], n.up(name, k))

            def chunk_at(k=1):
                dve.wait_ge(sems["lin_evac"], n.up("lin_evac", k))

            def step(ins):
                ins.then_inc(sems["dve_step"], 1)
                dve.wait_ge(sems["dve_step"], n.up("dve_step"))

            def give(name, ins):
                ins.then_inc(sems[name], 1)
                return n.up(name)

            def over(t, k):
                return t.unsqueeze(1).broadcast_to([t.shape[0], k, t.shape[1]])

            def inverse(b, w, slot=0, after=()):
                wait("std_ready")
                for name in after:
                    dve.wait_ge(sems[name], n.at(name))
                r, t = rstd[:, 0:w], tmp[:, 0:w]
                step(dve.reciprocal(r, std[:, slot, 0:w]))
                step(dve.scalar_tensor_tensor(t, b[:, 0:w], EPS, r, ALU.add, ALU.mult))
                step(dve.tensor_tensor(t, t, r, ALU.mult))
                step(dve.tensor_scalar(t, t, -0.5, 1.5, ALU.mult, ALU.add))
                step(dve.tensor_tensor(r, r, t, ALU.mult))

            def layernorm(src, dst, rng):
                w = rng[1] - rng[0]
                s, d = src[:, :, rng[0]:rng[1]], dst[:, :, rng[0]:rng[1]]
                wait("mean_done")
                k = give("xc_ready", dve.tensor_tensor(d, s, over(aux[0][:, 0:w], KC), ALU.subtract))
                inverse(aux[1], w)
                dve.wait_ge(sems["xc_ready"], k)
                step(dve.tensor_tensor(d, d, over(rstd[:, 0:w], KC), ALU.mult))

            def affine(t, rng, g, b, name):
                for c in range(KC):
                    ins = dve.tensor_scalar(t[:, c, rng[0]:rng[1]], t[:, c, rng[0]:rng[1]], g(c), b(c), ALU.mult, ALU.add)
                give(name, ins)

            def modulate(rng, shift, scale):
                for s in range(rng[0] // S, 2):
                    for c in range(KC):
                        t = H[:, c, s * S:(s + 1) * S]
                        ins = dve.tensor_scalar(t, t, mod[:, scale + c, s:s + 1], mod[:, shift + c, s:s + 1], ALU.mult, ALU.add)
                give("h_ready", ins)

            def merge(w, rng, first):
                for c in range(KC):
                    chunk_at(2)
                    m = M[:, c, rng[0]:rng[1]]
                    if first:
                        give("m_ready", dve.tensor_tensor(m, gate_buf[:, c % 2, 0:w], y_buf[:, c % 2, 0:w], ALU.mult))
                    else:
                        step(dve.tensor_tensor(y_buf[:, c % 2, 0:w], gate_buf[:, c % 2, 0:w], y_buf[:, c % 2, 0:w], ALU.mult))
                        give("m_ready", dve.tensor_tensor(m, m, y_buf[:, c % 2, 0:w], ALU.add))

            def residual(rng, alpha):
                w = rng[1] - rng[0]
                for c in range(KC):
                    chunk_at()
                    x = X[:, c, rng[0]:rng[1]]
                    k = give("r_ready", dve.scalar_tensor_tensor(x, x, alpha, gate_buf[:, c % 2, 0:w], ALU.mult, ALU.add))
                dve.wait_ge(sems["r_ready"], k)

            def post(l, rng, g, b):
                layernorm(X, X, rng)
                affine(X, rng, lambda c: v1(l, g, c), lambda c: v1(l, b, c), "x_ready")
                dve.wait_ge(sems["x_ready"], n.at("x_ready"))

            def ff(w, hid):
                def turn(i, loads, first):
                    for c in range(loads):
                        base = n.up("lin_evac", 2)
                        dve.wait_ge(sems["lin_evac"], val(base, i, 2 * SLOTS))
                        if i is None:
                            dst = hid[:, first + c, 0:w]
                        else:
                            dst = hid[:, bass.ds(i * SLOTS + (first + c), 1), 0:w].rearrange("p a t -> p (a t)")
                        dve.tensor_tensor(dst, gate_buf[:, c % 2, 0:w], y_buf[:, c % 2, 0:w], ALU.mult).then_inc(sems["hid_ready"], 1)
                turns = 2 * FC * KC // (SLOTS * TILES)
                with dve.Fori(0, turns) as i:
                    turn(i, SLOTS, 0)
                n.up("lin_evac", 2 * SLOTS * (turns - 1))
                turn(None, FC - SLOTS * turns, SLOTS * turns)
                n.up("hid_ready", FC)

            def convolve(l, streams):
                wait("pads_ready")
                wait("y_ready", 0)
                out = CV[:, :, :].rearrange("p c (s t) -> p c s t", t=S)
                base = n.at("dve_step")
                for c in range(KC):
                    dve.tensor_scalar(out[:, c, streams, :], YP[:, c, streams, 0:S], v1(l, "conv_w", c * TAPS), v1(l, "conv_b", c),
                                      ALU.mult, ALU.add).then_inc(sems["dve_step"], 1)
                at = VEC1["conv_w"][0]
                with dve.Fori(1, TAPS) as t:
                    for c in range(KC):
                        dve.wait_ge(sems["dve_step"], t * KC + (base + c + 1 - KC))
                        dve.scalar_tensor_tensor(out[:, c, streams, :], YP[:, c, streams, bass.ds(t, S)],
                                                 vec1[:, l, bass.ds(t + (at + c * TAPS), 1)], out[:, c, streams, :],
                                                 ALU.mult, ALU.add).then_inc(sems["dve_step"], 1)
                n.up("dve_step", KC * TAPS)
                dve.wait_ge(sems["dve_step"], n.at("dve_step"))

            def attention(items, scale):
                p_tile = probs if scale is not None else w2["probs"]

                def top(j):
                    w, bias, sink, qk_scale = items[j]
                    wait("s_done")
                    src = aux[j % 2][:, 0:w]
                    st = small[:, j % 2, :]
                    if scale is None:
                        src = w2["scores"][:, j % 2, 0:w]
                        step(dve.scalar_tensor_tensor(src, aux[j % 2][:, 0:w], qk_scale, bias, ALU.mult, ALU.add))
                    step(dve.reduce_max(st[:, 0:1], src, AXX))
                    if sink is not None:
                        give("nb_ready", dve.tensor_scalar(st[:, 1:2], st[:, 0:1], sink, -1.0, ALU.max, ALU.mult))
                    else:
                        give("nb_ready", dve.tensor_scalar(st[:, 1:2], st[:, 0:1], -1.0 if scale is None else -scale, None, ALU.mult))

                def normalise(j):
                    w, _, sink, _ = items[j]
                    wait("p_ready")
                    st = small[:, j % 2, :]
                    if sink is not None:
                        step(dve.tensor_tensor(st[:, 2:3], st[:, 2:3], st[:, 4:5], ALU.add))
                    step(dve.reciprocal(st[:, 3:4], st[:, 2:3]))
                    give("pn_ready", dve.tensor_scalar(p_tile[:, j % 2, 0:w], p_tile[:, j % 2, 0:w], st[:, 3:4], None, ALU.mult))
                for j in range(len(items)):
                    top(j)
                    if j >= 1:
                        normalise(j - 1)
                normalise(len(items) - 1)

            def gla(l, s):
                sl = slice(s * S, (s + 1) * S)
                full = l == 0 or s == LAT
                chunk_at(4)
                wait("ln_ready")
                step(dve.scalar_tensor_tensor(Z[:, :, :], Z[:, :, :], 0.0, B[:, :, :], ALU.min, ALU.subtract))
                for d in range(2):
                    for h in range(GH):
                        src, dst = Z[:, d * GH + h, :], B[:, d * GH + h, :]
                        if d == 1:
                            src, dst = src[:, ::-1], dst[:, ::-1]
                        ins = dve.tensor_tensor_scan(dst, src, src, 0.0, ALU.add, ALU.bypass)
                step(ins)
                if full:
                    def halves(t, half):
                        v = t.rearrange("p h (b two e) -> p (h b) two e", two=2, e=half)
                        return v[:, :, 0, :], v[:, :, 1, :]

                    def differences(j):
                        half, d = LEVELS[j // 2], j % 2
                        if j >= 2:
                            dve.wait_ge(sems["gram_done"], n.at("gram_done") + j - 1)
                        left, right = halves(B[:, d * GH:(d + 1) * GH, :], half)
                        dl, dr = halves(DL[:, j % 2], half)
                        blocks = left.shape[1]
                        if d == 0:
                            mid = left[:, :, half - 1:half].broadcast_to([P, blocks, half])
                            dve.tensor_tensor(dr, right, mid, ALU.subtract)
                            give("diff_ready", dve.tensor_tensor(dl, mid, left, ALU.subtract))
                        else:
                            mid = right[:, :, 0:1].broadcast_to([P, blocks, half])
                            dve.tensor_tensor(dl, left, mid, ALU.subtract)
                            give("diff_ready", dve.tensor_tensor(dr, mid, right, ALU.subtract))

                    def decay(j):
                        half, d = LEVELS[j // 2], j % 2
                        wait("lev_exp")
                        dl, dr = halves(DL[:, j % 2], half)
                        ql, qr = halves(QG[:, s], half)
                        kl, kr = halves(KG[:, s], half)
                        dve.tensor_tensor(dl, dl, kl if d == 0 else ql, ALU.mult)
                        give("lev_ready", dve.tensor_tensor(dr, dr, qr if d == 0 else kr, ALU.mult))

                    def place(j):
                        pair = [aux[2 * (j % 2)], aux[2 * (j % 2) + 1]]
                        dve.wait_ge(sems["gram_done"], n.at("gram_done") + j + 1)
                        if j < 2:
                            kt, qs = (0, P) if j == 0 else (1, 0)
                            give("a_copied", dve.tensor_copy(A[:, :, kt, qs:qs + P], pair[0][:, :].rearrange("p (h q) -> p h q", h=GH)))
                            return
                        dve.wait_ge(sems["a_copied"], n.at("a_copied"))
                        for kt in range(QT):
                            ins = dve.copy_predicated(A[:, :, kt, kt * P:(kt + 1) * P], over(masks[:, j - 2, :], GH),
                                                      pair[kt][:, :].rearrange("p (h q) -> p h q", h=GH))
                        give("a_copied", ins)
                    last = 2 * len(LEVELS)
                    for j in range(last):
                        differences(j)
                        if j >= 1:
                            decay(j - 1)
                        if j >= 2:
                            place(j - 2)
                    decay(last - 1)
                    place(last - 2)
                    place(last - 1)
                    place(last)
                    n.up("gram_done", last + 1)
                if s == CTX:
                    for d in range(2):
                        at = S - 1 if d == 0 else 0
                        b = B[:, d * GH:(d + 1) * GH, :]
                        ins = dve.tensor_tensor(DL[:, d], b[:, :, at:at + 1].broadcast_to([P, GH, S]), b, ALU.subtract)
                    give("hat_diff", ins)
                else:
                    give("hat_diff", dve.tensor_copy(small[:, 0, 7:8], B[:, 0, 0:1]))
                wait("hat_exp")
                t = KG if s == CTX else QG
                for d in range(2):
                    ins = dve.tensor_tensor(DL[:, d], DL[:, d], t[:, s], ALU.mult)
                give("hat_ready", ins)
                if s == CTX:
                    chunk_at(8)
                if full:
                    chunk_at(GH)

            dve.wait_ge(sems["params"], PARAMS)
            step(dve.tensor_copy(masks[:, :, :], view(arena2, 0, N_MASK, P)))
            for l in range(DEPTH):
                rest = (0, T) if l == 0 else (S, T)
                w = rest[1] - rest[0]
                streams = slice(0, 2) if l == 0 else slice(1, 2)
                chunk_at(24)
                at, _ = VEC1["b_ada"]
                step(dve.tensor_tensor(mod[:, :, :], mod[:, :, :], vec1[:, l, at:at + 48].unsqueeze(2).broadcast_to([P, 48, 2]), ALU.add))
                for c in (8, 32):
                    ins = dve.tensor_scalar(mod[:, c:c + 8, :], mod[:, c:c + 8, :], 1.0, None, ALU.add)
                step(ins)
                if l == 0:
                    dve.wait_ge(sems["x_landed"], 16)
                layernorm(X, H, (0, T))
                modulate((0, T), 0, 8)
                for c in range(KC):
                    chunk_at(2)
                    y = YP[:, c, streams, PAD:PAD + S]
                    give("y_ready", dve.tensor_tensor(y, y, gate_buf[:, c % 2, 0:w].rearrange("p (s t) -> p s t", t=S), ALU.mult))
                dve.wait_ge(sems["y_ready"], n.at("y_ready"))
                convolve(l, streams)
                ins = dve.tensor_copy(small[:, 0, 6:7], CV[:, 0, S:S + 1])
                give("conv_done", ins)
                layernorm(CV, CV, rest)
                affine(CV, rest, lambda c: v1(l, "conv_ln_g", c), lambda c: v1(l, "conv_ln_b", c), "cn_ready")
                chunk_at(2 + 8 + 2 + 8 + 4 + 4)
                merge(w, rest, True)
                heads = [(K, c, (0, T), "k_norm") for c in range(KVH)] + [(Q, c, rest, "q_norm") for c in range(HEADS)]
                base = n.at("qk_normed")

                def normed(j):
                    t, c, rng, name = heads[j]
                    wr = rng[1] - rng[0]
                    inverse(aux[j % 2], wr, j % 2, [x for x in ("qk_normed", "qk_ready") if n.at(x)])
                    x = t[:, c, rng[0]:rng[1]]
                    give("qk_normed", dve.scalar_tensor_tensor(x, x, v1(l, name), rstd[:, 0:wr], ALU.mult, ALU.mult))

                def rotated(j):
                    t, c, _, _ = heads[j]
                    wait("rot_done")
                    x = t[:, c, S:T]
                    dve.wait_ge(sems["qk_normed"], base + j + 1)
                    step(dve.tensor_tensor(x, x, c1("cos"), ALU.mult))
                    step(dve.tensor_tensor(tmp[:, 0:S], aux[2 + j % 2][:, 0:S], c1("sin"), ALU.mult))
                    give("qk_ready", dve.tensor_tensor(x, x, tmp[:, 0:S], ALU.add))
                for j in range(len(heads)):
                    normed(j)
                    if j >= 1:
                        rotated(j - 1)
                rotated(len(heads) - 1)
                items = []
                for s in ((CTX, LAT) if l == 0 else (LAT,)):
                    items += [(S if s == CTX else T, None, None, None)] * (HEADS * QT)
                attention(items, float(DH) ** -0.5)
                merge(w, rest, False)
                chunk_at(2)
                gla(l, CTX)
                gla(l, LAT)
                for h in range(GH):
                    inverse(aux[h % 2], w, h % 2, ["og_ready"] if n.at("og_ready") else [])
                    for c in range(2):
                        x = Q[:, 2 * h + c, rest[0]:rest[1]]
                        ins = dve.scalar_tensor_tensor(x, x, v1(l, "gla_norm", c), rstd[:, 0:w], ALU.mult, ALU.mult)
                    give("og_ready", ins)
                dve.wait_ge(sems["og_ready"], n.at("og_ready"))
                for c in range(KC):
                    chunk_at()
                    x = Q[:, c, rest[0]:rest[1]]
                    give("y_ready", dve.tensor_tensor(x, x, gate_buf[:, c % 2, 0:w], ALU.mult))
                merge(w, rest, False)
                residual(rest, ALPHA)
                post(l, rest, "ln1_g", "ln1_b")
                layernorm(X, H, rest)
                modulate(rest, 24, 32)
                ff(w, HID)
                residual(rest, ALPHA)
                post(l, rest, "ln2_g", "ln2_b")

            lat = (S, T)
            dve.wait_ge(sems["b2_landed"], 32)

            def rms(g, name):
                inverse(aux[1], S)
                for c in range(KC):
                    ins = dve.scalar_tensor_tensor(H[:, c, S:T], X[:, c, S:T], g(c), rstd[:, 0:S], ALU.mult, ALU.mult)
                give(name, ins)
            for l in range(DEPTH):
                rms(lambda c: v2(l, "attn_norm", c), "h_ready")
                dve.memset(w2["zp"][:, :, 0:2], 0.0)
                step(dve.memset(w2["up"][:, :, 0:16], 0.0))
                chunk_at(16)
                inverse(aux[0], S, 0, ["h_ready"])
                for c in range(2):
                    ins = dve.scalar_tensor_tensor(w2["cq"][:, c, :], w2["cq"][:, c, :], v2(l, "q_norm", c), rstd[:, 0:S], ALU.mult, ALU.mult)
                give("qk_normed", ins)
                dve.wait_ge(sems["qk_normed"], n.at("qk_normed"))
                inverse(aux[1], S, 1)
                give("qk_normed", dve.scalar_tensor_tensor(w2["ckv"][:, 0, :], w2["ckv"][:, 0, :], v2(l, "kv_norm"), rstd[:, 0:S], ALU.mult, ALU.mult))
                step(dve.tensor_tensor(w2["zp"][:, :, 2:], w2["gc"][:, :, :], w2["uc"][:, :, :], ALU.mult))
                for c in range(2):
                    y = w2["yb"][:, c, :]
                    step(dve.tensor_scalar(y, w2["zp"][:, c, 0:S], v2(l, "conv_w", c), None, ALU.mult))
                    for t in (1, 2):
                        step(dve.scalar_tensor_tensor(y, w2["zp"][:, c, t:t + S], v2(l, "conv_w", 2 * t + c), y, ALU.mult, ALU.add))
                give("yb_ready", dve.tensor_tensor(w2["mx"][:, 2:4, :], w2["yb"][:, :, :], w2["gb"][:, :, :], ALU.mult))
                prev, e = w2["up"], 16 + S
                for i, window in enumerate(POOLS):
                    cur = w2[f"p{window}"]
                    lo, sh = window - 1, window // 2
                    step(dve.tensor_tensor(cur[:, :, lo:e], prev[:, :, lo:e], prev[:, :, lo - sh:e - sh], ALU.add))
                    prev = cur
                ic = c2("inv_count").rearrange("p (c t) -> p c t", c=2)
                for i, window in enumerate(POOLS):
                    c, r = i // 2, 64 * (i % 2)
                    ins = dve.tensor_tensor(w2["pooled"][r:r + 64, c, :], w2[f"p{window}"][r:r + 64, c, 16:], ic[r:r + 64, c, :], ALU.mult)
                step(ins)
                give("pooled_ready", dve.tensor_tensor(w2["pooled"][:, :, :], w2["pooled"][:, :, :], w2["up"][:, :, 16:], ALU.subtract))
                cos, sin = c2("cos"), c2("sin")
                chunk_at(9)
                wait("rot_done")
                kr = w2["kr"][NOPE:QK, 0, :]
                step(dve.tensor_tensor(kr, kr, cos[NOPE:QK, :], ALU.mult))
                step(dve.tensor_tensor(tmp[NOPE:QK, 0:S], aux[2][NOPE:QK, 0:S], sin[NOPE:QK, :], ALU.mult))
                give("qk_ready", dve.tensor_tensor(w2["kh"][NOPE:QK, :, :], over(kr, MH), over(tmp[NOPE:QK, 0:S], MH), ALU.add))
                dve.wait_ge(sems["qk_ready"], n.at("qk_ready"))
                for h in range(MH):
                    wait("rot_done")
                    x, t = w2["qh"][0:QK, h, :], tmp[0:QK, 0:S]
                    step(dve.tensor_tensor(x, x, cos[0:QK, :], ALU.mult))
                    step(dve.tensor_tensor(t, aux[2 + (h + 1) % 2][0:QK, 0:S], sin[0:QK, :], ALU.mult))
                    give("qk_ready", dve.tensor_tensor(x, x, t, ALU.add))
                    dve.wait_ge(sems["qk_ready"], n.at("qk_ready"))
                chunk_at(2)
                items = []
                causal = c2("causal").rearrange("p (q k) -> p q k", q=QT)
                window = c2("window").rearrange("p (h q k) -> p h q k", h=SH, q=QT)
                for h in range(MH):
                    items += [(S, causal[:, qt, :], None, float(QK) ** -0.5) for qt in range(QT)]
                for h in range(SH):
                    items += [(S, window[:, h, qt, :], v2(l, "sinks", h), float(SHD) ** -0.5) for qt in range(QT)]
                attention(items, None)
                dve.wait_ge(sems["yb_ready"], n.at("yb_ready"))
                for g in range(4):
                    inverse(aux[g % 2], S, g % 2, ["og_ready"])
                    for c in range(2 * g, 2 * g + 2):
                        x = w2["mx"][:, c, :]
                        ins = dve.scalar_tensor_tensor(x, x, v2(l, "mix_norm", c), rstd[:, 0:S], ALU.mult, ALU.mult)
                    give("og_ready", ins)
                dve.wait_ge(sems["og_ready"], n.at("og_ready"))
                residual(lat, 1.0)
                rms(lambda c: v2(l, "ffn_norm", c), "h_ready")
                ff(S, HID2)
                residual(lat, 1.0)
            rms(lambda c: vec2[:, DEPTH * N_VEC2 + c:DEPTH * N_VEC2 + c + 1], "fin_ready")


def tiles(w):
    k, m = w.shape
    return w.reshape(k // P, P, m // P, P).transpose(2, 0, 1, 3)


def token_tiles(w):
    k, m = w.shape
    return w.reshape(k // P, P, m // P, P).transpose(0, 2, 1, 3).reshape(-1, P, P)


def paired(a, b):
    return np.stack([tiles(a), tiles(b)], 1)


def layer1_tiles(w):
    wi = w["w_in"]
    k, v, kg, vg, glr, q, qg, r, ca, cg, g_att, g_gla, g_conv = np.split(
        wi, np.cumsum([256, 256, 512, 1024, 32, 1024, 512, 1024, 1024, 1024, 1024, 1024]), axis=1)
    parts = [tiles(w["w_ada"]), paired(ca, cg), tiles(k), tiles(q), token_tiles(v)]
    parts += [token_tiles(vg[:, j * 2 * P:(j + 1) * 2 * P]) for j in range(4)]
    parts += [tiles(kg), tiles(qg), paired(g_conv, w["w_conv_o"]), paired(g_att, w["w_att_o"]), tiles(r),
              paired(g_gla, w["w_gla_o"]), tiles(w["w_out"]), paired(w["w_ff_gate"], w["w_ff_up"]), tiles(w["w_ff_down"])]
    return [p.reshape(-1, P, P) for p in parts], glr


def layer2_tiles(w):
    cq, ckv, kr, gb, gc, uc, up, qs, ks, vs = np.split(
        w["w_in"], np.cumsum([256, 128, 32, 256, 256, 256, 256, 256, 128]), axis=1)
    kr = np.concatenate([kr, np.zeros((D, P - ROPE), kr.dtype)], 1)
    qs = qs.reshape(D, 2, 2, SHD).transpose(0, 2, 1, 3).reshape(D, SH * SHD)
    gate, upw = np.split(w["w_gate_up"], 2, axis=1)
    parts = [tiles(x) for x in (cq, ckv, kr, gb, gc, uc, up, qs, ks)] + [token_tiles(vs), tiles(w["w_o"]), paired(gate, upw),
                                                                     tiles(w["w_down"])]
    return [p.reshape(-1, P, P) for p in parts]


def columns(*vectors):
    return np.concatenate([v.reshape(-1, P).T for v in vectors], 1)


def constants():
    eye = np.eye(P, dtype=np.float32)
    c = {"ident": eye}
    for m in (1024, 256, 128):
        c[f"mean{m}"] = np.full((P, P), 1.0 / m, np.float32)
    rot = np.zeros((P, P), np.float32)
    rot[np.arange(1, P, 2), np.arange(0, P, 2)] = -1.0
    rot[np.arange(0, P, 2), np.arange(1, P, 2)] = 1.0
    c["rot"] = rot
    t = np.arange(S)
    half = DH // 2
    inv = np.float32(10000.0) ** (-np.arange(0, half, 2, dtype=np.float32) / np.float32(half))
    ang = np.concatenate([(t // 64).astype(np.float32)[:, None] * inv, (t % 64).astype(np.float32)[:, None] * inv], -1)
    ang = np.repeat(ang.T, 2, 0).astype(np.float64)
    c["cos"], c["sin"] = np.cos(ang), np.sin(ang)
    const1 = np.concatenate([c[k] for k in CONST1], 1).astype(np.float32)

    d = {}
    rot = np.zeros((P, P), np.float32)
    h = ROPE // 2
    rot[NOPE + h + np.arange(h), NOPE + np.arange(h)] = -1.0
    rot[NOPE + np.arange(h), NOPE + h + np.arange(h)] = 1.0
    d["rot"] = rot
    inv = np.float32(1.0) / (np.float32(10000.0) ** (np.arange(0, ROPE, 2, dtype=np.float32) / np.float32(ROPE)))
    ang = (t.astype(np.float32)[:, None] * inv).astype(np.float64).T
    cos, sin = np.ones((P, S)), np.zeros((P, S))
    cos[NOPE:QK], sin[NOPE:QK] = np.concatenate([np.cos(ang)] * 2), np.concatenate([np.sin(ang)] * 2)
    d["cos"], d["sin"] = cos, sin
    count = np.ones((P, 2, S))
    for g, wdw in enumerate(POOLS):
        count[64 * (g % 2):64 * (g % 2) + 64, g // 2] = 1.0 / np.minimum(t + 1, wdw)
    d["inv_count"] = count.reshape(P, -1)
    q, k = t[:, None], t[None, :]
    d["causal"] = np.where(k <= q, 0.0, NEG).reshape(QT, P, S).transpose(1, 0, 2).reshape(P, -1)
    dist = q - k
    ok = (dist >= 0) & (dist < WINDOW)
    slopes = [2.0 ** (-8.0 * (i + 1) / SH) for i in range(SH)]
    d["window"] = np.stack([np.where(ok, -s * dist, NEG) for s in slopes]).reshape(SH, QT, P, S).transpose(2, 0, 1, 3).reshape(P, -1)
    const2 = np.concatenate([d[k] for k in CONST2], 1).astype(np.float32)

    j, i = np.arange(P)[:, None], np.arange(P)[None, :]
    masks = []
    for half in LEVELS[1:]:
        same = j // (2 * half) == i // (2 * half)
        left, right = j % (2 * half) < half, i % (2 * half) >= half
        masks += [same & left & right, (same & left & right).T]
    masks.append(i == j)
    return const1, const2, np.stack(masks, 1).astype(np.float32)


def kernel(**x):
    from concourse import bacc
    from concourse.bass_utils import run_bass_kernel_spmd

    x = {k: np.asarray(v) for k, v in x.items()}
    const1, const2, masks = constants()
    stream, glrs, vec1 = [], [], []
    for l in range(DEPTH):
        parts, glr = layer1_tiles({k: x[k][l] for k in ("w_ada", "w_in", "w_conv_o", "w_att_o", "w_gla_o", "w_out", "w_ff_gate",
                                                        "w_ff_up", "w_ff_down")})
        stream += parts
        glrs.append(glr.reshape(KC, P, 2 * RANK).transpose(1, 0, 2).reshape(P, -1))
        conv_w = x["conv_w_dw"][l].reshape(TAPS, KC, P).transpose(2, 1, 0).reshape(P, -1)
        vec1.append(np.concatenate([columns(x["b_ada"][l], x["q_norm"][l], x["k_norm"][l], x["gla_b_a"][l], x["gla_norm"][l],
                                            x["conv_b_dw"][l], x["conv_ln_g"][l], x["conv_ln_b"][l], x["ln1_g"][l], x["ln1_b"][l],
                                            x["ln2_g"][l], x["ln2_b"][l]), conv_w], 1))
    vec2, small2 = [], []
    for l in range(DEPTH):
        stream += layer2_tiles({"w_in": x["w_in_2"][l], "w_o": x["w_o_2"][l], "w_gate_up": x["w_gate_up_2"][l], "w_down": x["w_down_2"][l]})
        vec2 += [columns(x["attn_norm_2"][l], x["mla_q_norm_2"][l], x["mla_kv_norm_2"][l], x["conv_w_2"][l], x["pool_scale_2"][l],
                         x["mix_norm_2"][l], x["ffn_norm_2"][l]), np.broadcast_to(x["swa_sinks_2"][l], (P, SH))]
        pool = np.zeros((P, 2, P), np.float32)
        for g in range(4):
            r = 64 * (g % 2)
            pool[r:r + 64, g // 2, r:r + 64] = x["pool_w_2"][l, g]
        small2.append(np.concatenate([x["w_uq_2"][l].reshape(2, P, -1).transpose(1, 0, 2).reshape(P, -1), x["w_ukv_2"][l],
                                      pool.reshape(P, -1)], 1))
    vec2.append(columns(x["final_norm_2"]))
    both = np.concatenate([x["ctx"][0], x["x"][0]], 0)
    arrays = {
        "stream": np.concatenate(stream).reshape(LOADS, TILES, P, P).transpose(0, 2, 1, 3).reshape(LOADS, P, TILES * P),
        "tokens": both.T.reshape(KC, P, T).transpose(1, 0, 2),
        "cvec": np.stack([x["c_ctx"], x["c"][0]], 1).reshape(KC, P, 2).transpose(1, 0, 2),
        "vec1": np.stack(vec1, 1),
        "vec2": np.concatenate(vec2, 1),
        "w_glr": np.stack(glrs, 1),
        "w_a2": np.stack([x["gla_w_a2"][l].transpose(1, 0, 2).reshape(RANK, -1) for l in range(DEPTH)], 1),
        "const1": const1, "const2": const2,
        "small2": np.stack(small2, 1),
        "masks": masks,
    }
    arrays = {k: np.ascontiguousarray(a) for k, a in arrays.items()}
    nc = bacc.Bacc("TRN2", target_bir_lowering=False, num_devices=1)
    args = [nc.dram_tensor(f"in_{k}", a.shape, mybir.dt.from_np(a.dtype), kind="ExternalInput").ap() for k, a in arrays.items()]
    out = nc.dram_tensor("out", (P, KC, S), mybir.dt.float32, kind="ExternalOutput").ap()
    program(nc, *args, out)
    r = run_bass_kernel_spmd(nc, [{f"in_{k}": a for k, a in arrays.items()}], core_ids=[0])
    got = np.asarray(r.results[0]["out"])
    return np.ascontiguousarray(got.transpose(2, 1, 0).reshape(1, S, D))
```

```python
import concourse.bass as bass
import numpy as np
from concourse import mybir
from concourse.alu_op_type import AluOpType as ALU
from contextlib import ExitStack

P = 128
D = 1024
KC = D // P
S = 256
QT = S // P
CTX, LAT = 0, 1
DEPTH = 2
EPS = 1e-6
ALPHA = (2.0 * DEPTH) ** 0.25
HEADS, KVH, DH = 8, 2, 128
GH, GDK, GDV, RANK, TAU = 4, 128, 256, 16, 16.0
TAPS = 31
PAD = TAPS // 2
FF = 2816
FC = FF // P
HALF = FC // 2
LEVELS = (128, 64, 32, 16, 8, 4, 2, 1)
MH, NOPE, ROPE, MV = 4, 64, 32, 64
QK = NOPE + ROPE
SH, SHD = 4, 64
WINDOW = 128
POOLS = (2, 4, 8, 16)
NEG = -1e30
PER_HALF = {"lin_done": 2 * HALF + KC, "lin_evac": 2 * HALF + KC, "lo_ready": 3 * HALF, "hi_ready": 3 * HALF,
            "w_used": 3 * HALF, "s_ready": HALF, "r_ready": KC, "dve_step": 2 * HALF}
TILES = 8
SLOTS = 3
ADA_COLS = 256
ADA_CHUNKS = ADA_COLS // P
ADA_GROUPS = 6 * D // ADA_COLS
ADA_LOADS = KC * ADA_CHUNKS // TILES
ADA_FIRST = 2 * D // ADA_COLS
PASS_LOADS = 16 + 2 + 8 + 2 + 8 + 4 + 4 + 3 * 16 + 8 + 8 + 3 * FC
USED = DEPTH * ADA_GROUPS * ADA_LOADS + 3 * PASS_LOADS + (2 + 2 + 8 + 4) + DEPTH * (16 + 8 + 3 * FC)
LOADS = -(-(USED + SLOTS) // SLOTS) * SLOTS
VEC1 = {}
for _name, _n in (("b_ada", 48), ("q_norm", 1), ("k_norm", 1), ("gla_b_a", 8), ("gla_norm", 2), ("conv_b", 8),
                  ("conv_ln_g", 8), ("conv_ln_b", 8), ("ln1_g", 8), ("ln1_b", 8), ("ln2_g", 8), ("ln2_b", 8),
                  ("conv_w", 8 * TAPS)):
    VEC1[_name] = sum(n for _, n in VEC1.values()), _n
N_VEC1 = sum(n for _, n in VEC1.values())
VEC2 = {}
for _name, _n in (("attn_norm", 8), ("q_norm", 2), ("kv_norm", 1), ("conv_w", 6), ("pool_scale", 2), ("mix_norm", 8),
                  ("ffn_norm", 8), ("sinks", 4)):
    VEC2[_name] = sum(n for _, n in VEC2.values()), _n
N_VEC2 = sum(n for _, n in VEC2.values())
ROWS = 16
CONST1 = {}
for _name, _n in (("ident", P), ("mean1024", P), ("mean256", P), ("mean128", P), ("rot", P), ("cos", S), ("sin", S),
                  ("head128", (KVH + HEADS) * ROWS), ("head256", 4 * ROWS), ("pair", 2), ("alpha", 2)):
    CONST1[_name] = sum(n for _, n in CONST1.values()), _n
N_CONST1 = sum(n for _, n in CONST1.values())
CONST2 = {}
for _name, _n in (("rot", P), ("cos", S), ("sin", S), ("inv_count", 2 * S), ("causal", QT * S), ("window", SH * QT * S)):
    CONST2[_name] = sum(n for _, n in CONST2.values()), _n
N_CONST2 = sum(n for _, n in CONST2.values())
GLR = 32 + RANK
N_SMALL2 = 2 * MH * QK + MH * (NOPE + MV) + 2 * P
N_MASK = 2 * (len(LEVELS) - 1) + 1


class Tally:

    def __init__(self):
        self.of = {}

    def up(self, name, k=1):
        self.of[name] = self.of.get(name, 0) + k
        return self.of[name]

    def at(self, name):
        return self.of.get(name, 0)


def spread(units, steps):
    return [[u for k, u in enumerate(units) if k * steps // len(units) == j] for j in range(steps)]


def attention_fill(l, s):
    units = [("qg", c) for c in range(GH)] + [("glr", 0)] + [("vg", c) for c in range(GH)]
    if l == 0:
        units += [("ada", (s, g)) for g in (range(ADA_FIRST, 16) if s == CTX else range(4, 14))]
    return units


def gla_fill(l, s):
    units = [("cy", c) for c in range(KC)]
    if s == LAT:
        units += [("r", c) for c in range(KC)]
    if l == 0:
        groups = [(0, g) for g in range(16, ADA_GROUPS)] + [(1, g) for g in range(4)] if s == CTX else [(1, g) for g in range(14, ADA_GROUPS)]
        units += [("ada", g) for g in groups]
    return units

STEPS = 2 * len(LEVELS) + 1


def gla_steps(l, s):
    if l == DEPTH - 1 and s == CTX:
        return [[("kg", 2), ("kg", 3)] + [("vg", c) for c in range(GH)]]
    units = gla_fill(l, s)
    return [units[:5]] + spread(units[5:], STEPS)


def program(nc, stream, xt_in, cvec_in, vec1_in, vec2_in, glr_in, a2_in, const1_in, const2_in, small2_in, mask_in, out):
    F32 = mybir.dt.float32
    F32R = mybir.dt.float32r
    U8 = mybir.dt.uint8
    ACT = mybir.ActivationFunctionType
    AXX = mybir.AxisListType.X
    with ExitStack() as ctx:
        def sb(name, shape, dt=F32):
            return ctx.enter_context(nc.sbuf_tensor(name, shape, dt))

        def sem(name):
            return ctx.enter_context(nc.semaphore(name))

        w_raw = sb("w_raw", [P, SLOTS, TILES * P])
        w_hi = sb("w_hi", [P, SLOTS, TILES * P], F32R)
        w_lo = sb("w_lo", [P, SLOTS, TILES * P], F32R)
        X = sb("X", [P, KC, 2 * S])
        h_hi = sb("h_hi", [P, KC, S], F32R)
        h_lo = sb("h_lo", [P, KC, S], F32R)
        s_hi = sb("s_hi", [P, HALF, S], F32R)
        s_lo = sb("s_lo", [P, HALF, S], F32R)
        M = sb("M", [P, KC, S])
        arena1 = sb("arena1", [P, 10240])
        arena2 = sb("arena2", [P, 8192])
        gate_buf = sb("gate_buf", [P, 2, S])
        y_buf = sb("y_buf", [P, 2, S])
        std = sb("std", [P, 2, S])
        rstd = sb("rstd", [P, S])
        tmp = sb("tmp", [P, S])
        vec1 = sb("vec1", [P, DEPTH, N_VEC1])
        vec2 = sb("vec2", [P, DEPTH * N_VEC2 + KC])
        cvec = sb("cvec", [P, KC, 2])
        c_hl = sb("c_hl", [P, KC, 4], F32R)
        mod_rows = sb("mod_rows", [4, 2, ADA_COLS])
        mod = sb("mod", [P, DEPTH, 48, 2])
        wglr = sb("wglr", [P, DEPTH * KC * GLR])
        wglr_hi = sb("wglr_hi", [P, DEPTH * KC * GLR], F32R)
        wglr_lo = sb("wglr_lo", [P, DEPTH * KC * GLR], F32R)
        wa2 = sb("wa2", [GLR, DEPTH, GH * GDK])
        const1 = sb("const1", [P, N_CONST1])
        masks = sb("masks", [P, N_MASK, P], U8)
        small = sb("small", [P, 2, 16])

        def view(t, at, *shape):
            n = int(np.prod(shape))
            v = t[:, at:at + n]
            if len(shape) == 2:
                return v.rearrange("p (a b) -> p a b", a=shape[0])
            if len(shape) == 3:
                return v.rearrange("p (a b c) -> p a b c", a=shape[0], b=shape[1])
            if len(shape) == 4:
                return v.rearrange("p (a b c d) -> p a b c d", a=shape[0], b=shape[1], c=shape[2])
            return v

        Q = view(arena1, 0, HEADS, S)
        K = view(arena1, 2048, KVH, 2 * S)
        V = view(arena1, 3072, 2 * QT, KVH * DH)
        state = view(arena1, 4096, 2, GH, GDV)
        KG = view(arena1, 6144, GH, S)
        QG = view(arena1, 7168, GH, S)
        VG = view(arena1, 8192, QT, GH * GDV)
        YP = view(arena2, 0, KC, S + 2 * PAD)
        CV = view(arena2, KC * (S + 2 * PAD), KC, S)
        W = CV
        pt_at = KC * (2 * S + 2 * PAD)
        probs = view(arena2, pt_at, 2, 2 * S)
        probsT = view(arena2, pt_at + 4 * S, 2, 2 * QT, P)
        glr = view(arena2, pt_at + 8 * S, S)
        assert pt_at + 9 * S <= 8192
        Z = view(arena2, 0, 2 * GH, S)
        DL = view(arena2, 0, 2, GH, S)
        B = view(arena2, 2048, 2 * GH, S)
        A = view(arena2, 4096, GH, QT, S)
        KT = view(arena2, 6144, 2, QT, GH, P)
        rbuf = view(arena2, 6144, KC, S)
        gbuf = view(arena2, 2048, KC, S)
        osq = view(arena2, 0, KC, S)
        hsq = view(arena1, 7168, KVH + HEADS, S)
        a = 0
        w2 = {}
        for name, shape in (("cq", (2, S)), ("ckv", (1, S)), ("kr", (1, S)), ("qh", (MH, S)), ("kh", (MH, S)),
                            ("vm", (QT, MH * MV)), ("gb", (2, S)), ("gc", (2, S)), ("uc", (2, S)), ("zp", (2, S + 2)),
                            ("up", (2, S + 16)), ("qs", (2, S)), ("ks", (1, S))):
            w2[name] = view(arena1, a, *shape)
            a += int(np.prod(shape))
        small2 = view(arena1, 10240 - DEPTH * N_SMALL2, DEPTH, N_SMALL2)
        assert a <= 10240 - DEPTH * N_SMALL2
        a = 0
        for name, shape in (("probs", (2, 2 * S)), ("probsT", (2, 2 * QT, P)), ("scores", (2, 2 * S)), ("p2", (2, S + 16)),
                            ("p4", (2, S + 16))):
            w2[name] = view(arena2, a, *shape)
            a += int(np.prod(shape))
        assert a + N_CONST2 <= 8192
        const2 = arena2[:, 8192 - N_CONST2:8192]
        w2["p8"] = view(arena2, 0, 2, S + 16)
        w2["p16"] = view(arena2, 1024, 2, S + 16)
        w2["pooled"] = view(arena2, 2048, 2, S)
        w2["vs"] = M[:, 0, :].rearrange("p (a b) -> p a b", a=QT)
        w2["vf"] = M[:, 1, :]
        w2["mx"] = X[:, :, 0:S]

        def c1(name):
            at, n = CONST1[name]
            return const1[:, at:at + n]

        def c2(name):
            at, n = CONST2[name]
            return const2[:, at:at + n]

        def v1(l, name, c=0):
            at = VEC1[name][0] + c
            return vec1[:, l, at:at + 1]

        def v2(l, name, c=0):
            at = l * N_VEC2 + VEC2[name][0] + c
            return vec2[:, at:at + 1]

        lin = [ctx.enter_context(nc.psum_tensor(f"lin{i}", [P, 512], F32)) for i in range(4)]
        aux = [ctx.enter_context(nc.psum_tensor(f"aux{i}", [P, 512], F32)) for i in range(4)]

        landed = [sem(f"landed{i}") for i in range(SLOTS)]
        NAMES = ("hi_ready",
                 "lo_ready",
                 "w_used",
                 "lin_done",
                 "lin_evac",
                 "params", "c_landed", "x_landed", "b2_landed", "stored",
                 "c_ready",
                 "glr_split",
                 "silu_ready",
                 "x_ready", "r_ready",
                 "mean_done", "xc_ready", "sq_ready", "var_done", "std_ready",
                 "t_ready", "hi_part", "h_ready",
                 "y_ready", "conv_done", "cv32_ready", "m_ready",
                 "s_ready",
                 "row_ready", "spread_done", "qk_normed", "rot_done", "qk_ready",
                 "s_done", "nb_ready", "p_ready", "pn_ready", "pt_done", "pt_ready", "o_done", "o_hi", "o_ready",
                 "ln_ready", "diff_ready", "lev_exp", "lev_ready", "gram_done", "a_copied", "hat_diff", "hat_exp", "hat_ready",
                 "og_ready", "dve_step", "act_step", "pooled_ready", "yb_ready", "fin_ready")
        sems = {name: sem(name) for name in NAMES}
        block = ctx.enter_context(nc.Block())

        class Place:

            def __init__(self):
                self.n = Tally()
                self.tile = 0
                self.bank = 0
                self.split = 0
                self.tile_done = 0
                self.turn = None

            def value(self, name, base):
                if self.turn is None or not PER_HALF.get(name):
                    return base
                return self.turn * PER_HALF[name] + base

            def up(self, name, k=1):
                return self.value(name, self.n.up(name, k))

            def now(self, name):
                return self.value(name, self.n.at(name))

            def next_bank(self):
                b = self.bank
                self.bank = (b + 1) % 4
                return lin[b]

            def enter(self, i):
                self.turn = i
                self.start = dict(self.n.of)
                self.first = self.tile, self.split

            def leave(self):
                self.turn = None
                for name, k in PER_HALF.items():
                    if self.n.at(name) != self.start.get(name, 0):
                        assert self.n.at(name) - self.start.get(name, 0) == k, (name, self.n.at(name) - self.start.get(name, 0), k)
                        self.n.up(name, k)
                self.split += self.split - self.first[1]
                self.tile += self.tile - self.first[0]
                self.tile_done = self.tile

        PARAMS = 16 * 5

        @block.sync
        def _(sp):
            sp.dma_start(cvec[:, :, :], cvec_in).then_inc(sems["c_landed"], 16)
            sp.dma_start(X[:, :, :], xt_in).then_inc(sems["x_landed"], 16)
            sp.dma_start(const1[:, :], const1_in).then_inc(sems["x_landed"], 16)
            for s in range(SLOTS):
                sp.dma_start(w_raw[:, s, :], stream[s]).then_inc(landed[s], 16)
            sp.dma_start(vec1[:, :, :], vec1_in).then_inc(sems["params"], 16)
            sp.dma_start(wglr[:, :], glr_in).then_inc(sems["params"], 16)
            sp.dma_start(wa2[:, :, :], a2_in).then_inc(sems["params"], 16)
            sp.dma_start(view(arena2, pt_at, N_MASK, P), mask_in).then_inc(sems["params"], 16)
            sp.dma_start(vec2[:, :], vec2_in).then_inc(sems["params"], 16)
            with sp.Fori(1, LOADS // SLOTS) as i:
                for s in range(SLOTS):
                    sp.wait_ge(sems["lo_ready"], i * SLOTS + (s + 1 - SLOTS))
                    sp.dma_start(w_raw[:, s, :], stream[bass.ds(i * SLOTS + s, 1)].rearrange("a p n -> p (a n)")
                                 ).then_inc(landed[s], 16)
            sp.wait_ge(sems["fin_ready"], 1)
            sp.dma_start(out, W[:, :, :]).then_inc(sems["stored"], 16)
            sp.wait_ge(sems["stored"], 16)

        @block.gpsimd
        def _(pool):
            with pool.Fori(0, LOADS // SLOTS) as i:
                for s in range(SLOTS):
                    pool.wait_ge(sems["hi_ready"], i * SLOTS + (s + 1))
                    pool.tensor_tensor(w_lo[:, s, :], w_raw[:, s, :], w_hi[:, s, :].bitcast(F32), ALU.subtract
                                       ).then_inc(sems["lo_ready"], 1)

        @block.tensor
        def _(pe):
            at = Place()
            n = at.n

            def weight(tiles=1):
                t = at.tile
                at.tile += tiles
                load, k = divmod(t, TILES)
                if k == 0:
                    pe.wait_ge(sems["lo_ready"], at.value("lo_ready", load + 1))
                cols = slice(k * P, (k + tiles) * P)
                return w_hi[:, load % SLOTS, cols], w_lo[:, load % SLOTS, cols], k == 0 and load > 0

            def used(mm, first):
                if first:
                    mm.then_inc(sems["w_used"], 1)

            def bank():
                c = n.up("lin_done")
                if c > 4:
                    pe.wait_ge(sems["lin_evac"], at.value("lin_evac", c - 4))
                return at.next_bank()

            def done(mm):
                mm.then_inc(sems["lin_done"], 1)

            def dense(hi, lo, ready=None, kcs=KC):
                o = bank()[:, 0:S]
                for k in range(kcs):
                    whi, wlo, first = weight()
                    if ready:
                        pe.wait_ge(sems[ready[0]], at.value(ready[0], ready[1] + k + 1))
                    used(pe.matmul(o, whi, hi[:, k, :], start=k == 0, stop=False), first)
                    pe.matmul(o, whi, lo[:, k, :], start=False, stop=False)
                    mm = pe.matmul(o, wlo, hi[:, k, :], start=False, stop=k == kcs - 1)
                done(mm)

            def dense_together(chunks, ready):
                banks, start = [bank() for _ in range(chunks)], at.tile
                for k in range(KC):
                    pe.wait_ge(sems[ready[0]], at.value(ready[0], ready[1] + k + 1))
                    for c, o in enumerate(banks):
                        at.tile = start + c * KC + k
                        whi, wlo, first = weight()
                        mm = pe.matmul(o[:, 0:S], whi, h_hi[:, k, :], start=k == 0, stop=False)
                        used(mm, first if c == 0 else k == KC - 1)
                        pe.matmul(o[:, 0:S], whi, h_lo[:, k, :], start=False, stop=False)
                        mm = pe.matmul(o[:, 0:S], wlo, h_hi[:, k, :], start=False, stop=k == KC - 1)
                        if k == KC - 1:
                            done(mm)

            def token_major():
                banks = [bank(), bank()]
                for k in range(KC):
                    whi, wlo, first = weight(2)
                    for tt, o in enumerate(banks):
                        xhi, xlo = h_hi[:, k, tt * P:(tt + 1) * P], h_lo[:, k, tt * P:(tt + 1) * P]
                        mm = pe.matmul(o[:, 0:2 * P], xhi, whi, start=k == 0, stop=False)
                        used(mm, first and tt == 0)
                        pe.matmul(o[:, 0:2 * P], xhi, wlo, start=False, stop=False)
                        mm = pe.matmul(o[:, 0:2 * P], xlo, whi, start=False, stop=k == KC - 1)
                        if k == KC - 1:
                            done(mm)

            ada_open = []

            def ada(group):
                o = bank()
                for k in range(KC):
                    whi, wlo, first = weight(ADA_CHUNKS)
                    used(pe.matmul(o[0:4, 0:ADA_COLS], c_hl[:, k, :], whi, start=k == 0, stop=False), first)
                    mm = pe.matmul(o[0:4, 0:ADA_COLS], c_hl[:, k, :], wlo, start=False, stop=k == KC - 1)
                done(mm)
                rows_moved, b = n.at("lin_done"), len(ada_open) % 2
                ada_open.append(rows_moved)
                o = bank()
                pe.wait_ge(sems["lin_evac"], at.value("lin_evac", rows_moved))
                for c in range(ADA_CHUNKS):
                    mm = pe.matmul(o[:, 2 * c:2 * c + 2], mod_rows[:, b, c * P:(c + 1) * P], c1("pair")[0:4, :], start=True, stop=True)
                done(mm)

            def unit(l, s, u):
                kind, c = u
                if kind in ("qg", "kg", "r"):
                    dense(h_hi, h_lo)
                elif kind == "cy":
                    dense(s_hi, s_lo, ("s_ready", n.at("s_ready") - KC))
                elif kind == "vg":
                    token_major()
                elif kind == "glr":
                    o = bank()
                    for k in range(KC):
                        a = (l * KC + k) * GLR
                        pe.matmul(o[0:GLR, 0:S], wglr_hi[:, a:a + GLR], h_hi[:, k, :], start=k == 0, stop=False)
                        pe.matmul(o[0:GLR, 0:S], wglr_hi[:, a:a + GLR], h_lo[:, k, :], start=False, stop=False)
                        mm = pe.matmul(o[0:GLR, 0:S], wglr_lo[:, a:a + GLR], h_hi[:, k, :], start=False, stop=k == KC - 1)
                    done(mm)
                else:
                    ada(c)

            def mean_chunk(x, k):
                mm = pe.matmul(aux[0][:, 0:S], c1("mean1024"), x[:, k, :], start=k == 0, stop=k == KC - 1)
                if k == KC - 1:
                    mm.then_inc(sems["mean_done"], 1)

            def variance(squares):
                for k in range(KC):
                    if k % 2 == 0:
                        pe.wait_ge(sems["sq_ready"], at.up("sq_ready"))
                    mm = pe.matmul(aux[1][:, 0:S], c1("mean1024"), squares[:, k, :], start=k == 0, stop=k == KC - 1)
                mm.then_inc(sems["var_done"], 1)

            def layernorm(x, ready=None):
                for k in range(KC):
                    if ready:
                        pe.wait_ge(sems[ready], at.up(ready))
                    mean_chunk(x, k)
                variance(M)

            def head_rows(chunks):
                for j, (name, h, squares) in enumerate(chunks):
                    a = h * ROWS
                    mm = pe.matmul(aux[0][0:ROWS, 0:S], c1(name)[:, a:a + ROWS], squares, start=j == 0, stop=j == len(chunks) - 1)
                mm.then_inc(sems["var_done"], 1)

            def spread_row(o, h):
                return pe.matmul(o, c1("ident")[0:ROWS, h:h + 1].broadcast_to([ROWS, P]), rstd[0:ROWS, :], start=True, stop=True)

            def rotate(heads, j, q0, r0):
                pe.wait_ge(sems["qk_normed"], at.value("qk_normed", q0 + j + 1))
                if j >= 2:
                    pe.wait_ge(sems["qk_ready"], at.value("qk_ready", r0 + j - 1))
                pe.matmul(aux[3 * (j % 2)][:, 0:S], c1("rot"), heads[j][0], start=True, stop=True).then_inc(sems["rot_done"], 1)

            def attention(items, p_tile, pt_tile, fill, run):
                def scores(j):
                    qs, keys, _, _ = items[j]
                    if j >= 2:
                        pe.wait_ge(sems["p_ready"], at.value("p_ready", n.at("p_ready") + j - 1))
                    w = 2 * S // len(qs)
                    for g, q in enumerate(qs):
                        mm = pe.matmul(aux[j % 2][:, g * w:(g + 1) * w], q, keys, start=True, stop=True)
                    mm.then_inc(sems["s_done"], 1)

                def transposes(j):
                    pe.wait_ge(sems["pn_ready"], at.up("pn_ready"))
                    if j >= 1:
                        pe.wait_ge(sems["pt_ready"], pt0 + j)
                    for k in range(4):
                        mm = pe.transpose(aux[2][:, k * P:(k + 1) * P], p_tile[:, j % 2, k * P:(k + 1) * P], c1("ident"))
                    mm.then_inc(sems["pt_done"], 1)

                def values(j):
                    qs, _, vs, rows = items[j]
                    pe.wait_ge(sems["pt_ready"], pt0 + j + 1)
                    if j >= 1:
                        pe.wait_ge(sems["o_ready"], at.up("o_ready"))
                    per = 4 // len(qs)
                    for g in range(len(qs)):
                        for k in range(per):
                            mm = pe.matmul(aux[3][rows[0]:rows[1], g * P:(g + 1) * P], vs[k], pt_tile[:, j % 2, g * per + k, :],
                                           start=k == 0, stop=k == per - 1)
                    mm.then_inc(sems["o_done"], 1)
                pt0 = n.at("pt_ready")
                for j in range(len(items)):
                    scores(j)
                    for u in fill[j]:
                        run(u)
                    if j >= 1:
                        transposes(j - 1)
                    if j >= 2:
                        values(j - 2)
                transposes(len(items) - 1)
                values(len(items) - 2)
                values(len(items) - 1)
                n.up("pt_ready", len(items))
                n.up("p_ready", len(items))
                pe.wait_ge(sems["o_ready"], at.up("o_ready"))

            def residual(hi, lo, ready, x):
                for c in range(KC):
                    dense(hi, lo, ready if c == 0 else None)
                    if c >= 2:
                        pe.wait_ge(sems["r_ready"], at.up("r_ready"))
                        mean_chunk(x, c - 2)
                for c in range(KC - 2, KC):
                    pe.wait_ge(sems["r_ready"], at.up("r_ready"))
                    mean_chunk(x, c)

            def feed_forward(x):
                h0 = n.at("h_ready") - KC
                with pe.Fori(0, 2) as i:
                    at.enter(i)
                    pe.wait_ge(sems["lin_evac"], at.value("lin_evac", n.at("lin_done")))
                    at.bank = 0
                    dense_together(2, ("h_ready", h0))
                    for c in range(2, 2 * HALF):
                        dense(h_hi, h_lo)
                    s0 = n.at("s_ready")
                    n.up("s_ready", HALF)
                    for c in range(KC):
                        dense(s_hi, s_lo, ("s_ready", s0) if c == 0 else None, kcs=HALF)
                    n.up("r_ready", KC)
                    at.leave()
                for c in range(KC if x is not None else 0):
                    pe.wait_ge(sems["r_ready"], n.at("r_ready") - KC + c + 1)
                    mean_chunk(x, c)

            def gla(l, s, full):
                fill = gla_steps(l, s)
                for j in range(4):
                    o = bank()
                    for k in range(2):
                        d, h = divmod(2 * j + k, GH)
                        mm = pe.matmul(o[:, k * S:(k + 1) * S], wa2[32 * d:32 * d + RANK, l, h * GDK:(h + 1) * GDK],
                                       glr[32 * d:32 * d + RANK, :], start=True, stop=True)
                    done(mm)
                for u in fill[0]:
                    unit(l, s, u)
                if full:
                    a0 = n.at("a_copied")
                    for j in range(STEPS):
                        for u in fill[j + 1]:
                            unit(l, s, u)
                        pair = [aux[2 * (j % 2)], aux[2 * (j % 2) + 1]]
                        if j < STEPS - 1:
                            pe.wait_ge(sems["lev_ready"], at.up("lev_ready"))
                        if j >= 2:
                            pe.wait_ge(sems["a_copied"], at.value("a_copied", a0 + j - 1))
                        if j < 2:
                            ks, qs = (0, P) if j == 0 else (P, 0)
                            for h in range(GH):
                                mm = pe.matmul(pair[0][:, h * P:(h + 1) * P], DL[:, j % 2, h, ks:ks + P],
                                               DL[:, j % 2, h, qs:qs + P], start=True, stop=True)
                        elif j < STEPS - 1:
                            for kt in range(QT):
                                for h in range(GH):
                                    part = DL[:, j % 2, h, kt * P:(kt + 1) * P]
                                    mm = pe.matmul(pair[kt][:, h * P:(h + 1) * P], part, part, start=True, stop=True)
                        else:
                            for kt in range(QT):
                                for h in range(GH):
                                    tok = slice(kt * P, (kt + 1) * P)
                                    for rep in range(2):
                                        mm = pe.matmul(pair[kt][:, h * P:(h + 1) * P], KG[:, h, tok], QG[:, h, tok],
                                                       start=rep == 0, stop=rep == 1)
                        mm.then_inc(sems["gram_done"], 1)
                    n.up("a_copied", STEPS)
                pe.wait_ge(sems["hat_ready"], at.up("hat_ready"))
                if s == CTX:
                    for d in range(2):
                        for kt in range(QT):
                            o = bank()
                            for h in range(GH):
                                mm = pe.transpose(o[:, h * P:(h + 1) * P], DL[:, d, h, kt * P:(kt + 1) * P], c1("ident"))
                            done(mm)
                    pe.wait_ge(sems["lin_evac"], at.value("lin_evac", n.at("lin_done")))
                    for j in range(4):
                        o = bank()
                        for k in range(2):
                            d, h = divmod(2 * j + k, GH)
                            for kt in range(QT):
                                mm = pe.matmul(o[:, k * GDV:(k + 1) * GDV], KT[:, d, kt, h, :],
                                               VG[:, kt, h * GDV:(h + 1) * GDV], start=kt == 0, stop=kt == QT - 1)
                        done(mm)
                if full:
                    pe.wait_ge(sems["a_copied"], at.value("a_copied", n.at("a_copied")))
                    for h in range(GH):
                        o = bank()
                        for c in range(2):
                            e = h * GDV + c * P
                            for kt in range(QT):
                                mm = pe.matmul(o[:, c * S:(c + 1) * S], VG[:, kt, e:e + P], A[:, h, kt, :],
                                               start=kt == 0, stop=kt == QT - 1 and s == CTX)
                            if s == LAT:
                                for d in range(2):
                                    mm = pe.matmul(o[:, c * S:(c + 1) * S], state[:, d, h, c * P:(c + 1) * P],
                                                   DL[:, d, h, :], start=False, stop=d == 1)
                        done(mm)

            pe.wait_ge(sems["x_landed"], 2 * 16)
            for l in range(DEPTH):
                for s in (CTX, LAT):
                    full = l == 0 or s == LAT
                    x = X[:, :, s * S:(s + 1) * S]
                    ready = "h_ready", n.at("h_ready")
                    layernorm(x)
                    if l == 0 and s == CTX:
                        pe.wait_ge(sems["c_ready"], at.up("c_ready", 2))
                        for g in range(ADA_FIRST):
                            ada((0, g))
                        pe.wait_ge(sems["glr_split"], at.up("glr_split", 2))
                    n.up("h_ready", KC)
                    if full:
                        dense_together(2, ready)
                        for c in range(2, 2 * KC):
                            dense(h_hi, h_lo)
                        for c in range(KVH + HEADS):
                            dense(h_hi, h_lo)
                    else:
                        dense_together(KVH, ready)
                    token_major()
                    if not full:
                        unit(l, s, ("glr", 0))
                    heads = [(K[:, c, s * S:(s + 1) * S], c) for c in range(KVH)] + [(Q[:, c, :], KVH + c) for c in range(HEADS) if full]
                    pe.wait_ge(sems["sq_ready"], at.up("sq_ready"))
                    head_rows([("head128", c, hsq[:, c, :]) for _, c in heads])
                    for c in range(GH if full else 2):
                        dense(h_hi, h_lo)
                    pe.wait_ge(sems["row_ready"], at.up("row_ready"))
                    q0, r0 = n.at("qk_normed"), n.at("qk_ready")
                    for j in range(len(heads)):
                        if j >= 2:
                            pe.wait_ge(sems["qk_normed"], at.value("qk_normed", q0 + j - 1))
                        spread_row(aux[1 + j % 2][:, 0:S], heads[j][1]).then_inc(sems["spread_done"], 1)
                        if s == LAT and j >= 1:
                            rotate(heads, j - 1, q0, r0)
                    if s == LAT:
                        rotate(heads, len(heads) - 1, q0, r0)
                        n.up("qk_ready", len(heads))
                        pe.wait_ge(sems["qk_ready"], at.value("qk_ready", n.at("qk_ready")))
                    n.up("qk_normed", len(heads))
                    pe.wait_ge(sems["qk_normed"], at.value("qk_normed", n.at("qk_normed")))
                    if full:
                        items = []
                        for h in range(HEADS):
                            g = h // (HEADS // KVH)
                            if s == CTX:
                                items.append(([Q[:, h, qt * P:(qt + 1) * P] for qt in range(QT)], K[:, g, 0:S],
                                              [V[:, kt, g * DH:(g + 1) * DH] for kt in range(QT)], (0, P)))
                            else:
                                items += [([Q[:, h, qt * P:(qt + 1) * P]], K[:, g, :],
                                           [V[:, kt, g * DH:(g + 1) * DH] for kt in range(2 * QT)], (0, P)) for qt in range(QT)]
                        attention(items, probs, probsT, spread(attention_fill(l, s), len(items)), lambda u: unit(l, s, u))
                        pe.wait_ge(sems["conv_done"], at.up("conv_done"))
                        for k in range(KC):
                            mean_chunk(CV, k)
                        for c in range(KC):
                            dense(h_hi, h_lo)
                            dense(s_hi, s_lo)
                            if c == 3:
                                variance(osq)
                        for c in range(KC):
                            dense(h_hi, h_lo)
                        n.up("s_ready", KC)
                    pe.wait_ge(sems["lin_evac"], at.value("lin_evac", n.at("lin_done")))
                    gla(l, s, full)
                    if not full:
                        continue
                    pe.wait_ge(sems["sq_ready"], at.up("sq_ready"))
                    head_rows([("head256", c // 2, osq[:, c, :]) for c in range(KC)])
                    first = KC if s == CTX else 0
                    for c in range(first + KC):
                        dense(h_hi, h_lo)
                        if c == 4:
                            pe.wait_ge(sems["row_ready"], at.up("row_ready"))
                            for h in range(GH):
                                mm = spread_row(aux[1 + h // 2][:, h % 2 * S:h % 2 * S + S], h)
                                if h % 2:
                                    mm.then_inc(sems["spread_done"], 1)
                    ready = "s_ready", n.at("s_ready")
                    n.up("s_ready", KC)
                    for c in range(KC):
                        dense(s_hi, s_lo, ready if c == 0 else None)
                    ready = "h_ready", n.at("h_ready")
                    n.up("h_ready", KC)
                    residual(h_hi, h_lo, ready, x)
                    variance(M)
                    layernorm(x, "x_ready")
                    n.up("h_ready", KC)
                    feed_forward(x)
                    variance(M)
                    n.up("x_ready", KC)

            x = X[:, :, S:2 * S]
            pe.wait_ge(sems["b2_landed"], 32)
            for l in range(DEPTH):
                variance(M)
                ready = "h_ready", n.at("h_ready")
                n.up("h_ready", KC)
                dense_together(2, ready)
                dense(h_hi, h_lo)
                dense(h_hi, h_lo)
                for c in range(12):
                    dense(h_hi, h_lo)
                    if c == 3:
                        pe.wait_ge(sems["sq_ready"], at.up("sq_ready", 2))
                        for k in range(2):
                            mm = pe.matmul(aux[0][:, 0:S], c1("mean256"), gate_buf[:, k, :], start=k == 0, stop=k == 1)
                        mm.then_inc(sems["var_done"], 1)
                        pe.matmul(aux[1][:, 0:S], c1("mean128"), y_buf[:, 0, :], start=True, stop=True).then_inc(sems["var_done"], 1)
                pe.wait_ge(sems["qk_normed"], at.up("qk_normed", 2))
                wuq = small2[:, l, 0:2 * MH * QK]
                wukv = small2[:, l, 2 * MH * QK:2 * MH * QK + MH * (NOPE + MV)]
                wpool = small2[:, l, 2 * MH * QK + MH * (NOPE + MV):N_SMALL2]
                for h in range(MH):
                    o = bank()
                    for k in range(2):
                        a = (k * MH + h) * QK
                        mm = pe.matmul(o[0:QK, 0:S], wuq[:, a:a + QK], w2["cq"][:, k, :], start=k == 0, stop=k == 1)
                    done(mm)
                for h in range(MH):
                    o = bank()
                    a = h * (NOPE + MV)
                    done(pe.matmul(o[0:NOPE, 0:S], wukv[:, a:a + NOPE], w2["ckv"][:, 0, :], start=True, stop=True))
                o = bank()
                vcols = wukv.rearrange("p (h e) -> p h e", h=MH)[:, :, NOPE:]
                for tt in range(QT):
                    mm = pe.matmul(o[:, tt * MH * MV:(tt + 1) * MH * MV], w2["ckv"][:, 0, tt * P:(tt + 1) * P], vcols,
                                   start=True, stop=True)
                done(mm)
                o = bank()
                for tt in range(QT):
                    mm = pe.transpose(o[:, tt * P:(tt + 1) * P], w2["vf"][:, tt * P:(tt + 1) * P], c1("ident"))
                done(mm)
                rot = c2("rot")
                pe.wait_ge(sems["lin_evac"], at.value("lin_evac", n.at("lin_done")))
                pe.matmul(aux[2][NOPE:QK, 0:S], rot[NOPE:QK, NOPE:QK], w2["kr"][NOPE:QK, 0, :], start=True, stop=True
                          ).then_inc(sems["rot_done"], 1)
                for h in range(MH):
                    if h >= 1:
                        pe.wait_ge(sems["qk_ready"], at.value("qk_ready", n.at("qk_ready") + h))
                    pe.matmul(aux[2 + (h + 1) % 2][0:QK, 0:S], rot[0:QK, 0:QK], w2["qh"][0:QK, h, :], start=True, stop=True
                              ).then_inc(sems["rot_done"], 1)
                pe.wait_ge(sems["pooled_ready"], at.up("pooled_ready"))
                for c in range(2):
                    o = bank()
                    done(pe.matmul(o[:, 0:S], wpool[:, c * P:(c + 1) * P], w2["pooled"][:, c, :], start=True, stop=True))
                pe.wait_ge(sems["qk_ready"], at.up("qk_ready", MH + 1))
                items = []
                for h in range(MH):
                    items.append(([w2["qh"][0:QK, h, qt * P:(qt + 1) * P] for qt in range(QT)], w2["kh"][0:QK, h, :],
                                  [w2["vm"][:, kt, h * MV:(h + 1) * MV] for kt in range(QT)], (64 * (h % 2), 64 * (h % 2) + 64)))
                for h in range(SH):
                    g, j = divmod(h, 2)
                    items.append(([w2["qs"][64 * g:64 * g + 64, j, qt * P:(qt + 1) * P] for qt in range(QT)],
                                  w2["ks"][64 * g:64 * g + 64, 0, :],
                                  [w2["vs"][:, kt, g * SHD:(g + 1) * SHD] for kt in range(QT)], (64 * (h % 2), 64 * (h % 2) + 64)))
                attention(items, w2["probs"], w2["probsT"], [[]] * len(items), None)
                pe.wait_ge(sems["sq_ready"], at.up("sq_ready", 4))
                head_rows([("head256", c // 2, M[:, c, :]) for c in range(KC)])
                pe.wait_ge(sems["row_ready"], at.up("row_ready"))
                for h in range(4):
                    mm = spread_row(aux[1 + h // 2][:, h % 2 * S:h % 2 * S + S], h)
                    if h % 2:
                        mm.then_inc(sems["spread_done"], 1)
                ready = "s_ready", n.at("s_ready")
                n.up("s_ready", KC)
                for c in range(KC):
                    dense(s_hi, s_lo, ready if c == 0 else None)
                n.up("r_ready", KC)
                variance(M)
                n.up("h_ready", KC)
                feed_forward(None)
            variance(M)

        @block.scalar
        def _(act):
            at = Place()
            n = at.n

            def split_to(load):
                while at.split < load:
                    m = at.split
                    at.split += 1
                    slot, turn = m % SLOTS, m // SLOTS
                    add = 16 * (turn + 1)
                    act.wait_ge(landed[slot], add if at.turn is None else at.turn * (16 * HALF) + add)
                    if m - SLOTS >= at.tile_done // TILES:
                        act.wait_ge(sems["w_used"], at.value("w_used", m - SLOTS + 1))
                    act.activation(w_hi[:, slot, :], w_raw[:, slot, :], ACT.Copy).then_inc(sems["hi_ready"], 1)

            def arrived(tiles=KC):
                at.tile += tiles
                if tiles:
                    split_to((at.tile - 1) // TILES + SLOTS)
                act.wait_ge(sems["lin_done"], at.up("lin_done"))
                at.tile_done = at.tile
                n.up("lin_evac")
                return at.next_bank()

            def moved(ins):
                ins.then_inc(sems["lin_evac"], 1)
                split_to(at.tile // TILES + SLOTS)

            def step(ins):
                ins.then_inc(sems["act_step"], 1)
                act.wait_ge(sems["act_step"], n.up("act_step"))

            def root(b, rows=P, slot=0):
                act.wait_ge(sems["var_done"], at.up("var_done"))
                act.activation(std[0:rows, slot, :], b[0:rows, 0:S], ACT.Sqrt, bias=EPS).then_inc(sems["std_ready"], 1)
                n.up("std_ready")

            def squares(src, dst, ready=None, pieces=range(0, KC, 2)):
                for p in pieces:
                    if ready:
                        act.wait_ge(sems[ready], at.up(ready))
                    act.activation(dst[:, p:p + 2, :], src[:, p:p + 2, :], ACT.Square).then_inc(sems["sq_ready"], 1)
                    n.up("sq_ready")

            def high_parts(shift=None):
                for c in range(KC):
                    act.wait_ge(sems["t_ready"], at.up("t_ready"))
                    act.activation(h_hi[:, c, :], W[:, c, :], ACT.Identity if shift else ACT.Copy,
                                                   bias=shift(c) if shift else 0.0).then_inc(sems["hi_part"], 1)
                    n.up("hi_part")

            def modulated(l, s, shift, before=None):
                squares(W, M, "xc_ready")
                root(aux[1])
                if before:
                    before()
                high_parts(lambda c: mod[:, l, shift + c, s:s + 1])

            def post(l, x, b):
                squares(W, M, "xc_ready")
                root(aux[1])
                for c in range(KC):
                    act.wait_ge(sems["t_ready"], at.up("t_ready"))
                    act.activation(x[:, c, :], W[:, c, :], ACT.Identity, bias=v1(l, b, c)).then_inc(sems["x_ready"], 1)
                    n.up("x_ready")

            def buffered(c, name):
                if c >= 2:
                    act.wait_ge(sems[name], at.value(name, n.at(name) - KC + c - 1))

            def residual(gate):
                r0 = n.at("r_ready")
                n.up("r_ready", KC)
                for c in range(KC):
                    o = arrived()
                    if c >= 2:
                        act.wait_ge(sems["r_ready"], at.value("r_ready", r0 + c - 1))
                    if gate is None:
                        moved(act.activation(gate_buf[:, c % 2, :], o[:, 0:S], ACT.Copy))
                    else:
                        moved(act.activation(gate_buf[:, c % 2, :], o[:, 0:S], ACT.Copy, scale=gate(c)))

            def feed_forward(gate):
                with act.Fori(0, 2) as i:
                    at.enter(i)
                    at.bank = 0
                    act.wait_ge(sems["r_ready"], at.value("r_ready", n.at("r_ready")))
                    s0 = n.at("s_ready")
                    n.up("s_ready", HALF)
                    for c in range(HALF):
                        o = arrived()
                        if c >= 2:
                            act.wait_ge(sems["s_ready"], at.value("s_ready", s0 + c - 1))
                        moved(act.activation(gate_buf[:, c % 2, :], o[:, 0:S], ACT.Silu))
                        o = arrived()
                        moved(act.activation(y_buf[:, c % 2, :], o[:, 0:S], ACT.Copy))
                    r0 = n.at("r_ready")
                    n.up("r_ready", KC)
                    for c in range(KC):
                        o = arrived(HALF)
                        if c >= 2:
                            act.wait_ge(sems["r_ready"], at.value("r_ready", r0 + c - 1))
                        if gate is None:
                            moved(act.activation(gate_buf[:, c % 2, :], o[:, 0:S], ACT.Copy))
                        else:
                            moved(act.activation(gate_buf[:, c % 2, :], o[:, 0:S], ACT.Copy, scale=gate(c)))
                    at.leave()

            def attention(items, scale, p_tile, pt_tile, high, fill, run):
                def soft(j):
                    groups, _, sink, _ = items[j]
                    act.wait_ge(sems["nb_ready"], at.up("nb_ready"))
                    w = 2 * S // groups
                    st = small[:, j % 2, :]
                    if sink is not None:
                        for g in range(groups):
                            act.activation(st[:, 8 + g:9 + g], sink, ACT.Exp, bias=st[:, 2 + g:3 + g])
                    src = aux[j % 2] if scale is not None else w2["scores"][:, j % 2, :]
                    for g in range(groups):
                        ins = act.activation(p_tile[:, j % 2, g * w:(g + 1) * w], src[:, g * w:(g + 1) * w], ACT.Exp,
                                             scale=1.0 if scale is None else scale, bias=st[:, 2 + g:3 + g],
                                             accum_out=st[:, 4 + g:5 + g])
                    ins.then_inc(sems["p_ready"], 1)
                    n.up("p_ready")

                def move_probs(j):
                    act.wait_ge(sems["pt_done"], at.up("pt_done"))
                    act.activation(pt_tile[:, j % 2, :, :], aux[2][:, :].rearrange("p (a b) -> p a b", b=P), ACT.Copy).then_inc(sems["pt_ready"], 1)
                    n.up("pt_ready")

                def move_output(j):
                    groups, place, _, rows = items[j]
                    act.wait_ge(sems["o_done"], at.up("o_done"))
                    act.activation(place, aux[3][rows[0]:rows[1], 0:groups * P], ACT.Copy).then_inc(sems["o_hi" if high else "o_ready"], 1)
                    n.up("o_hi" if high else "o_ready")
                for j in range(len(items)):
                    soft(j)
                    for u in fill[j]:
                        run(u)
                    if j >= 1:
                        move_probs(j - 1)
                    if j >= 2:
                        move_output(j - 2)
                move_probs(len(items) - 1)
                move_output(len(items) - 2)
                move_output(len(items) - 1)
                if high:
                    n.up("o_ready", len(items))

            def ada(l, group):
                b = at.n.of.get("ada", 0) % 2
                at.n.up("ada")
                o = arrived(ADA_CHUNKS * KC)
                moved(act.activation(mod_rows[:, b, :], o[0:4, 0:ADA_COLS], ACT.Copy))
                o = arrived(0)
                moved(act.activation(mod[:, l, ADA_CHUNKS * group:ADA_CHUNKS * (group + 1), :], o[:, 0:2 * ADA_CHUNKS].rearrange("p (c s) -> p c s", s=2), ACT.Copy))

            def unit(l, u):
                kind, c = u
                if kind == "kg":
                    moved(act.activation(KG[:, c, :], arrived()[:, 0:S], ACT.Copy))
                elif kind == "qg":
                    moved(act.activation(QG[:, c, :], arrived()[:, 0:S], ACT.Copy, scale=float(GDK) ** -0.5))
                elif kind == "glr":
                    moved(act.activation(glr[0:GLR, :], arrived(0)[0:GLR, 0:S], ACT.Copy))
                elif kind == "vg":
                    for tt in range(QT):
                        o = arrived()
                        moved(act.activation(VG[:, tt, 2 * P * c:2 * P * (c + 1)], o[:, 0:2 * P], ACT.Copy))
                elif kind == "cy":
                    o = arrived()
                    buffered(c, "m_ready") if c else n.up("m_ready", KC)
                    moved(act.activation(y_buf[:, c % 2, :], o[:, 0:S], ACT.Copy))
                elif kind == "r":
                    moved(act.activation(rbuf[:, c, :], arrived()[:, 0:S], ACT.Copy))
                else:
                    ada(*c)

            def gla(l, s, full):
                fill = gla_steps(l, s)
                if full:
                    act.wait_ge(sems["s_ready"], at.value("s_ready", n.at("s_ready")))
                for j in range(4):
                    o = arrived(0)
                    for k in range(2):
                        ins = act.activation(Z[:, 2 * j + k, :], o[:, k * S:(k + 1) * S], ACT.Identity,
                                             bias=v1(l, "gla_b_a", 2 * j + k))
                    moved(ins)
                act.wait_ge(sems["lin_evac"], n.at("lin_evac"))
                step(act.activation(B[:, :, :], Z[:, :, :], ACT.Abs))
                step(act.activation(B[:, :, :], B[:, :, :], ACT.Exp, scale=-1.0))
                for d in range(2):
                    act.activation(B[:, d * GH:(d + 1) * GH, :], B[:, d * GH:(d + 1) * GH, :], ACT.Ln, bias=1.0).then_inc(sems["ln_ready"], 1)
                n.up("ln_ready", 2)
                for u in fill[0]:
                    unit(l, u)
                if full:
                    for j in range(STEPS):
                        if j < STEPS - 1:
                            act.wait_ge(sems["diff_ready"], at.up("diff_ready"))
                            act.activation(DL[:, j % 2], DL[:, j % 2], ACT.Exp, scale=1.0 / TAU).then_inc(sems["lev_exp"], 1)
                            n.up("lev_exp")
                        for u in fill[j + 1]:
                            unit(l, u)
                act.wait_ge(sems["hat_diff"], at.up("hat_diff"))
                src = DL if s == CTX else B[:, :, :].rearrange("p (d h) t -> p d h t", d=2)
                act.activation(DL[:, :, :, :], src[:, :, :, :], ACT.Exp, scale=1.0 / TAU).then_inc(sems["hat_exp"], 1)
                n.up("hat_exp")
                if s == CTX:
                    for d in range(2):
                        for kt in range(QT):
                            o = arrived(0)
                            moved(act.activation(KT[:, d, kt, :, :], o[:, :].rearrange("p (h k) -> p h k", h=GH), ACT.Copy))
                    for j in range(4):
                        o = arrived(0)
                        d, h = divmod(2 * j, GH)
                        moved(act.activation(state[:, d, h:h + 2, :], o[:, :].rearrange("p (h e) -> p h e", h=2), ACT.Copy))
                if full:
                    act.wait_ge(sems["m_ready"], at.value("m_ready", n.at("m_ready")))
                    for h in range(GH):
                        o = arrived(0)
                        moved(act.activation(Q[:, 2 * h:2 * h + 2, :], o[:, :].rearrange("p (c t) -> p c t", c=2), ACT.Copy))

            act.wait_ge(sems["c_landed"], 16)
            step(act.activation(cvec[:, :, :], cvec[:, :, :], ACT.Silu))
            act.activation(c_hl[:, :, 0:2], cvec[:, :, :], ACT.Copy).then_inc(sems["c_ready"], 1)
            n.up("c_ready")
            split_to(SLOTS)

            def first_modulation():
                for g in range(ADA_FIRST):
                    ada(0, g)
                act.wait_ge(sems["params"], PARAMS)
                act.activation(wglr_hi[:, :], wglr[:, :], ACT.Copy).then_inc(sems["glr_split"], 1)
            for l in range(DEPTH):
                for s in (CTX, LAT):
                    full = l == 0 or s == LAT
                    x = X[:, :, s * S:(s + 1) * S]
                    modulated(l, s, 0, first_modulation if l == 0 and s == CTX else None)
                    if full:
                        n.up("y_ready", KC)
                        for c in range(KC):
                            o = arrived()
                            moved(act.activation(YP[:, c, PAD:PAD + S], o[:, 0:S], ACT.Copy))
                            o = arrived()
                            buffered(c, "y_ready")
                            moved(act.activation(gate_buf[:, c % 2, :], o[:, 0:S], ACT.Sigmoid))
                    heads = [K[:, c, s * S:(s + 1) * S] for c in range(KVH)] + [Q[:, c, :] for c in range(HEADS) if full]
                    for c, t in enumerate(heads):
                        moved(act.activation(t, arrived()[:, 0:S], ACT.Copy))
                        act.wait_ge(sems["lin_evac"], at.now("lin_evac"))
                        ins = act.activation(hsq[:, c, :], t, ACT.Square)
                    ins.then_inc(sems["sq_ready"], 1)
                    n.up("sq_ready")
                    for tt in range(QT):
                        o = arrived()
                        moved(act.activation(V[:, s * QT + tt, :], o[:, 0:KVH * DH], ACT.Copy))
                    if not full:
                        unit(l, ("glr", 0))
                    root(aux[0], ROWS)
                    for c in range(GH if full else 2):
                        unit(l, ("kg", c))
                    if full:
                        if s == CTX:
                            items = [(QT, s_hi[:, h, :], None, (0, P)) for h in range(HEADS)]
                        else:
                            items = [(1, s_hi[:, h, qt * P:(qt + 1) * P], None, (0, P)) for h in range(HEADS) for qt in range(QT)]
                        attention(items, float(DH) ** -0.5, probs, probsT, True, spread(attention_fill(l, s), len(items)),
                                  lambda u: unit(l, u))
                        n.up("m_ready", KC)
                        act.wait_ge(sems["y_ready"], n.at("y_ready"))
                        for c in range(KC):
                            o = arrived()
                            buffered(c, "m_ready")
                            moved(act.activation(gate_buf[:, c % 2, :], o[:, 0:S], ACT.Sigmoid))
                            o = arrived()
                            moved(act.activation(y_buf[:, c % 2, :], o[:, 0:S], ACT.Copy))
                            if c < 2:
                                squares(CV, osq, "xc_ready", range(4 * c, 4 * c + 4, 2))
                            if c == 3:
                                root(aux[1])
                        for c in range(KC):
                            act.wait_ge(sems["t_ready"], at.up("t_ready"))
                            act.activation(CV[:, c, :], CV[:, c, :], ACT.Silu, bias=v1(l, "conv_ln_b", c)).then_inc(sems["act_step"], 1)
                            n.up("act_step")
                        cv0 = n.at("act_step") - KC
                        for c in range(KC):
                            moved(act.activation(Q[:, c, :], arrived()[:, 0:S], ACT.Sigmoid))
                            act.wait_ge(sems["act_step"], cv0 + c + 1)
                            act.activation(s_hi[:, c, :], CV[:, c, :], ACT.Copy).then_inc(sems["cv32_ready"], 1)
                            n.up("cv32_ready")
                        n.up("s_ready", KC)
                    gla(l, s, full)
                    if not full:
                        continue
                    act.wait_ge(sems["lin_evac"], n.at("lin_evac"))
                    act.activation(osq[:, :, :], Q[:, :, :], ACT.Square).then_inc(sems["sq_ready"], 1)
                    n.up("sq_ready")
                    root(aux[0], ROWS)
                    if s == CTX:
                        for c in range(KC):
                            unit(l, ("r", c))
                    act.wait_ge(sems["lin_evac"], n.at("lin_evac"))
                    act.activation(rbuf[:, :, :], rbuf[:, :, :], ACT.Silu).then_inc(sems["silu_ready"], 1)
                    for c in range(KC):
                        moved(act.activation(gbuf[:, c, :], arrived()[:, 0:S], ACT.Sigmoid))
                    n.up("s_ready", KC)
                    n.up("m_ready", KC)
                    for c in range(KC):
                        o = arrived()
                        buffered(c, "m_ready")
                        moved(act.activation(y_buf[:, c % 2, :], o[:, 0:S], ACT.Copy))
                    act.wait_ge(sems["m_ready"], n.at("m_ready"))
                    residual(lambda c: mod[:, l, 16 + c, s:s + 1])
                    if l == DEPTH - 1:
                        act.wait_ge(sems["r_ready"], n.at("r_ready"))
                        act.dma_start(const2, const2_in).then_inc(sems["b2_landed"], 16)
                        act.dma_start(small2, small2_in).then_inc(sems["b2_landed"], 16)
                    post(l, x, "ln1_b")
                    modulated(l, s, 24)
                    feed_forward(lambda c: mod[:, l, 40 + c, s:s + 1])
                    post(l, x, "ln2_b")

            x = X[:, :, S:2 * S]

            def rms():
                squares(x, M)
                root(aux[1])

            act.wait_ge(sems["b2_landed"], 32)
            act.wait_ge(sems["x_ready"], n.at("x_ready"))
            for l in range(DEPTH):
                rms()
                high_parts()

                def move(dst, rows=(0, P), scale=1.0, tiles=KC):
                    o = arrived(tiles)
                    src = o[rows[0]:rows[1], 0:dst.free_size()]
                    if len(dst.shape) == 3:
                        src = src.rearrange("p (a b) -> p a b", a=dst.shape[1])
                    moved(act.activation(dst, src, ACT.Copy, scale=scale))
                for c in range(2):
                    move(w2["cq"][:, c, :])
                move(w2["ckv"][:, 0, :])
                move(w2["kr"][NOPE:QK, 0, :], (NOPE, QK))
                act.wait_ge(sems["lin_evac"], n.at("lin_evac"))
                act.wait_ge(sems["r_ready"], n.at("r_ready"))
                act.activation(gate_buf[:, :, :], w2["cq"][:, :, :], ACT.Square).then_inc(sems["sq_ready"], 1)
                n.up("sq_ready")
                act.activation(y_buf[:, 0, :], w2["ckv"][:, 0, :], ACT.Square).then_inc(sems["sq_ready"], 1)
                n.up("sq_ready")
                move(w2["vf"])
                for name in ("uc", "gc", "gb"):
                    for c in range(2):
                        move(w2[name][:, c, :])
                    if name == "uc":
                        move(w2["up"][:, 0, 16:])
                        root(aux[0], slot=0)
                        root(aux[1], slot=1)
                        move(w2["up"][:, 1, 16:])
                for c in range(2):
                    move(w2["qs"][:, c, :])
                move(w2["ks"][:, 0, :])
                for h in range(MH):
                    move(w2["qh"][0:QK, h, :], (0, QK), tiles=0)
                for h in range(MH):
                    move(w2["kh"][0:NOPE, h, :], (0, NOPE), tiles=0)
                move(w2["vm"][:, :, :], tiles=0)
                move(w2["vs"][:, :, :], tiles=0)
                for c in range(2):
                    move(w2["mx"][:, 4 + c, :], scale=v2(l, "pool_scale", c), tiles=0)
                items = []
                for h in range(MH):
                    r = 64 * (h % 2)
                    items.append((QT, w2["mx"][r:r + 64, h // 2, :], None, (r, r + 64)))
                for h in range(SH):
                    r = 64 * (h % 2)
                    items.append((QT, w2["mx"][r:r + 64, 6 + h // 2, :], v2(l, "sinks", h), (r, r + 64)))
                attention(items, None, w2["probs"], w2["probsT"], False, [[]] * len(items), None)
                act.wait_ge(sems["yb_ready"], l + 1)
                act.wait_ge(sems["o_ready"], n.at("o_ready"))
                squares(w2["mx"], M)
                root(aux[0], ROWS)
                n.up("s_ready", KC)
                residual(None)
                act.wait_ge(sems["r_ready"], n.at("r_ready"))
                rms()
                high_parts()
                feed_forward(None)
                act.wait_ge(sems["r_ready"], n.at("r_ready"))
            rms()
            at.tile_done = LOADS * TILES
            split_to(LOADS)

        @block.vector
        def _(dve):
            at = Place()
            n = at.n

            def step(ins):
                ins.then_inc(sems["dve_step"], 1)
                dve.wait_ge(sems["dve_step"], at.up("dve_step"))

            def over(t, k):
                return t.unsqueeze(1).broadcast_to([t.shape[0], k, t.shape[1]])

            def inverse(b, rows=P, slot=0, name="dve_step"):
                dve.wait_ge(sems["std_ready"], at.up("std_ready"))
                r, t, v = rstd[0:rows, :], tmp[0:rows, :], b[0:rows, 0:S]
                step(dve.reciprocal(r, std[0:rows, slot, :]))
                step(dve.scalar_tensor_tensor(t, v, EPS, r, ALU.add, ALU.mult))
                step(dve.scalar_tensor_tensor(t, t, -0.5, r, ALU.mult, ALU.mult))
                dve.scalar_tensor_tensor(r, t, 1.5, r, ALU.add, ALU.mult).then_inc(sems[name], 1)
                n.up(name)
                dve.wait_ge(sems[name], at.now(name))

            def centre(src, dst):
                dve.wait_ge(sems["mean_done"], at.up("mean_done"))
                for p in range(0, KC, 2):
                    dve.tensor_tensor(dst[:, p:p + 2, :], src[:, p:p + 2, :], over(aux[0][:, 0:S], 2), ALU.subtract).then_inc(sems["xc_ready"], 1)
                    n.up("xc_ready")

            def scale_chunk(src, g, c):
                dve.scalar_tensor_tensor(W[:, c, :], src[:, c, :], g(c), rstd[:, :], ALU.mult, ALU.mult).then_inc(sems["t_ready"], 1)
                n.up("t_ready")

            def low_part(c, shift):
                dve.wait_ge(sems["hi_part"], at.up("hi_part"))
                hi = h_hi[:, c, :].bitcast(F32)
                if shift:
                    dve.scalar_tensor_tensor(h_lo[:, c, :], W[:, c, :], shift(c), hi, ALU.add, ALU.subtract).then_inc(sems["h_ready"], 1)
                    n.up("h_ready")
                else:
                    dve.tensor_tensor(h_lo[:, c, :], W[:, c, :], hi, ALU.subtract).then_inc(sems["h_ready"], 1)
                    n.up("h_ready")

            def to_h(src, g, shift):
                for c in range(KC):
                    scale_chunk(src, g, c)
                    if c >= 1:
                        low_part(c - 1, shift)
                low_part(KC - 1, shift)

            def modulated(l, x, s, shift, scale, before=None):
                centre(x, W)
                inverse(aux[1])
                if before:
                    before()
                dve.wait_ge(sems["xc_ready"], at.now("xc_ready"))
                to_h(W, lambda c: mod[:, l, scale + c, s:s + 1], lambda c: mod[:, l, shift + c, s:s + 1])

            def post(l, x, g):
                centre(x, W)
                inverse(aux[1])
                dve.wait_ge(sems["xc_ready"], at.now("xc_ready"))
                for c in range(KC):
                    scale_chunk(W, lambda c: v1(l, g, c), c)
                dve.wait_ge(sems["x_ready"], at.up("x_ready", KC))

            def both_parts(hi, lo, y, name):
                step(dve.tensor_copy(hi, y))
                dve.tensor_tensor(lo, y, hi.bitcast(F32), ALU.subtract).then_inc(sems[name], 1)
                n.up(name)

            def merge_chunk(c, gate, first=False):
                if first:
                    dve.tensor_tensor(M[:, c, :], gate, y_buf[:, c % 2, :], ALU.mult).then_inc(sems["m_ready"], 1)
                    n.up("m_ready")
                else:
                    step(dve.tensor_tensor(y_buf[:, c % 2, :], gate, y_buf[:, c % 2, :], ALU.mult))
                    dve.tensor_tensor(M[:, c, :], M[:, c, :], y_buf[:, c % 2, :], ALU.add).then_inc(sems["m_ready"], 1)
                    n.up("m_ready")

            def residual(x, alpha):
                for c in range(KC):
                    dve.wait_ge(sems["lin_evac"], at.up("lin_evac"))
                    dve.scalar_tensor_tensor(x[:, c, :], x[:, c, :], alpha, gate_buf[:, c % 2, :], ALU.mult, ALU.add).then_inc(sems["r_ready"], 1)
                    n.up("r_ready")

            def feed_forward(x, scaled):
                a, _ = CONST1["alpha"]
                with dve.Fori(0, 2) as i:
                    at.enter(i)
                    for c in range(HALF):
                        dve.wait_ge(sems["lin_evac"], at.up("lin_evac", 2))
                        y = y_buf[:, c % 2, :]
                        step(dve.tensor_tensor(y, gate_buf[:, c % 2, :], y, ALU.mult))
                        both_parts(s_hi[:, c, :], s_lo[:, c, :], y, "s_ready")
                    dve.wait_ge(sems["r_ready"], at.now("r_ready"))
                    residual(x, const1[:, bass.ds(i + a, 1)] if scaled else 1.0)
                    at.leave()
                dve.wait_ge(sems["r_ready"], at.now("r_ready"))

            PARTS = 6
            CONV_PIECES, PIECE = KC // 2 * PARTS, (TAPS - 1) // PARTS

            def convolve(l, piece, y0):
                q, part = divmod(piece, PARTS)
                w_at = VEC1["conv_w"][0]
                if part == 0:
                    dve.wait_ge(sems["y_ready"], y0 + 2 * q + 2)
                    for c in (2 * q, 2 * q + 1):
                        dve.tensor_scalar(CV[:, c, :], YP[:, c, 0:S], v1(l, "conv_w", c * TAPS), v1(l, "conv_b", c),
                                          ALU.mult, ALU.add).then_inc(sems["dve_step"], 1)
                        n.up("dve_step")
                base = n.at("dve_step")
                tap = 1 + part * PIECE
                with dve.Fori(0, PIECE) as t:
                    for k in range(2):
                        c = 2 * q + k
                        dve.wait_ge(sems["dve_step"], t * 2 + (base + k - 1))
                        dve.scalar_tensor_tensor(CV[:, c, :], YP[:, c, bass.ds(t + tap, S)],
                                                 vec1[:, l, bass.ds(t + (w_at + c * TAPS + tap), 1)], CV[:, c, :],
                                                 ALU.mult, ALU.add).then_inc(sems["dve_step"], 1)
                n.up("dve_step", 2 * PIECE)

            def attention(items, scale, p_tile, high, fill, run):
                def top(j):
                    groups, bias, sink, qk_scale, _ = items[j]
                    dve.wait_ge(sems["s_done"], at.up("s_done"))
                    st = small[:, j % 2, :]
                    src = aux[j % 2][:, :]
                    if scale is None:
                        src = w2["scores"][:, j % 2, :]
                        step(dve.scalar_tensor_tensor(src, aux[j % 2][:, :], qk_scale, bias, ALU.mult, ALU.add))
                    step(dve.reduce_max(st[:, 0:groups], src.rearrange("p (g k) -> p g k", g=groups), AXX))
                    if sink is not None:
                        dve.tensor_scalar(st[:, 2:2 + groups], st[:, 0:groups], sink, -1.0, ALU.max, ALU.mult).then_inc(sems["nb_ready"], 1)
                        n.up("nb_ready")
                    else:
                        dve.tensor_scalar(st[:, 2:2 + groups], st[:, 0:groups], -1.0 if scale is None else -scale, None, ALU.mult).then_inc(sems["nb_ready"], 1)
                        n.up("nb_ready")

                def normalise(j):
                    groups, _, sink, _, _ = items[j]
                    dve.wait_ge(sems["p_ready"], at.up("p_ready"))
                    w = 2 * S // groups
                    st = small[:, j % 2, :]
                    if sink is not None:
                        step(dve.tensor_tensor(st[:, 4:4 + groups], st[:, 4:4 + groups], st[:, 8:8 + groups], ALU.add))
                    step(dve.reciprocal(st[:, 6:6 + groups], st[:, 4:4 + groups]))
                    for g in range(groups):
                        p = p_tile[:, j % 2, g * w:(g + 1) * w]
                        ins = dve.tensor_scalar(p, p, st[:, 6 + g:7 + g], None, ALU.mult)
                    ins.then_inc(sems["pn_ready"], 1)
                    n.up("pn_ready")

                def low(j):
                    groups, _, _, _, (hi, lo) = items[j]
                    dve.wait_ge(sems["o_hi"], at.up("o_hi"))
                    dve.tensor_tensor(lo, aux[3][:, 0:groups * P], hi.bitcast(F32), ALU.subtract).then_inc(sems["o_ready"], 1)
                    n.up("o_ready")
                for j in range(len(items)):
                    top(j)
                    if j >= 1:
                        normalise(j - 1)
                    for u in fill[j]:
                        run(u)
                    if high and j >= 2:
                        low(j - 2)
                normalise(len(items) - 1)
                if high:
                    low(len(items) - 2)
                    low(len(items) - 1)

            pending = []

            def modulation():
                for l, g, chunk in pending:
                    dve.wait_ge(sems["lin_evac"], chunk)
                    c = ADA_CHUNKS * g
                    m = mod[:, l, c:c + ADA_CHUNKS, :]
                    b = vec1[:, l, VEC1["b_ada"][0] + c:VEC1["b_ada"][0] + c + ADA_CHUNKS].unsqueeze(2).broadcast_to([P, ADA_CHUNKS, 2])
                    one = 1.0 if c // KC in (1, 4) else 0.0
                    step(dve.scalar_tensor_tensor(m, m, one, b, ALU.add, ALU.add))
                pending.clear()

            def unit(l, u, y0=None):
                kind, c = u
                if kind == "conv":
                    convolve(l, c, y0)
                elif kind == "cy":
                    dve.wait_ge(sems["lin_evac"], at.up("lin_evac"))
                    merge_chunk(c, Q[:, c, :])
                else:
                    n.up("lin_evac", 2 if kind in ("vg", "ada") else 1)
                    if kind == "ada":
                        pending.append((c[0], c[1], n.at("lin_evac")))

            def gla(l, s, full):
                fill = gla_steps(l, s)
                dve.wait_ge(sems["lin_evac"], at.up("lin_evac", 4))
                for d in range(2):
                    dve.wait_ge(sems["ln_ready"], at.up("ln_ready"))
                    zd = Z[:, d * GH:(d + 1) * GH, :]
                    step(dve.scalar_tensor_tensor(zd, zd, 0.0, B[:, d * GH:(d + 1) * GH, :], ALU.min, ALU.subtract))
                    for h in range(GH):
                        src, dst = Z[:, d * GH + h, :], B[:, d * GH + h, :]
                        if d == 1:
                            src, dst = src[:, ::-1], dst[:, ::-1]
                        ins = dve.tensor_tensor_scan(dst, src, src, 0.0, ALU.add, ALU.bypass)
                step(ins)
                if full:
                    g0 = n.at("gram_done")

                    def halves(t, half):
                        v = t.rearrange("p h (b two e) -> p (h b) two e", two=2, e=half)
                        return v[:, :, 0, :], v[:, :, 1, :]

                    def differences(j):
                        half, d = LEVELS[j // 2], j % 2
                        if j >= 2:
                            dve.wait_ge(sems["gram_done"], g0 + j - 1)
                        left, right = halves(B[:, d * GH:(d + 1) * GH, :], half)
                        dl, dr = halves(DL[:, j % 2], half)
                        blocks = left.shape[1]
                        if d == 0:
                            mid = left[:, :, half - 1:half].broadcast_to([P, blocks, half])
                            dve.tensor_tensor(dr, right, mid, ALU.subtract)
                            dve.tensor_tensor(dl, mid, left, ALU.subtract).then_inc(sems["diff_ready"], 1)
                            n.up("diff_ready")
                        else:
                            mid = right[:, :, 0:1].broadcast_to([P, blocks, half])
                            dve.tensor_tensor(dl, left, mid, ALU.subtract)
                            dve.tensor_tensor(dr, mid, right, ALU.subtract).then_inc(sems["diff_ready"], 1)
                            n.up("diff_ready")

                    def decay(j):
                        half, d = LEVELS[j // 2], j % 2
                        dve.wait_ge(sems["lev_exp"], at.up("lev_exp"))
                        dl, dr = halves(DL[:, j % 2], half)
                        ql, qr = halves(QG, half)
                        kl, kr = halves(KG, half)
                        dve.tensor_tensor(dl, dl, kl if d == 0 else ql, ALU.mult)
                        dve.tensor_tensor(dr, dr, qr if d == 0 else kr, ALU.mult).then_inc(sems["lev_ready"], 1)
                        n.up("lev_ready")

                    def place(j):
                        pair = [aux[2 * (j % 2)], aux[2 * (j % 2) + 1]]
                        dve.wait_ge(sems["gram_done"], g0 + j + 1)
                        if j < 2:
                            kt, qs = (0, P) if j == 0 else (1, 0)
                            dve.tensor_copy(A[:, :, kt, qs:qs + P], pair[0][:, :].rearrange("p (h q) -> p h q", h=GH)).then_inc(sems["a_copied"], 1)
                            n.up("a_copied")
                            return
                        dve.wait_ge(sems["a_copied"], at.now("a_copied"))
                        for kt in range(QT):
                            ins = dve.copy_predicated(A[:, :, kt, kt * P:(kt + 1) * P], over(masks[:, j - 2, :], GH),
                                                      pair[kt][:, :].rearrange("p (h q) -> p h q", h=GH))
                        ins.then_inc(sems["a_copied"], 1)
                        n.up("a_copied")
                    for j in range(STEPS):
                        if j >= 1:
                            decay(j - 1)
                        if j < STEPS - 1:
                            differences(j)
                        if j >= 2:
                            place(j - 2)
                        for u in fill[j]:
                            unit(l, u)
                    for u in fill[STEPS]:
                        unit(l, u)
                    place(STEPS - 2)
                    place(STEPS - 1)
                    n.up("gram_done", STEPS)
                else:
                    for u in fill[0]:
                        unit(l, u)
                if s == CTX:
                    for d in range(2):
                        a = S - 1 if d == 0 else 0
                        b = B[:, d * GH:(d + 1) * GH, :]
                        ins = dve.tensor_tensor(DL[:, d], b[:, :, a:a + 1].broadcast_to([P, GH, S]), b, ALU.subtract)
                    ins.then_inc(sems["hat_diff"], 1)
                    n.up("hat_diff")
                else:
                    dve.tensor_copy(small[:, 0, 15:16], B[:, 0, 0:1]).then_inc(sems["hat_diff"], 1)
                    n.up("hat_diff")
                dve.wait_ge(sems["hat_exp"], at.up("hat_exp"))
                t = KG if s == CTX else QG
                for d in range(2):
                    ins = dve.tensor_tensor(DL[:, d], DL[:, d], t, ALU.mult)
                ins.then_inc(sems["hat_ready"], 1)
                n.up("hat_ready")
                modulation()
                n.up("lin_evac", (8 if s == CTX else 0) + (GH if full else 0))

            dve.wait_ge(sems["c_ready"], at.up("c_ready"))
            dve.tensor_tensor(c_hl[:, :, 2:4], cvec[:, :, :], c_hl[:, :, 0:2].bitcast(F32), ALU.subtract).then_inc(sems["c_ready"], 1)
            n.up("c_ready")

            def first_modulation():
                dve.wait_ge(sems["params"], PARAMS)
                step(dve.tensor_copy(masks[:, :, :], view(arena2, pt_at, N_MASK, P)))
                for g in range(ADA_FIRST):
                    unit(0, ("ada", (0, g)))
                modulation()
                dve.wait_ge(sems["glr_split"], at.up("glr_split"))
                dve.tensor_tensor(wglr_lo[:, :], wglr[:, :], wglr_hi[:, :].bitcast(F32), ALU.subtract).then_inc(sems["glr_split"], 1)
            for l in range(DEPTH):
                for s in (CTX, LAT):
                    full = l == 0 or s == LAT
                    x = X[:, :, s * S:(s + 1) * S]
                    modulated(l, x, s, 0, 8, first_modulation if l == 0 and s == CTX else None)
                    if full:
                        dve.memset(YP[:, :, 0:PAD], 0.0)
                        step(dve.memset(YP[:, :, PAD + S:2 * PAD + S], 0.0))
                        y0, piece = n.at("y_ready"), 0
                        for c in range(KC):
                            dve.wait_ge(sems["lin_evac"], at.up("lin_evac", 2))
                            y = YP[:, c, PAD:PAD + S]
                            dve.tensor_tensor(y, y, gate_buf[:, c % 2, :], ALU.mult).then_inc(sems["y_ready"], 1)
                            n.up("y_ready")
                            for _ in range(1 + c % 2 if c else 0):
                                convolve(l, piece, y0)
                                piece += 1
                        for _ in range(3):
                            convolve(l, piece, y0)
                            piece += 1
                    n.up("lin_evac", KVH + QT + (HEADS if full else 1))
                    inverse(aux[0], ROWS, name="row_ready")
                    heads = [(K[:, c, s * S:(s + 1) * S], "k_norm") for c in range(KVH)]
                    heads += [(Q[:, c, :], "q_norm") for c in range(HEADS) if full]
                    base = n.at("qk_normed")

                    def normed(j):
                        t, name = heads[j]
                        dve.wait_ge(sems["spread_done"], at.up("spread_done"))
                        dve.scalar_tensor_tensor(t, t, v1(l, name), aux[1 + j % 2][:, 0:S], ALU.mult, ALU.mult).then_inc(sems["qk_normed"], 1)
                        n.up("qk_normed")

                    def rotated(j):
                        t, _ = heads[j]
                        dve.wait_ge(sems["rot_done"], at.up("rot_done"))
                        dve.wait_ge(sems["qk_normed"], base + j + 1)
                        step(dve.tensor_tensor(t, t, c1("cos"), ALU.mult))
                        step(dve.tensor_tensor(tmp[:, :], aux[3 * (j % 2)][:, 0:S], c1("sin"), ALU.mult))
                        dve.tensor_tensor(t, t, tmp[:, :], ALU.add).then_inc(sems["qk_ready"], 1)
                        n.up("qk_ready")
                        dve.wait_ge(sems["qk_ready"], at.now("qk_ready"))
                    for j in range(len(heads)):
                        normed(j)
                        if s == LAT and j >= 1:
                            rotated(j - 1)
                    if s == LAT:
                        rotated(len(heads) - 1)
                    n.up("lin_evac", GH if full else 2)
                    if full:
                        if s == CTX:
                            items = [(QT, None, None, None, (s_hi[:, h, :], s_lo[:, h, :])) for h in range(HEADS)]
                        else:
                            items = [(1, None, None, None, (s_hi[:, h, qt * P:(qt + 1) * P], s_lo[:, h, qt * P:(qt + 1) * P]))
                                     for h in range(HEADS) for qt in range(QT)]
                        fill = spread(attention_fill(l, s), len(items))
                        pieces = spread([("conv", p) for p in range(piece, CONV_PIECES)], len(items))
                        attention(items, float(DH) ** -0.5, probs, True, [f + p for f, p in zip(fill, pieces)], lambda u: unit(l, u, y0))
                        dve.wait_ge(sems["dve_step"], at.now("dve_step"))
                        dve.tensor_copy(small[:, 0, 15:16], CV[:, 0, 0:1]).then_inc(sems["conv_done"], 1)
                        modulation()
                        centre(CV, CV)
                        for c in range(KC):
                            dve.wait_ge(sems["lin_evac"], at.up("lin_evac", 2))
                            merge_chunk(c, gate_buf[:, c % 2, :], first=True)
                            if c == 3:
                                inverse(aux[1])
                                dve.wait_ge(sems["xc_ready"], at.now("xc_ready"))
                                for k in range(KC):
                                    scale_chunk(CV, lambda k: v1(l, "conv_ln_g", k), k)
                        n.up("lin_evac", KC)
                        for c in range(KC):
                            dve.wait_ge(sems["cv32_ready"], at.up("cv32_ready"))
                            dve.tensor_tensor(s_lo[:, c, :], CV[:, c, :], s_hi[:, c, :].bitcast(F32), ALU.subtract).then_inc(sems["s_ready"], 1)
                            n.up("s_ready")
                    gla(l, s, full)
                    if not full:
                        continue
                    inverse(aux[0], ROWS, name="row_ready")
                    dve.wait_ge(sems["spread_done"], at.up("spread_done", 2))
                    if s == CTX:
                        n.up("lin_evac", KC)
                    for c in range(KC):
                        h, y = c // 2, Q[:, c, :]
                        if c == 0:
                            silu_at = at.up("silu_ready")
                        step(dve.scalar_tensor_tensor(y, y, v1(l, "gla_norm", c % 2), aux[1 + h // 2][:, h % 2 * S:h % 2 * S + S],
                                                      ALU.mult, ALU.mult))
                        if c == 0:
                            dve.wait_ge(sems["silu_ready"], silu_at)
                        step(dve.tensor_tensor(y, y, rbuf[:, c, :], ALU.mult))
                        both_parts(s_hi[:, c, :], s_lo[:, c, :], y, "s_ready")
                    n.up("lin_evac", KC)
                    for c in range(KC):
                        dve.wait_ge(sems["lin_evac"], at.up("lin_evac"))
                        merge_chunk(c, gbuf[:, c, :])
                        dve.wait_ge(sems["m_ready"], at.now("m_ready"))
                        both_parts(h_hi[:, c, :], h_lo[:, c, :], M[:, c, :], "h_ready")
                    residual(x, ALPHA)
                    post(l, x, "ln1_g")
                    modulated(l, x, s, 24, 32)
                    feed_forward(x, True)
                    post(l, x, "ln2_g")

            x = X[:, :, S:2 * S]
            dve.wait_ge(sems["b2_landed"], 32)

            def rms(g):
                inverse(aux[1])
                to_h(x, g, None)
            for l in range(DEPTH):
                rms(lambda c: v2(l, "attn_norm", c))
                dve.memset(w2["zp"][:, :, 0:2], 0.0)
                step(dve.memset(w2["up"][:, :, 0:16], 0.0))
                inverse(aux[0], slot=0)
                for c in range(2):
                    ins = dve.scalar_tensor_tensor(w2["cq"][:, c, :], w2["cq"][:, c, :], v2(l, "q_norm", c), rstd[:, :], ALU.mult, ALU.mult)
                ins.then_inc(sems["qk_normed"], 1)
                n.up("qk_normed")
                dve.wait_ge(sems["qk_normed"], at.now("qk_normed"))
                inverse(aux[1], slot=1)
                dve.scalar_tensor_tensor(w2["ckv"][:, 0, :], w2["ckv"][:, 0, :], v2(l, "kv_norm"), rstd[:, :], ALU.mult, ALU.mult).then_inc(sems["qk_normed"], 1)
                n.up("qk_normed")
                dve.wait_ge(sems["lin_evac"], at.up("lin_evac", 9))
                prev, e = w2["up"], 16 + S
                for i, window in enumerate(POOLS):
                    cur = w2[f"p{window}"]
                    lo, sh = window - 1, window // 2
                    step(dve.tensor_tensor(cur[:, :, lo:e], prev[:, :, lo:e], prev[:, :, lo - sh:e - sh], ALU.add))
                    prev = cur
                ic = c2("inv_count").rearrange("p (c t) -> p c t", c=2)
                for i, window in enumerate(POOLS):
                    c, r = i // 2, 64 * (i % 2)
                    ins = dve.tensor_tensor(w2["pooled"][r:r + 64, c, :], w2[f"p{window}"][r:r + 64, c, 16:], ic[r:r + 64, c, :], ALU.mult)
                step(ins)
                dve.tensor_tensor(w2["pooled"][:, :, :], w2["pooled"][:, :, :], w2["up"][:, :, 16:], ALU.subtract).then_inc(sems["pooled_ready"], 1)
                n.up("pooled_ready")
                dve.wait_ge(sems["lin_evac"], at.up("lin_evac", 4))
                step(dve.tensor_tensor(w2["zp"][:, :, 2:], w2["gc"][:, :, :], w2["uc"][:, :, :], ALU.mult))
                for c in range(2):
                    y = w2["uc"][:, c, :]
                    step(dve.tensor_scalar(y, w2["zp"][:, c, 0:S], v2(l, "conv_w", c), None, ALU.mult))
                    for t in (1, 2):
                        step(dve.scalar_tensor_tensor(y, w2["zp"][:, c, t:t + S], v2(l, "conv_w", 2 * t + c), y, ALU.mult, ALU.add))
                dve.tensor_tensor(w2["mx"][:, 2:4, :], w2["uc"][:, :, :], w2["gb"][:, :, :], ALU.mult).then_inc(sems["yb_ready"], 1)
                n.up("yb_ready")
                cos, sin = c2("cos"), c2("sin")
                dve.wait_ge(sems["lin_evac"], at.up("lin_evac", 3 + 2 * MH + 2))
                dve.wait_ge(sems["rot_done"], at.up("rot_done"))
                kr = w2["kr"][NOPE:QK, 0, :]
                step(dve.tensor_tensor(kr, kr, cos[NOPE:QK, :], ALU.mult))
                step(dve.tensor_tensor(tmp[NOPE:QK, :], aux[2][NOPE:QK, 0:S], sin[NOPE:QK, :], ALU.mult))
                dve.tensor_tensor(w2["kh"][NOPE:QK, :, :], over(kr, MH), over(tmp[NOPE:QK, :], MH), ALU.add).then_inc(sems["qk_ready"], 1)
                n.up("qk_ready")
                dve.wait_ge(sems["qk_ready"], at.now("qk_ready"))
                for h in range(MH):
                    dve.wait_ge(sems["rot_done"], at.up("rot_done"))
                    q, t = w2["qh"][0:QK, h, :], tmp[0:QK, :]
                    step(dve.tensor_tensor(q, q, cos[0:QK, :], ALU.mult))
                    step(dve.tensor_tensor(t, aux[2 + (h + 1) % 2][0:QK, 0:S], sin[0:QK, :], ALU.mult))
                    dve.tensor_tensor(q, q, t, ALU.add).then_inc(sems["qk_ready"], 1)
                    n.up("qk_ready")
                    dve.wait_ge(sems["qk_ready"], at.now("qk_ready"))
                n.up("lin_evac", 2)
                items = []
                causal = c2("causal")
                window = c2("window").rearrange("p (h k) -> p h k", h=SH)
                for h in range(MH):
                    items.append((QT, causal, None, float(QK) ** -0.5, None))
                for h in range(SH):
                    items.append((QT, window[:, h, :], v2(l, "sinks", h), float(SHD) ** -0.5, None))
                attention(items, None, w2["probs"], False, [[]] * len(items), None)
                dve.wait_ge(sems["yb_ready"], at.now("yb_ready"))
                inverse(aux[0], ROWS, name="row_ready")
                dve.wait_ge(sems["spread_done"], at.up("spread_done", 2))
                for c in range(KC):
                    g, y = c // 2, w2["mx"][:, c, :]
                    step(dve.scalar_tensor_tensor(y, y, v2(l, "mix_norm", c), aux[1 + g // 2][:, g % 2 * S:g % 2 * S + S], ALU.mult, ALU.mult))
                    both_parts(s_hi[:, c, :], s_lo[:, c, :], y, "s_ready")
                residual(x, 1.0)
                dve.wait_ge(sems["r_ready"], at.now("r_ready"))
                rms(lambda c: v2(l, "ffn_norm", c))
                feed_forward(x, False)
            inverse(aux[1])
            for c in range(KC):
                g = vec2[:, DEPTH * N_VEC2 + c:DEPTH * N_VEC2 + c + 1]
                ins = dve.scalar_tensor_tensor(W[:, c, :], x[:, c, :], g, rstd[:, :], ALU.mult, ALU.mult)
            ins.then_inc(sems["fin_ready"], 1)
            n.up("fin_ready")


def tiles(w):
    k, m = w.shape
    return w.reshape(k // P, P, m // P, P).transpose(2, 0, 1, 3)


def token_tiles(w):
    k, m = w.shape
    return w.reshape(k // P, P, m // P, P).transpose(0, 2, 1, 3).reshape(-1, P, P)


def paired(a, b):
    return np.stack([tiles(a), tiles(b)], 1)


def wide_tiles(w):
    return [token_tiles(w[:, g * ADA_COLS:(g + 1) * ADA_COLS]) for g in range(ADA_GROUPS)]


def half_tiles(gate, up, down):
    both, parts, cut = paired(gate, up), [], HALF * P
    for i in range(2):
        parts += [both[i * HALF:(i + 1) * HALF], tiles(down[i * cut:(i + 1) * cut])]
    return parts


def first_stack_tiles(layers):
    ada = [wide_tiles(w["w_ada"]) for w in layers]
    parts = ada[0][:ADA_FIRST]
    for l, w in enumerate(layers):
        k, v, kg, vg, _, q, qg, r, ca, cg, g_att, g_gla, g_conv = np.split(
            w["w_in"], np.cumsum([256, 256, 512, 1024, 32, 1024, 512, 1024, 1024, 1024, 1024, 1024]), axis=1)
        chunks = {"qg": tiles(qg), "cy": tiles(w["w_conv_o"]), "r": tiles(r), "glr": np.zeros((1, 0, P, P), np.float32),
                  "vg": [token_tiles(vg[:, j * 2 * P:(j + 1) * 2 * P]) for j in range(GH)]}

        def unit(kind, c):
            return ada[c[0]][c[1]] if kind == "ada" else chunks[kind][c]
        for s in (CTX, LAT):
            if l == DEPTH - 1 and s == CTX:
                parts += [tiles(k), token_tiles(v), tiles(kg)] + chunks["vg"]
                continue
            parts += [paired(ca, cg), tiles(k), tiles(q), token_tiles(v), tiles(kg)]
            parts += [unit(*u) for u in attention_fill(l, s)]
            parts += [paired(g_att, w["w_att_o"]), tiles(g_conv)]
            parts += [unit(*u) for step in gla_steps(l, s) for u in step]
            parts += [tiles(r)] * (s == CTX) + [tiles(g_gla), tiles(w["w_gla_o"]), tiles(w["w_out"])]
            parts += half_tiles(w["w_ff_gate"], w["w_ff_up"], w["w_ff_down"])
    return [p.reshape(-1, P, P) for p in parts]


def second_stack_tiles(w):
    cq, ckv, kr, gb, gc, uc, up, qs, ks, vs = np.split(
        w["w_in"], np.cumsum([256, 128, 32, 256, 256, 256, 256, 256, 128]), axis=1)
    kr = np.pad(kr, ((0, 0), (NOPE, P - QK)))
    qs = qs.reshape(D, 2, 2, SHD).transpose(0, 2, 1, 3).reshape(D, SH * SHD)
    gate, upw = np.split(w["w_gate_up"], 2, axis=1)
    parts = [tiles(x) for x in (cq, ckv, kr, vs, uc, up, gc, gb, qs, ks, w["w_o"])] + half_tiles(gate, upw, w["w_down"])
    return [p.reshape(-1, P, P) for p in parts]


def columns(*vectors):
    return np.concatenate([v.reshape(-1, P).T for v in vectors], 1)


def constants():
    eye = np.eye(P, dtype=np.float32)
    c = {"ident": eye}
    for m in (1024, 256, 128):
        c[f"mean{m}"] = np.full((P, P), 1.0 / m, np.float32)
    rot = np.zeros((P, P), np.float32)
    rot[np.arange(1, P, 2), np.arange(0, P, 2)] = -1.0
    rot[np.arange(0, P, 2), np.arange(1, P, 2)] = 1.0
    c["rot"] = rot
    c["head128"] = np.concatenate([np.tile(np.eye(ROWS)[h], (P, 1)) / 128 for h in range(KVH + HEADS)], 1)
    c["head256"] = np.concatenate([np.tile(np.eye(ROWS)[h], (P, 1)) / 256 for h in range(4)], 1)
    c["pair"] = np.zeros((P, 2))
    c["pair"][[0, 2], 0] = c["pair"][[1, 3], 1] = 1.0
    c["alpha"] = np.tile([ALPHA, 1.0], (P, 1))
    t = np.arange(S)
    half = DH // 2
    inv = np.float32(10000.0) ** (-np.arange(0, half, 2, dtype=np.float32) / np.float32(half))
    ang = np.concatenate([(t // 64).astype(np.float32)[:, None] * inv, (t % 64).astype(np.float32)[:, None] * inv], -1)
    ang = np.repeat(ang.T, 2, 0).astype(np.float64)
    c["cos"], c["sin"] = np.cos(ang), np.sin(ang)
    const1 = np.concatenate([c[k] for k in CONST1], 1).astype(np.float32)

    d = {}
    rot = np.zeros((P, P), np.float32)
    h = ROPE // 2
    rot[NOPE + h + np.arange(h), NOPE + np.arange(h)] = -1.0
    rot[NOPE + np.arange(h), NOPE + h + np.arange(h)] = 1.0
    d["rot"] = rot
    inv = np.float32(1.0) / (np.float32(10000.0) ** (np.arange(0, ROPE, 2, dtype=np.float32) / np.float32(ROPE)))
    ang = (t.astype(np.float32)[:, None] * inv).astype(np.float64).T
    cos, sin = np.ones((P, S)), np.zeros((P, S))
    cos[NOPE:QK], sin[NOPE:QK] = np.concatenate([np.cos(ang)] * 2), np.concatenate([np.sin(ang)] * 2)
    d["cos"], d["sin"] = cos, sin
    count = np.ones((P, 2, S))
    for g, wdw in enumerate(POOLS):
        count[64 * (g % 2):64 * (g % 2) + 64, g // 2] = 1.0 / np.minimum(t + 1, wdw)
    d["inv_count"] = count.reshape(P, -1)
    q, k = t[:, None], t[None, :]
    d["causal"] = np.where(k <= q, 0.0, NEG).reshape(QT, P, S).transpose(1, 0, 2).reshape(P, -1)
    dist = q - k
    ok = (dist >= 0) & (dist < WINDOW)
    slopes = [2.0 ** (-8.0 * (i + 1) / SH) for i in range(SH)]
    d["window"] = np.stack([np.where(ok, -s * dist, NEG) for s in slopes]).reshape(SH, QT, P, S).transpose(2, 0, 1, 3).reshape(P, -1)
    const2 = np.concatenate([d[k] for k in CONST2], 1).astype(np.float32)

    j, i = np.arange(P)[:, None], np.arange(P)[None, :]
    masks = []
    for half in LEVELS[1:]:
        same = j // (2 * half) == i // (2 * half)
        left, right = j % (2 * half) < half, i % (2 * half) >= half
        masks += [same & left & right, (same & left & right).T]
    masks.append(i == j)
    return const1, const2, np.stack(masks, 1).astype(np.float32)


def kernel(**x):
    from concourse import bacc
    from concourse.bass_utils import run_bass_kernel_spmd

    x = {k: np.asarray(v) for k, v in x.items()}
    const1, const2, masks = constants()
    layers = [{k: x[k][l] for k in ("w_ada", "w_in", "w_conv_o", "w_att_o", "w_gla_o", "w_out", "w_ff_gate", "w_ff_up", "w_ff_down")}
              for l in range(DEPTH)]
    stream, glrs, vec1, a2 = first_stack_tiles(layers), [], [], np.zeros((GLR, DEPTH, GH * GDK), np.float32)
    for l in range(DEPTH):
        glr = np.zeros((D, GLR), np.float32)
        for d in range(2):
            col = 256 + 256 + 512 + 1024 + d * RANK
            glr[:, 32 * d:32 * d + RANK] = x["w_in"][l][:, col:col + RANK]
            a2[32 * d:32 * d + RANK, l] = x["gla_w_a2"][l, d]
        glrs.append(glr.reshape(KC, P, GLR).transpose(1, 0, 2).reshape(P, -1))
        conv_w = x["conv_w_dw"][l].reshape(TAPS, KC, P).transpose(2, 1, 0).reshape(P, -1)
        vec1.append(np.concatenate([columns(x["b_ada"][l], x["q_norm"][l], x["k_norm"][l], x["gla_b_a"][l], x["gla_norm"][l],
                                            x["conv_b_dw"][l], x["conv_ln_g"][l], x["conv_ln_b"][l], x["ln1_g"][l], x["ln1_b"][l],
                                            x["ln2_g"][l], x["ln2_b"][l]), conv_w], 1))
    vec2, small2 = [], []
    for l in range(DEPTH):
        stream += second_stack_tiles({"w_in": x["w_in_2"][l], "w_o": x["w_o_2"][l], "w_gate_up": x["w_gate_up_2"][l], "w_down": x["w_down_2"][l]})
        vec2 += [columns(x["attn_norm_2"][l], x["mla_q_norm_2"][l], x["mla_kv_norm_2"][l], x["conv_w_2"][l], x["pool_scale_2"][l],
                         x["mix_norm_2"][l], x["ffn_norm_2"][l]), np.broadcast_to(x["swa_sinks_2"][l], (P, SH))]
        pool = np.zeros((P, 2, P), np.float32)
        for g in range(4):
            r = 64 * (g % 2)
            pool[r:r + 64, g // 2, r:r + 64] = x["pool_w_2"][l, g]
        small2.append(np.concatenate([x["w_uq_2"][l].reshape(2, P, -1).transpose(1, 0, 2).reshape(P, -1), x["w_ukv_2"][l],
                                      pool.reshape(P, -1)], 1))
    vec2.append(columns(x["final_norm_2"]))
    stream.append(np.zeros(((LOADS - USED) * TILES, P, P), np.float32))
    both = np.concatenate([x["ctx"][0], x["x"][0]], 0)
    arrays = {
        "stream": np.concatenate(stream).reshape(LOADS, TILES, P, P).transpose(0, 2, 1, 3).reshape(LOADS, P, TILES * P),
        "tokens": both.T.reshape(KC, P, 2 * S).transpose(1, 0, 2),
        "cvec": np.stack([x["c_ctx"], x["c"][0]], 1).reshape(KC, P, 2).transpose(1, 0, 2),
        "vec1": np.stack(vec1, 1),
        "vec2": np.concatenate(vec2, 1),
        "w_glr": np.concatenate(glrs, 1),
        "w_a2": a2,
        "const1": const1, "const2": const2,
        "small2": np.stack(small2, 1),
        "masks": masks,
    }
    arrays = {k: np.ascontiguousarray(a) for k, a in arrays.items()}
    nc = bacc.Bacc("TRN2", target_bir_lowering=False, num_devices=1)
    args = [nc.dram_tensor(f"in_{k}", a.shape, mybir.dt.from_np(a.dtype), kind="ExternalInput").ap() for k, a in arrays.items()]
    out = nc.dram_tensor("out", (P, KC, S), mybir.dt.float32, kind="ExternalOutput").ap()
    program(nc, *args, out)
    r = run_bass_kernel_spmd(nc, [{f"in_{k}": a for k, a in arrays.items()}], core_ids=[0])
    got = np.asarray(r.results[0]["out"])
    return np.ascontiguousarray(got.transpose(2, 1, 0).reshape(1, S, D))
```

```python
import concourse.bass as bass
import numpy as np
from concourse import mybir
from concourse.alu_op_type import AluOpType as ALU
from contextlib import ExitStack

P = 128
D = 1024
KC = D // P
S = 256
QT = S // P
CTX, LAT = 0, 1
DEPTH = 2
EPS = 1e-6
ALPHA = (2.0 * DEPTH) ** 0.25
HEADS, KVH, DH = 8, 2, 128
GH, GDK, GDV, RANK, TAU = 4, 128, 256, 16, 16.0
TAPS = 31
PAD = TAPS // 2
FF = 2816
FC = FF // P
HALF = FC // 2
LEVELS = (128, 64, 32, 16, 8, 4, 2, 1)
MH, NOPE, ROPE, MV = 4, 64, 32, 64
QK = NOPE + ROPE
SH, SHD = 4, 64
WINDOW = 128
POOLS = (2, 4, 8, 16)
NEG = -1e30
PER_HALF = {"lin_done": 2 * HALF + KC, "lin_evac": 2 * HALF + KC, "lo_ready": 3 * HALF, "hi_ready": 3 * HALF,
            "w_used": 3 * HALF, "s_ready": HALF, "r_ready": KC, "dve_step": 2 * HALF, "sum_ready": 1}
TILES = 8
SLOTS = 3
ADA_COLS = 256
ADA_CHUNKS = ADA_COLS // P
ADA_GROUPS = 6 * D // ADA_COLS
ADA_LOADS = KC * ADA_CHUNKS // TILES
ADA_FIRST = 2 * D // ADA_COLS
PASS_LOADS = 16 + 2 + 8 + 2 + 8 + 4 + 4 + 3 * 16 + 8 + 8 + 3 * FC
USED = DEPTH * ADA_GROUPS * ADA_LOADS + 3 * PASS_LOADS + (2 + 2 + 8 + 4) + DEPTH * (16 + 8 + 3 * FC)
LOADS = -(-(USED + SLOTS) // SLOTS) * SLOTS
VEC1 = {}
for _name, _n in (("b_ada", 48), ("q_norm", 1), ("k_norm", 1), ("gla_b_a", 8), ("gla_norm", 2), ("conv_b", 8),
                  ("conv_ln_g", 8), ("conv_ln_b", 8), ("ln1_g", 8), ("ln1_b", 8), ("ln2_g", 8), ("ln2_b", 8),
                  ("conv_w", 8 * TAPS)):
    VEC1[_name] = sum(n for _, n in VEC1.values()), _n
N_VEC1 = sum(n for _, n in VEC1.values())
VEC2 = {}
for _name, _n in (("attn_norm", 8), ("q_norm", 2), ("kv_norm", 1), ("conv_w", 6), ("pool_scale", 2), ("mix_norm", 8),
                  ("ffn_norm", 8), ("sinks", 4)):
    VEC2[_name] = sum(n for _, n in VEC2.values()), _n
N_VEC2 = sum(n for _, n in VEC2.values())
ROWS = 16
CONST1 = {}
for _name, _n in (("ident", P), ("mean1024", P), ("mean256", P), ("mean128", P), ("rot", P), ("cos", S), ("sin", S),
                  ("head128", (KVH + HEADS) * ROWS), ("head256", 4 * ROWS), ("pair", 2), ("alpha", 2)):
    CONST1[_name] = sum(n for _, n in CONST1.values()), _n
N_CONST1 = sum(n for _, n in CONST1.values())
CONST2 = {}
for _name, _n in (("rot", P), ("cos", S), ("sin", S), ("inv_count", 2 * S), ("causal", QT * S), ("window", SH * QT * S)):
    CONST2[_name] = sum(n for _, n in CONST2.values()), _n
N_CONST2 = sum(n for _, n in CONST2.values())
GLR = 32 + RANK
N_SMALL2 = 2 * MH * QK + MH * (NOPE + MV) + 2 * P
N_MASK = 2 * (len(LEVELS) - 1) + 1


class Tally:

    def __init__(self):
        self.of = {}

    def up(self, name, k=1):
        self.of[name] = self.of.get(name, 0) + k
        return self.of[name]

    def at(self, name):
        return self.of.get(name, 0)


def spread(units, steps):
    return [[u for k, u in enumerate(units) if k * steps // len(units) == j] for j in range(steps)]


def returned(steps):
    out, held = [], []
    for step in steps:
        out.append([])
        for u in step:
            out[-1] += [u] + held
            held = [("adt", u[1])] if u[0] == "ada" else []
    out[-1] += held
    return out


FIRST_UNITS = returned([[("ada", (0, g)) for g in range(ADA_FIRST)]])[0]


def attention_fill(l, s):
    units = [("glr", 0)] + [("vg", c) for c in range(GH)]
    if l == 0:
        units += [("ada", (s, g)) for g in (range(ADA_FIRST, 16) if s == CTX else range(8))]
    return units


def gla_fill(l, s):
    units = [("cy", c) for c in range(KC)]
    if s == LAT:
        units += [("r", c) for c in range(KC)]
    groups = range(16, 20) if s == CTX else range(16, 22) if l else [8, 9, 12, 13, 14, 15]
    units += [("ada", (max(l, s), g)) for g in groups]
    return units


def out_fill(l, s):
    if s == LAT:
        return {}
    a, b = (0, 20), (0, 21)
    return {1: ("ada", a), 2: ("adt", a), 4: ("ada", b), 5: ("adt", b)}


def norm_fill(l, s):
    return [("ada", (max(l, s), g)) for g in ((22, 23) if s == CTX or l else (10, 11))]


STEPS = 2 * len(LEVELS) + 1


PASSES = [(l, s) for l in range(DEPTH) for s in (CTX, LAT)]


def whole(l, s):
    return s == LAT or l < DEPTH - 1


IDLE = 10
HAT_STEP = 8
STATE_UNITS = [("kt", c) for c in range(2 * QT)] + [("st", c) for c in range(2 * GH // 2)]


def gla_steps(l, s):
    if not whole(l, s):
        return [[("kg", 2), ("kg", 3)] + [("vg", c) for c in range(GH)]]
    units = gla_fill(l, s)
    steps = returned([units[:4], units[4:7]] + spread(units[7:], STEPS - 1))
    if s == CTX:
        for k, u in enumerate(STATE_UNITS):
            steps[HAT_STEP + 5 + k // 2].append(u)
    return steps


def program(nc, stream, xt_in, cvec_in, vec1_in, vec2_in, glr_in, a2_in, const1_in, const2_in, small2_in, mask_in, out):
    F32 = mybir.dt.float32
    F32R = mybir.dt.float32r
    U8 = mybir.dt.uint8
    ACT = mybir.ActivationFunctionType
    AXX = mybir.AxisListType.X
    with ExitStack() as ctx:
        def sb(name, shape, dt=F32):
            return ctx.enter_context(nc.sbuf_tensor(name, shape, dt))

        def sem(name):
            return ctx.enter_context(nc.semaphore(name))

        w_raw = sb("w_raw", [P, SLOTS, TILES * P])
        w_hi = sb("w_hi", [P, SLOTS, TILES * P], F32R)
        w_lo = sb("w_lo", [P, SLOTS, TILES * P], F32R)
        X = sb("X", [P, KC, 2 * S])
        h_hi = sb("h_hi", [P, KC, S], F32R)
        h_lo = sb("h_lo", [P, KC, S], F32R)
        s_hi = sb("s_hi", [P, HALF, S], F32R)
        s_lo = sb("s_lo", [P, HALF, S], F32R)
        M = sb("M", [P, KC, S])
        arena1 = sb("arena1", [P, 10240])
        arena2 = sb("arena2", [P, 8192])
        gate_buf = sb("gate_buf", [P, 2, S])
        y_buf = sb("y_buf", [P, 2, S])
        std = sb("std", [P, 2, S])
        rstd = sb("rstd", [P, S])
        tmp = sb("tmp", [P, S])
        vec1 = sb("vec1", [P, DEPTH, N_VEC1])
        vec2 = sb("vec2", [P, DEPTH * N_VEC2 + KC])
        cvec = sb("cvec", [P, KC, 2])
        c_hl = sb("c_hl", [P, KC, 4], F32R)
        mod_rows = sb("mod_rows", [4, 2, ADA_COLS])
        mod = sb("mod", [P, DEPTH, 48, 2])
        wglr = sb("wglr", [P, DEPTH * KC * GLR])
        wglr_hi = sb("wglr_hi", [P, DEPTH * KC * GLR], F32R)
        wglr_lo = sb("wglr_lo", [P, DEPTH * KC * GLR], F32R)
        wa2 = sb("wa2", [GLR, DEPTH, GH * GDK])
        const1 = sb("const1", [P, N_CONST1])
        masks = sb("masks", [P, N_MASK, P], U8)
        small = sb("small", [P, 2, 16])

        def view(t, at, *shape):
            n = int(np.prod(shape))
            v = t[:, at:at + n]
            if len(shape) == 2:
                return v.rearrange("p (a b) -> p a b", a=shape[0])
            if len(shape) == 3:
                return v.rearrange("p (a b c) -> p a b c", a=shape[0], b=shape[1])
            if len(shape) == 4:
                return v.rearrange("p (a b c d) -> p a b c d", a=shape[0], b=shape[1], c=shape[2])
            return v

        Q = view(arena1, 0, HEADS, S)
        K = view(arena1, 2048, KVH, 2 * S)
        V = view(arena1, 3072, 2 * QT, KVH * DH)
        state = view(arena1, 4096, 2, GH, GDV)
        KG = view(arena1, 6144, GH, S)
        QG = view(arena1, 7168, GH, S)
        VG = view(arena1, 8192, QT, GH * GDV)
        YP = view(arena2, 0, KC, S + 2 * PAD)
        CV = view(arena2, KC * (S + 2 * PAD), KC, S)
        W = CV
        pt_at = KC * (2 * S + 2 * PAD)
        probs = view(arena2, pt_at, 2, 2 * S)
        probsT = view(arena2, pt_at + 4 * S, 2, 2 * QT, P)
        glr = view(arena2, pt_at + 8 * S, S)
        assert pt_at + 9 * S <= 8192
        Z = view(arena2, 0, 2 * GH, S)
        DL = view(arena2, 0, 2, GH, S)
        HAT = view(arena1, 0, GH, 2, S)
        B = view(arena2, 2048, 2 * GH, S)
        A = view(arena2, 4096, GH, QT, S)
        KT = view(arena2, 6144, 2, QT, GH, P)
        rbuf = view(arena2, 6144, KC, S)
        early = view(arena2, 4096, KC, S)
        gbuf = view(arena2, 2048, KC, S)
        osq = view(arena2, 0, KC, S)
        hsq = view(arena1, 7168, KVH + HEADS, S)
        a = 0
        w2 = {}
        for name, shape in (("cq", (2, S)), ("ckv", (1, S)), ("kr", (1, S)), ("qh", (MH, S)), ("kh", (MH, S)),
                            ("vm", (QT, MH * MV)), ("gb", (2, S)), ("gc", (2, S)), ("uc", (2, S)), ("zp", (2, S + 2)),
                            ("up", (2, S + 16)), ("qs", (2, S)), ("ks", (1, S))):
            w2[name] = view(arena1, a, *shape)
            a += int(np.prod(shape))
        small2 = view(arena1, 10240 - DEPTH * N_SMALL2, DEPTH, N_SMALL2)
        assert a <= 10240 - DEPTH * N_SMALL2
        a = 0
        for name, shape in (("probs", (2, 2 * S)), ("probsT", (2, 2 * QT, P)), ("scores", (2, 2 * S)), ("p2", (2, S + 16)),
                            ("p4", (2, S + 16))):
            w2[name] = view(arena2, a, *shape)
            a += int(np.prod(shape))
        assert a + N_CONST2 <= 8192
        const2 = arena2[:, 8192 - N_CONST2:8192]
        w2["p8"] = view(arena2, 0, 2, S + 16)
        w2["p16"] = view(arena2, 1024, 2, S + 16)
        w2["pooled"] = view(arena2, 2048, 2, S)
        w2["vs"] = M[:, 0, :].rearrange("p (a b) -> p a b", a=QT)
        w2["vf"] = M[:, 1, :]
        w2["mx"] = X[:, :, 0:S]

        def c1(name):
            at, n = CONST1[name]
            return const1[:, at:at + n]

        def c2(name):
            at, n = CONST2[name]
            return const2[:, at:at + n]

        def v1(l, name, c=0):
            at = VEC1[name][0] + c
            return vec1[:, l, at:at + 1]

        def v2(l, name, c=0):
            at = l * N_VEC2 + VEC2[name][0] + c
            return vec2[:, at:at + 1]

        lin = [ctx.enter_context(nc.psum_tensor(f"lin{i}", [P, 512], F32)) for i in range(4)]
        aux = [ctx.enter_context(nc.psum_tensor(f"aux{i}", [P, 512], F32)) for i in range(4)]

        landed = [sem(f"landed{i}") for i in range(SLOTS)]
        NAMES = ("hi_ready",
                 "lo_ready",
                 "w_used",
                 "lin_done",
                 "lin_evac",
                 "params", "c_landed", "x_landed", "b2_landed", "stored",
                 "c_ready",
                 "glr_split",
                 "silu_ready",
                 "sum_ready",
                 "x_ready", "r_ready",
                 "mean_done", "xc_ready", "sq_ready", "var_done", "std_ready",
                 "t_ready", "early_ready", "hi_part", "h_ready",
                 "y_ready", "conv_done", "sigmoid_ready", "m_ready",
                 "s_ready",
                 "row_ready", "spread_done", "qk_normed", "rot_done", "qk_ready",
                 "s_done", "nb_ready", "p_ready", "pn_ready", "pt_done", "pt_ready", "o_done", "o_hi", "o_ready",
                 "ln_ready", "diff_ready", "lev_exp", "lev_ready", "gram_done", "a_copied", "hat_diff", "hat_exp", "hat_ready",
                 "og_ready", "dve_step", "act_step", "pooled_ready", "yb_ready", "fin_ready")
        sems = {name: sem(name) for name in NAMES}
        block = ctx.enter_context(nc.Block())

        class Place:

            def __init__(self):
                self.n = Tally()
                self.tile = 0
                self.bank = 0
                self.split = 0
                self.tile_done = 0
                self.turn = None

            def value(self, name, base):
                if self.turn is None or not self.per.get(name):
                    return base
                return self.turn * self.per[name] + base

            def up(self, name, k=1):
                return self.value(name, self.n.up(name, k))

            def now(self, name):
                return self.value(name, self.n.at(name))

            def next_bank(self):
                b = self.bank
                self.bank = (b + 1) % 4
                return lin[b]

            def enter(self, i, **other):
                self.turn, self.per = i, dict(PER_HALF, **other)
                self.start = dict(self.n.of)
                self.first = self.tile, self.split

            def leave(self):
                self.turn = None
                for name, k in self.per.items():
                    if self.n.at(name) != self.start.get(name, 0):
                        assert self.n.at(name) - self.start.get(name, 0) == k, (name, self.n.at(name) - self.start.get(name, 0), k)
                        self.n.up(name, k)
                self.split += self.split - self.first[1]
                self.tile += self.tile - self.first[0]
                self.tile_done = self.tile

        PARAMS = 16 * 6

        @block.sync
        def _(sp):
            sp.dma_start(cvec[:, :, :], cvec_in).then_inc(sems["c_landed"], 16)
            sp.dma_start(X[:, :, 0:S], xt_in[:, :, 0:S]).then_inc(sems["x_landed"], 16)
            sp.dma_start(const1[:, :], const1_in).then_inc(sems["x_landed"], 16)
            for s in range(SLOTS):
                sp.dma_start(w_raw[:, s, :], stream[s]).then_inc(landed[s], 16)
            sp.dma_start(vec1[:, :, :], vec1_in).then_inc(sems["params"], 16)
            sp.dma_start(wglr[:, :], glr_in).then_inc(sems["params"], 16)
            sp.dma_start(wa2[:, :, :], a2_in).then_inc(sems["params"], 16)
            sp.dma_start(view(arena2, pt_at, N_MASK, P), mask_in).then_inc(sems["params"], 16)
            sp.dma_start(vec2[:, :], vec2_in).then_inc(sems["params"], 16)
            sp.dma_start(X[:, :, S:2 * S], xt_in[:, :, S:2 * S]).then_inc(sems["params"], 16)
            with sp.Fori(1, LOADS // SLOTS) as i:
                for s in range(SLOTS):
                    sp.wait_ge(sems["lo_ready"], i * SLOTS + (s + 1 - SLOTS))
                    sp.dma_start(w_raw[:, s, :], stream[bass.ds(i * SLOTS + s, 1)].rearrange("a p n -> p (a n)")
                                 ).then_inc(landed[s], 16)
            sp.wait_ge(sems["fin_ready"], 1)
            sp.dma_start(out, W[:, :, :]).then_inc(sems["stored"], 16)
            sp.wait_ge(sems["stored"], 16)

        @block.gpsimd
        def _(pool):
            with pool.Fori(0, LOADS // SLOTS) as i:
                for s in range(SLOTS):
                    pool.wait_ge(sems["hi_ready"], i * SLOTS + (s + 1))
                    pool.tensor_tensor(w_lo[:, s, :], w_raw[:, s, :], w_hi[:, s, :].bitcast(F32), ALU.subtract
                                       ).then_inc(sems["lo_ready"], 1)

        @block.tensor
        def _(pe):
            at = Place()
            n = at.n

            def weight(tiles=1):
                t = at.tile
                at.tile += tiles
                load, k = divmod(t, TILES)
                if k == 0:
                    pe.wait_ge(sems["lo_ready"], at.value("lo_ready", load + 1))
                cols = slice(k * P, (k + tiles) * P)
                return w_hi[:, load % SLOTS, cols], w_lo[:, load % SLOTS, cols], k == 0 and load > 0

            def used(mm, first):
                if first:
                    mm.then_inc(sems["w_used"], 1)

            def bank():
                c = n.up("lin_done")
                if c > 4:
                    pe.wait_ge(sems["lin_evac"], at.value("lin_evac", c - 4))
                return at.next_bank()

            def done(mm):
                mm.then_inc(sems["lin_done"], 1)

            def dense(hi, lo, ready=None, kcs=KC):
                o = bank()[:, 0:S]
                for k in range(kcs):
                    whi, wlo, first = weight()
                    if ready:
                        pe.wait_ge(sems[ready[0]], at.value(ready[0], ready[1] + k + 1))
                    used(pe.matmul(o, whi, hi[:, k, :], start=k == 0, stop=False), first)
                    pe.matmul(o, whi, lo[:, k, :], start=False, stop=False)
                    mm = pe.matmul(o, wlo, hi[:, k, :], start=False, stop=k == kcs - 1)
                done(mm)

            def dense_together(chunks, ready):
                banks, start = [bank() for _ in range(chunks)], at.tile
                for k in range(KC):
                    pe.wait_ge(sems[ready[0]], at.value(ready[0], ready[1] + k + 1))
                    for c, o in enumerate(banks):
                        at.tile = start + c * KC + k
                        whi, wlo, first = weight()
                        mm = pe.matmul(o[:, 0:S], whi, h_hi[:, k, :], start=k == 0, stop=False)
                        used(mm, first if c == 0 else k == KC - 1)
                        pe.matmul(o[:, 0:S], whi, h_lo[:, k, :], start=False, stop=False)
                        mm = pe.matmul(o[:, 0:S], wlo, h_hi[:, k, :], start=False, stop=k == KC - 1)
                        if k == KC - 1:
                            done(mm)

            def token_major():
                banks = [bank(), bank()]
                for k in range(KC):
                    whi, wlo, first = weight(2)
                    for tt, o in enumerate(banks):
                        xhi, xlo = h_hi[:, k, tt * P:(tt + 1) * P], h_lo[:, k, tt * P:(tt + 1) * P]
                        mm = pe.matmul(o[:, 0:2 * P], xhi, whi, start=k == 0, stop=False)
                        used(mm, first and tt == 0)
                        pe.matmul(o[:, 0:2 * P], xhi, wlo, start=False, stop=False)
                        mm = pe.matmul(o[:, 0:2 * P], xlo, whi, start=False, stop=k == KC - 1)
                        if k == KC - 1:
                            done(mm)

            rows = {}

            def ada(group):
                o = bank()
                for k in range(KC):
                    whi, wlo, first = weight(ADA_CHUNKS)
                    used(pe.matmul(o[0:4, 0:ADA_COLS], c_hl[:, k, :], whi, start=k == 0, stop=False), first)
                    mm = pe.matmul(o[0:4, 0:ADA_COLS], c_hl[:, k, :], wlo, start=False, stop=k == KC - 1)
                done(mm)
                rows[group] = len(rows) % 2, n.at("lin_done")

            def ada_back(group):
                o = bank()
                b, moved = rows[group]
                pe.wait_ge(sems["lin_evac"], at.value("lin_evac", moved))
                for c in range(ADA_CHUNKS):
                    mm = pe.matmul(o[:, 2 * c:2 * c + 2], mod_rows[:, b, c * P:(c + 1) * P], c1("pair")[0:4, :], start=True, stop=True)
                done(mm)

            def unit(l, s, u):
                kind, c = u
                if kind in ("kg", "r"):
                    dense(h_hi, h_lo)
                elif kind == "cy":
                    dense(s_hi, s_lo, ("s_ready", n.at("s_ready") - KC))
                elif kind == "vg":
                    token_major()
                elif kind == "kt":
                    d, kt = divmod(c, QT)
                    if c == 0:
                        pe.wait_ge(sems["hat_ready"], at.up("hat_ready", 2))
                    o = bank()
                    for h in range(GH):
                        mm = pe.transpose(o[:, h * P:(h + 1) * P], HAT[:, h, d, kt * P:(kt + 1) * P], c1("ident"))
                    done(mm)
                elif kind == "st":
                    pe.wait_ge(sems["lin_evac"], at.value("lin_evac", n.at("lin_done")))
                    o = bank()
                    for k in range(2):
                        d, h = divmod(2 * c + k, GH)
                        for kt in range(QT):
                            mm = pe.matmul(o[:, k * GDV:(k + 1) * GDV], KT[:, d, kt, h, :],
                                           VG[:, kt, h * GDV:(h + 1) * GDV], start=kt == 0, stop=kt == QT - 1)
                    done(mm)
                elif kind == "glr":
                    o = bank()
                    for k in range(KC):
                        a = (l * KC + k) * GLR
                        pe.matmul(o[0:GLR, 0:S], wglr_hi[:, a:a + GLR], h_hi[:, k, :], start=k == 0, stop=False)
                        pe.matmul(o[0:GLR, 0:S], wglr_hi[:, a:a + GLR], h_lo[:, k, :], start=False, stop=False)
                        mm = pe.matmul(o[0:GLR, 0:S], wglr_lo[:, a:a + GLR], h_hi[:, k, :], start=False, stop=k == KC - 1)
                    done(mm)
                elif kind == "ada":
                    ada(c)
                else:
                    ada_back(c)

            def mean_chunk(x, k):
                mm = pe.matmul(aux[0][:, 0:S], c1("mean1024"), x[:, k, :], start=k == 0, stop=k == KC - 1)
                if k == KC - 1:
                    mm.then_inc(sems["mean_done"], 1)

            def variance(squares):
                for k in range(KC):
                    if k % 2 == 0:
                        pe.wait_ge(sems["sq_ready"], at.up("sq_ready"))
                    mm = pe.matmul(aux[1][:, 0:S], c1("mean1024"), squares[:, k, :], start=k == 0, stop=k == KC - 1)
                mm.then_inc(sems["var_done"], 1)

            def keep_clock(k):
                for _ in range(k):
                    pe.matmul(aux[3][:, 0:S], c1("mean1024"), const1[:, 0:S], start=True, stop=True)

            def layernorm(x, ready=None):
                for k in range(KC):
                    if ready:
                        pe.wait_ge(sems[ready], at.up(ready))
                    mean_chunk(x, k)
                variance(M)

            def head_rows(chunks):
                for j, (name, h, squares) in enumerate(chunks):
                    a = h * ROWS
                    mm = pe.matmul(aux[0][0:ROWS, 0:S], c1(name)[:, a:a + ROWS], squares, start=j == 0, stop=j == len(chunks) - 1)
                mm.then_inc(sems["var_done"], 1)

            def spread_row(o, h):
                return pe.matmul(o, c1("ident")[0:ROWS, h:h + 1].broadcast_to([ROWS, P]), rstd[0:ROWS, :], start=True, stop=True)

            def rotate(heads, j, q0, r0):
                pe.wait_ge(sems["qk_normed"], at.value("qk_normed", q0 + j + 1))
                if j >= 2:
                    pe.wait_ge(sems["qk_ready"], at.value("qk_ready", r0 + j - 1))
                pe.matmul(aux[3 * (j % 2)][:, 0:S], c1("rot"), heads[j][0], start=True, stop=True).then_inc(sems["rot_done"], 1)

            def attention(items, p_tile, pt_tile, fill, run):
                def scores(j):
                    qs, keys, _, _ = items[j]
                    if j >= 2:
                        pe.wait_ge(sems["p_ready"], at.value("p_ready", n.at("p_ready") + j - 1))
                    w = 2 * S // len(qs)
                    for g, q in enumerate(qs):
                        mm = pe.matmul(aux[j % 2][:, g * w:(g + 1) * w], q, keys, start=True, stop=True)
                    mm.then_inc(sems["s_done"], 1)

                def transposes(j):
                    pe.wait_ge(sems["pn_ready"], at.up("pn_ready"))
                    if j >= 1:
                        pe.wait_ge(sems["pt_ready"], pt0 + j)
                    for k in range(4):
                        mm = pe.transpose(aux[2][:, k * P:(k + 1) * P], p_tile[:, j % 2, k * P:(k + 1) * P], c1("ident"))
                    mm.then_inc(sems["pt_done"], 1)

                def values(j):
                    qs, _, vs, rows = items[j]
                    pe.wait_ge(sems["pt_ready"], pt0 + j + 1)
                    if j >= 1:
                        pe.wait_ge(sems["o_ready"], at.up("o_ready"))
                    per = 4 // len(qs)
                    for g in range(len(qs)):
                        for k in range(per):
                            mm = pe.matmul(aux[3][rows[0]:rows[1], g * P:(g + 1) * P], vs[k], pt_tile[:, j % 2, g * per + k, :],
                                           start=k == 0, stop=k == per - 1)
                    mm.then_inc(sems["o_done"], 1)
                pt0 = n.at("pt_ready")
                for j in range(len(items) + 3):
                    if j < len(items):
                        scores(j)
                    if 2 <= j < len(items) + 2:
                        transposes(j - 2)
                    if j >= 3:
                        values(j - 3)
                    if j < len(items):
                        for u in fill[j]:
                            run(u)
                n.up("pt_ready", len(items))
                n.up("p_ready", len(items))
                pe.wait_ge(sems["o_ready"], at.up("o_ready"))

            def sum_to_mean():
                pe.matmul(aux[0][:, 0:S], c1("mean1024"), std[:, 1, :], start=True, stop=True).then_inc(sems["mean_done"], 1)

            def feed_forward():
                h0 = n.at("h_ready") - KC
                with pe.Fori(0, 2) as i:
                    at.enter(i)
                    pe.wait_ge(sems["lin_evac"], at.value("lin_evac", n.at("lin_done")))
                    at.bank = 0
                    dense_together(2, ("h_ready", h0))
                    for c in range(2, 2 * HALF):
                        dense(h_hi, h_lo)
                    s0 = n.at("s_ready")
                    n.up("s_ready", HALF)
                    for c in range(KC):
                        dense(s_hi, s_lo, ("s_ready", s0) if c == 0 else None, kcs=HALF)
                    n.up("r_ready", KC)
                    n.up("sum_ready")
                    at.leave()

            def gla(l, s, full):
                fill = gla_steps(l, s)
                for j in range(4):
                    o = bank()
                    for k in range(2):
                        d, h = divmod(2 * j + k, GH)
                        mm = pe.matmul(o[:, k * S:(k + 1) * S], wa2[32 * d:32 * d + RANK, l, h * GDK:(h + 1) * GDK],
                                       glr[32 * d:32 * d + RANK, :], start=True, stop=True)
                    done(mm)
                for u in fill[0]:
                    unit(l, s, u)
                if full:
                    a0 = n.at("a_copied")
                    for j in range(STEPS):
                        for u in fill[j + 1]:
                            unit(l, s, u)
                        pair = [aux[2 * (j % 2)], aux[2 * (j % 2) + 1]]
                        if j < STEPS - 1:
                            pe.wait_ge(sems["lev_ready"], at.up("lev_ready"))
                        if j >= 2:
                            pe.wait_ge(sems["a_copied"], at.value("a_copied", a0 + j - 1))
                        if j < 2:
                            ks, qs = (0, P) if j == 0 else (P, 0)
                            for h in range(GH):
                                mm = pe.matmul(pair[0][:, h * P:(h + 1) * P], DL[:, j % 2, h, ks:ks + P],
                                               DL[:, j % 2, h, qs:qs + P], start=True, stop=True)
                        elif j < STEPS - 1:
                            for kt in range(QT):
                                for h in range(GH):
                                    part = DL[:, j % 2, h, kt * P:(kt + 1) * P]
                                    mm = pe.matmul(pair[kt][:, h * P:(h + 1) * P], part, part, start=True, stop=True)
                        else:
                            for kt in range(QT):
                                for h in range(GH):
                                    tok = slice(kt * P, (kt + 1) * P)
                                    for rep in range(2):
                                        mm = pe.matmul(pair[kt][:, h * P:(h + 1) * P], KG[:, h, tok], QG[:, h, tok],
                                                       start=rep == 0, stop=rep == 1)
                        mm.then_inc(sems["gram_done"], 1)
                    n.up("a_copied", STEPS)
                if not full:
                    pe.wait_ge(sems["x_ready"], n.at("x_ready"))
                    for k in range(KC):
                        mean_chunk(X[:, :, S:2 * S], k)
                    for u in STATE_UNITS:
                        if u == ("st", 0):
                            variance(M)
                        unit(l, s, u)
                elif s == LAT:
                    pe.wait_ge(sems["hat_ready"], at.up("hat_ready", 2))
                if full:
                    pe.wait_ge(sems["a_copied"], at.value("a_copied", n.at("a_copied")))
                    for h in range(GH):
                        o = bank()
                        for c in range(2):
                            e = h * GDV + c * P
                            for kt in range(QT):
                                mm = pe.matmul(o[:, c * S:(c + 1) * S], VG[:, kt, e:e + P], A[:, h, kt, :],
                                               start=kt == 0, stop=kt == QT - 1 and s == CTX)
                            if s == LAT:
                                for d in range(2):
                                    mm = pe.matmul(o[:, c * S:(c + 1) * S], state[:, d, h, c * P:(c + 1) * P],
                                                   HAT[:, h, d, :], start=False, stop=d == 1)
                        done(mm)

            pe.wait_ge(sems["x_landed"], 2 * 16)
            for turn, (l, s) in enumerate(PASSES):
                    full = whole(l, s)
                    x = X[:, :, s * S:(s + 1) * S]
                    ready = "h_ready", n.at("h_ready")
                    norm_left = turn > 0 and whole(*PASSES[turn - 1])
                    if turn == 0:
                        layernorm(x)
                        pe.wait_ge(sems["c_ready"], at.up("c_ready", 2))
                        for u in FIRST_UNITS:
                            unit(l, s, u)
                        pe.wait_ge(sems["glr_split"], at.up("glr_split", 2))
                    n.up("h_ready", KC)
                    if full:
                        dense_together(2, ready)
                        for c in range(2, 2 * KC):
                            if norm_left and c == 2:
                                pe.wait_ge(sems["sum_ready"], n.at("sum_ready"))
                                sum_to_mean()
                            if norm_left and c == 4:
                                variance(M)
                            dense(h_hi, h_lo)
                        for c in range(KVH + HEADS):
                            dense(h_hi, h_lo)
                    else:
                        dense_together(KVH, ready)
                        pe.wait_ge(sems["sum_ready"], n.at("sum_ready"))
                        sum_to_mean()
                    token_major()
                    if not full:
                        variance(M)
                        unit(l, s, ("glr", 0))
                    heads = [(K[:, c, s * S:(s + 1) * S], c) for c in range(KVH)] + [(Q[:, c, :], KVH + c) for c in range(HEADS) if full]
                    pe.wait_ge(sems["sq_ready"], at.up("sq_ready"))
                    head_rows([("head128", c, hsq[:, c, :]) for _, c in heads])
                    for c in range(GH if full else 2):
                        dense(h_hi, h_lo)
                    pe.wait_ge(sems["row_ready"], at.up("row_ready"))
                    q0, r0 = n.at("qk_normed"), n.at("qk_ready")
                    for j in range(len(heads)):
                        if j >= 2:
                            pe.wait_ge(sems["qk_normed"], at.value("qk_normed", q0 + j - 1))
                        spread_row(aux[1 + j % 2][:, 0:S], heads[j][1]).then_inc(sems["spread_done"], 1)
                        if s == LAT and j >= 1:
                            rotate(heads, j - 1, q0, r0)
                        if j in (2, 4, 6, 8):
                            dense(h_hi, h_lo)
                    if s == LAT:
                        rotate(heads, len(heads) - 1, q0, r0)
                        n.up("qk_ready", len(heads))
                        pe.wait_ge(sems["qk_ready"], at.value("qk_ready", n.at("qk_ready")))
                    n.up("qk_normed", len(heads))
                    pe.wait_ge(sems["qk_normed"], at.value("qk_normed", n.at("qk_normed")))
                    if full:
                        items = []
                        for h in range(HEADS):
                            g = h // (HEADS // KVH)
                            if s == CTX:
                                items.append(([Q[:, h, qt * P:(qt + 1) * P] for qt in range(QT)], K[:, g, 0:S],
                                              [V[:, kt, g * DH:(g + 1) * DH] for kt in range(QT)], (0, P)))
                            else:
                                items += [([Q[:, h, qt * P:(qt + 1) * P]], K[:, g, :],
                                           [V[:, kt, g * DH:(g + 1) * DH] for kt in range(2 * QT)], (0, P)) for qt in range(QT)]
                        attention(items, probs, probsT, returned(spread(attention_fill(l, s), len(items))), lambda u: unit(l, s, u))
                        pe.wait_ge(sems["conv_done"], at.up("conv_done"))
                        for k in range(KC):
                            mean_chunk(CV, k)
                        for c in range(KC):
                            dense(h_hi, h_lo)
                            dense(s_hi, s_lo)
                            if c == 4:
                                variance(osq)
                        for c in range(KC):
                            dense(h_hi, h_lo)
                        n.up("s_ready", KC)
                    pe.wait_ge(sems["lin_evac"], at.value("lin_evac", n.at("lin_done")))
                    gla(l, s, full)
                    if not full:
                        continue
                    pe.wait_ge(sems["sq_ready"], at.up("sq_ready"))
                    head_rows([("head256", c // 2, osq[:, c, :]) for c in range(KC)])
                    first = KC if s == CTX else 0
                    for c in range(first + KC):
                        dense(h_hi, h_lo)
                        if c == 4:
                            pe.wait_ge(sems["row_ready"], at.up("row_ready"))
                            for h in range(GH):
                                mm = spread_row(aux[1 + h // 2][:, h % 2 * S:h % 2 * S + S], h)
                                if h % 2:
                                    mm.then_inc(sems["spread_done"], 1)
                    ready = "s_ready", n.at("s_ready")
                    n.up("s_ready", KC)
                    for c in range(KC):
                        dense(s_hi, s_lo, ready if c == 0 else None)
                    ready = "h_ready", n.at("h_ready")
                    n.up("h_ready", KC)
                    for c in range(KC):
                        dense(h_hi, h_lo, ready if c == 0 else None)
                        if c == 1 and turn < 2:
                            pe.wait_ge(sems["x_ready"], n.at("x_ready"))
                            ns = PASSES[turn + 1][1]
                            for k in range(KC):
                                mean_chunk(X[:, :, ns * S:(ns + 1) * S], k)
                        if c == 4 and turn < 2:
                            variance(M)
                        if c in out_fill(l, s):
                            unit(l, s, out_fill(l, s)[c])
                    n.up("r_ready", KC)
                    pe.wait_ge(sems["sum_ready"], at.up("sum_ready"))
                    sum_to_mean()
                    beside = norm_fill(l, s)
                    unit(l, s, beside[0])
                    variance(M)
                    unit(l, s, ("adt", beside[0][1]))
                    unit(l, s, beside[1])
                    layernorm(x, "x_ready")
                    unit(l, s, ("adt", beside[1][1]))
                    keep_clock(IDLE)
                    n.up("h_ready", KC)
                    feed_forward()
                    if turn == 3:
                        pe.wait_ge(sems["sum_ready"], n.at("sum_ready"))
                        sum_to_mean()
                        variance(M)
                        keep_clock(IDLE)
                    n.up("x_ready", KC)

            x = X[:, :, S:2 * S]
            pe.wait_ge(sems["b2_landed"], 32)
            for l in range(DEPTH):
                variance(M)
                keep_clock(IDLE)
                ready = "h_ready", n.at("h_ready")
                n.up("h_ready", KC)
                dense_together(2, ready)
                dense(h_hi, h_lo)
                dense(h_hi, h_lo)
                for c in range(12):
                    dense(h_hi, h_lo)
                    if c == 3:
                        pe.wait_ge(sems["sq_ready"], at.up("sq_ready", 2))
                        for k in range(2):
                            mm = pe.matmul(aux[0][:, 0:S], c1("mean256"), gate_buf[:, k, :], start=k == 0, stop=k == 1)
                        mm.then_inc(sems["var_done"], 1)
                        pe.matmul(aux[1][:, 0:S], c1("mean128"), y_buf[:, 0, :], start=True, stop=True).then_inc(sems["var_done"], 1)
                pe.wait_ge(sems["qk_normed"], at.up("qk_normed", 2))
                wuq = small2[:, l, 0:2 * MH * QK]
                wukv = small2[:, l, 2 * MH * QK:2 * MH * QK + MH * (NOPE + MV)]
                wpool = small2[:, l, 2 * MH * QK + MH * (NOPE + MV):N_SMALL2]
                for h in range(MH):
                    o = bank()
                    for k in range(2):
                        a = (k * MH + h) * QK
                        mm = pe.matmul(o[0:QK, 0:S], wuq[:, a:a + QK], w2["cq"][:, k, :], start=k == 0, stop=k == 1)
                    done(mm)
                for h in range(MH):
                    o = bank()
                    a = h * (NOPE + MV)
                    done(pe.matmul(o[0:NOPE, 0:S], wukv[:, a:a + NOPE], w2["ckv"][:, 0, :], start=True, stop=True))
                o = bank()
                vcols = wukv.rearrange("p (h e) -> p h e", h=MH)[:, :, NOPE:]
                for tt in range(QT):
                    mm = pe.matmul(o[:, tt * MH * MV:(tt + 1) * MH * MV], w2["ckv"][:, 0, tt * P:(tt + 1) * P], vcols,
                                   start=True, stop=True)
                done(mm)
                o = bank()
                for tt in range(QT):
                    mm = pe.transpose(o[:, tt * P:(tt + 1) * P], w2["vf"][:, tt * P:(tt + 1) * P], c1("ident"))
                done(mm)
                rot = c2("rot")
                pe.wait_ge(sems["lin_evac"], at.value("lin_evac", n.at("lin_done")))
                pe.matmul(aux[2][NOPE:QK, 0:S], rot[NOPE:QK, NOPE:QK], w2["kr"][NOPE:QK, 0, :], start=True, stop=True
                          ).then_inc(sems["rot_done"], 1)
                for h in range(MH):
                    if h >= 1:
                        pe.wait_ge(sems["qk_ready"], at.value("qk_ready", n.at("qk_ready") + h))
                    pe.matmul(aux[2 + (h + 1) % 2][0:QK, 0:S], rot[0:QK, 0:QK], w2["qh"][0:QK, h, :], start=True, stop=True
                              ).then_inc(sems["rot_done"], 1)
                pe.wait_ge(sems["pooled_ready"], at.up("pooled_ready"))
                for c in range(2):
                    o = bank()
                    done(pe.matmul(o[:, 0:S], wpool[:, c * P:(c + 1) * P], w2["pooled"][:, c, :], start=True, stop=True))
                pe.wait_ge(sems["qk_ready"], at.up("qk_ready", MH + 1))
                items = []
                for h in range(MH):
                    items.append(([w2["qh"][0:QK, h, qt * P:(qt + 1) * P] for qt in range(QT)], w2["kh"][0:QK, h, :],
                                  [w2["vm"][:, kt, h * MV:(h + 1) * MV] for kt in range(QT)], (64 * (h % 2), 64 * (h % 2) + 64)))
                for h in range(SH):
                    g, j = divmod(h, 2)
                    items.append(([w2["qs"][64 * g:64 * g + 64, j, qt * P:(qt + 1) * P] for qt in range(QT)],
                                  w2["ks"][64 * g:64 * g + 64, 0, :],
                                  [w2["vs"][:, kt, g * SHD:(g + 1) * SHD] for kt in range(QT)], (64 * (h % 2), 64 * (h % 2) + 64)))
                attention(items, w2["probs"], w2["probsT"], [[]] * len(items), None)
                pe.wait_ge(sems["sq_ready"], at.up("sq_ready", 4))
                head_rows([("head256", c // 2, M[:, c, :]) for c in range(KC)])
                keep_clock(IDLE // 2)
                pe.wait_ge(sems["row_ready"], at.up("row_ready"))
                for h in range(4):
                    mm = spread_row(aux[1 + h // 2][:, h % 2 * S:h % 2 * S + S], h)
                    if h % 2:
                        mm.then_inc(sems["spread_done"], 1)
                ready = "s_ready", n.at("s_ready")
                n.up("s_ready", KC)
                for c in range(KC):
                    dense(s_hi, s_lo, ready if c == 0 else None)
                n.up("r_ready", KC)
                variance(M)
                keep_clock(IDLE)
                n.up("h_ready", KC)
                feed_forward()
                n.up("sq_ready", KC // 2)
            variance(M)

        @block.scalar
        def _(act):
            at = Place()
            n = at.n

            def split_to(load):
                while at.split < load:
                    m = at.split
                    at.split += 1
                    slot, turn = m % SLOTS, m // SLOTS
                    add = 16 * (turn + 1)
                    act.wait_ge(landed[slot], add if at.turn is None else at.turn * (16 * HALF) + add)
                    if m - SLOTS >= at.tile_done // TILES:
                        act.wait_ge(sems["w_used"], at.value("w_used", m - SLOTS + 1))
                    act.activation(w_hi[:, slot, :], w_raw[:, slot, :], ACT.Copy).then_inc(sems["hi_ready"], 1)

            def arrived(tiles=KC):
                at.tile += tiles
                if tiles:
                    split_to((at.tile - 1) // TILES + SLOTS)
                act.wait_ge(sems["lin_done"], at.up("lin_done"))
                at.tile_done = at.tile
                n.up("lin_evac")
                return at.next_bank()

            def moved(ins):
                ins.then_inc(sems["lin_evac"], 1)
                split_to(at.tile // TILES + SLOTS)

            def step(ins):
                ins.then_inc(sems["act_step"], 1)
                act.wait_ge(sems["act_step"], n.up("act_step"))

            def warm():
                act.activation(small[:, 1, 14:15], c1("alpha")[:, 1:2], ACT.Sqrt)

            def root(b, rows=P, slot=0):
                act.wait_ge(sems["var_done"], at.up("var_done"))
                act.activation(std[0:rows, slot, :], b[0:rows, 0:S], ACT.Sqrt, bias=EPS).then_inc(sems["std_ready"], 1)
                n.up("std_ready")

            def squares(src, dst, ready=None, pieces=range(0, KC, 2)):
                for p in pieces:
                    if ready:
                        act.wait_ge(sems[ready], at.up(ready))
                    act.activation(dst[:, p:p + 2, :], src[:, p:p + 2, :], ACT.Square).then_inc(sems["sq_ready"], 1)
                    n.up("sq_ready")

            def high_parts(shift=None, src=W, ready="t_ready", dst=h_hi):
                for c in range(KC):
                    act.wait_ge(sems[ready], at.up(ready))
                    act.activation(dst[:, c, :], src[:, c, :], ACT.Identity if shift else ACT.Copy,
                                                   bias=shift(c) if shift else 0.0).then_inc(sems["hi_part"], 1)
                    n.up("hi_part")

            def modulated(l, s, shift, before=None):
                warm()
                squares(W, M, "xc_ready")
                root(aux[1])
                if before:
                    before()
                high_parts(lambda c: mod[:, l, shift + c, s:s + 1])

            def squares_behind(x, c, count):
                if c % 2 and c >= 3:
                    act.wait_ge(sems[count[0]], at.value(count[0], count[1] + c - 1))
                    squares(x, M, pieces=(c - 3,))
                if c == KC - 1:
                    act.wait_ge(sems[count[0]], at.value(count[0], count[1] + KC))
                    squares(x, M, pieces=(c - 1,))

            def post(l, x, b, beside=None, squared=False):
                warm()
                squares(W, M, "xc_ready")
                if beside:
                    unit(l, beside[0])
                root(aux[1])
                if beside:
                    unit(l, ("adt", beside[0][1]))
                shifted(l, x, b, squared=squared)
                if beside:
                    unit(l, beside[1])

            def shifted(l, x, b, src=W, squared=False):
                x0 = n.at("x_ready")
                for c in range(KC):
                    act.wait_ge(sems["t_ready"], at.up("t_ready"))
                    act.activation(x[:, c, :], src[:, c, :], ACT.Identity, bias=v1(l, b, c)).then_inc(sems["x_ready"], 1)
                    n.up("x_ready")
                    if squared:
                        squares_behind(x, c, ("x_ready", x0))

            def buffered(c, name):
                if c >= 2:
                    act.wait_ge(sems[name], at.value(name, n.at(name) - KC + c - 1))

            def residual(gate, early=False, fill={}, squared=None):
                r0 = n.at("r_ready")
                n.up("r_ready", KC)
                for c in range(KC):
                    o = arrived()
                    if c >= 2:
                        act.wait_ge(sems["r_ready"], at.value("r_ready", r0 + c - 1))
                    if gate is None:
                        moved(act.activation(gate_buf[:, c % 2, :], o[:, 0:S], ACT.Copy))
                    else:
                        moved(act.activation(gate_buf[:, c % 2, :], o[:, 0:S], ACT.Copy, scale=gate(c)))
                    if squared is not None:
                        squares_behind(squared, c, ("r_ready", r0))
                    if c in fill:
                        unit(0, fill[c])
                    if early and c in (2, 3):
                        if c == 2:
                            warm()
                        squares(Q, M, "xc_ready", range(4 * c - 8, 4 * c - 4, 2))
                    if early and c == 5:
                        root(aux[1])

            def feed_forward(gate, squared=None):
                with act.Fori(0, 2) as i:
                    at.enter(i)
                    if squared is not None:
                        act.wait_ge(sems["sq_ready"], at.value("sq_ready", n.at("sq_ready")))
                    at.bank = 0
                    act.wait_ge(sems["r_ready"], at.value("r_ready", n.at("r_ready")))
                    s0 = n.at("s_ready")
                    n.up("s_ready", HALF)
                    for c in range(HALF):
                        o = arrived()
                        if c >= 2:
                            act.wait_ge(sems["s_ready"], at.value("s_ready", s0 + c - 1))
                        moved(act.activation(gate_buf[:, c % 2, :], o[:, 0:S], ACT.Silu))
                        o = arrived()
                        moved(act.activation(y_buf[:, c % 2, :], o[:, 0:S], ACT.Copy))
                    r0 = n.at("r_ready")
                    n.up("r_ready", KC)
                    for c in range(KC):
                        o = arrived(HALF)
                        if c >= 2:
                            act.wait_ge(sems["r_ready"], at.value("r_ready", r0 + c - 1))
                        if gate is None:
                            moved(act.activation(gate_buf[:, c % 2, :], o[:, 0:S], ACT.Copy))
                        else:
                            moved(act.activation(gate_buf[:, c % 2, :], o[:, 0:S], ACT.Copy, scale=gate(c)))
                        if squared is not None:
                            squares_behind(squared, c, ("r_ready", r0))
                    at.leave()

            def attention(items, scale, p_tile, pt_tile, high, fill, run):
                def soft(j):
                    groups, _, sink, _ = items[j]
                    act.wait_ge(sems["nb_ready"], at.up("nb_ready"))
                    w = 2 * S // groups
                    st = small[:, j % 2, :]
                    if sink is not None:
                        for g in range(groups):
                            act.activation(st[:, 8 + g:9 + g], sink, ACT.Exp, bias=st[:, 2 + g:3 + g])
                    src = aux[j % 2] if scale is not None else w2["scores"][:, j % 2, :]
                    for g in range(groups):
                        ins = act.activation(p_tile[:, j % 2, g * w:(g + 1) * w], src[:, g * w:(g + 1) * w], ACT.Exp,
                                             scale=1.0 if scale is None else scale, bias=st[:, 2 + g:3 + g],
                                             accum_out=st[:, 4 + g:5 + g])
                    ins.then_inc(sems["p_ready"], 1)
                    n.up("p_ready")

                def move_probs(j):
                    act.wait_ge(sems["pt_done"], at.up("pt_done"))
                    act.activation(pt_tile[:, j % 2, :, :], aux[2][:, :].rearrange("p (a b) -> p a b", b=P), ACT.Copy).then_inc(sems["pt_ready"], 1)
                    n.up("pt_ready")

                def move_output(j):
                    groups, place, _, rows = items[j]
                    act.wait_ge(sems["o_done"], at.up("o_done"))
                    act.activation(place, aux[3][rows[0]:rows[1], 0:groups * P], ACT.Copy).then_inc(sems["o_hi" if high else "o_ready"], 1)
                    n.up("o_hi" if high else "o_ready")
                for j in range(len(items) + 3):
                    if 2 <= j < len(items) + 2:
                        move_probs(j - 2)
                    if j < len(items):
                        soft(j)
                    if j == len(items) and not high:
                        warm()
                    if j >= 3:
                        move_output(j - 3)
                    if j < len(items):
                        for u in fill[j]:
                            run(u)
                if high:
                    n.up("o_ready", len(items))

            def ada():
                b = at.n.of.get("ada", 0) % 2
                at.n.up("ada")
                o = arrived(ADA_CHUNKS * KC)
                moved(act.activation(mod_rows[:, b, :], o[0:4, 0:ADA_COLS], ACT.Copy))

            def ada_back(l, group):
                o = arrived(0)
                moved(act.activation(mod[:, l, ADA_CHUNKS * group:ADA_CHUNKS * (group + 1), :], o[:, 0:2 * ADA_CHUNKS].rearrange("p (c s) -> p c s", s=2), ACT.Copy))

            def unit(l, u):
                kind, c = u
                if kind == "kg":
                    moved(act.activation(KG[:, c, :], arrived()[:, 0:S], ACT.Copy))
                elif kind == "qg":
                    moved(act.activation(QG[:, c, :], arrived()[:, 0:S], ACT.Copy, scale=float(GDK) ** -0.5))
                elif kind == "glr":
                    moved(act.activation(glr[0:GLR, :], arrived(0)[0:GLR, 0:S], ACT.Copy))
                elif kind == "vg":
                    for tt in range(QT):
                        o = arrived()
                        moved(act.activation(VG[:, tt, 2 * P * c:2 * P * (c + 1)], o[:, 0:2 * P], ACT.Copy))
                elif kind == "cy":
                    o = arrived()
                    buffered(c, "m_ready") if c else n.up("m_ready", KC)
                    moved(act.activation(y_buf[:, c % 2, :], o[:, 0:S], ACT.Copy))
                elif kind == "r":
                    moved(act.activation(rbuf[:, c, :], arrived()[:, 0:S], ACT.Copy))
                elif kind == "kt":
                    d, kt = divmod(c, QT)
                    moved(act.activation(KT[:, d, kt, :, :], arrived(0)[:, :].rearrange("p (h k) -> p h k", h=GH), ACT.Copy))
                elif kind == "st":
                    d, h = divmod(2 * c, GH)
                    moved(act.activation(state[:, d, h:h + 2, :], arrived(0)[:, :].rearrange("p (h e) -> p h e", h=2), ACT.Copy))
                elif kind == "ada":
                    ada()
                else:
                    ada_back(*c)

            def hat(s, d):
                act.wait_ge(sems["hat_diff"], at.up("hat_diff"))
                act.activation(HAT[:, :, d, :], HAT[:, :, d, :] if s == CTX else B[:, d * GH:(d + 1) * GH, :], ACT.Exp,
                               scale=1.0 / TAU).then_inc(sems["hat_exp"], 1)
                n.up("hat_exp")

            def gla(l, s, full):
                fill = gla_steps(l, s)
                if full:
                    act.wait_ge(sems["s_ready"], at.value("s_ready", n.at("s_ready")))
                for j in range(4):
                    o = arrived(0)
                    for k in range(2):
                        ins = act.activation(Z[:, 2 * j + k, :], o[:, k * S:(k + 1) * S], ACT.Identity,
                                             bias=v1(l, "gla_b_a", 2 * j + k))
                    moved(ins)
                act.wait_ge(sems["lin_evac"], n.at("lin_evac"))
                step(act.activation(B[:, :, :], Z[:, :, :], ACT.Abs))
                unit(l, fill[0][0])
                step(act.activation(B[:, :, :], B[:, :, :], ACT.Exp, scale=-1.0))
                unit(l, fill[0][1])
                for d in range(2):
                    act.activation(B[:, d * GH:(d + 1) * GH, :], B[:, d * GH:(d + 1) * GH, :], ACT.Ln, bias=1.0).then_inc(sems["ln_ready"], 1)
                n.up("ln_ready", 2)
                if full:
                    act.activation(small[:, 1, 14:15], c1("alpha")[:, 1:2], ACT.Exp)
                for u in fill[0][2:]:
                    unit(l, u)
                if full:
                    for j in range(STEPS):
                        if j < STEPS - 1:
                            act.wait_ge(sems["diff_ready"], at.up("diff_ready"))
                            act.activation(DL[:, j % 2], DL[:, j % 2], ACT.Exp, scale=1.0 / TAU).then_inc(sems["lev_exp"], 1)
                            n.up("lev_exp")
                        for u in fill[j + 1]:
                            unit(l, u)
                        if j in (HAT_STEP, HAT_STEP + 1):
                            hat(s, j - HAT_STEP)
                if not full:
                    for d in range(2):
                        hat(s, d)
                    warm()
                    squares(early, M, "xc_ready")
                    for u in STATE_UNITS:
                        if u == ("st", 0):
                            root(aux[1])
                        unit(l, u)
                    return
                warm()
                for h in range(GH):
                    o = arrived(0)
                    moved(act.activation(Q[:, 2 * h:2 * h + 2, :], o[:, :].rearrange("p (c t) -> p c t", c=2), ACT.Copy))
                    act.wait_ge(sems["lin_evac"], n.at("lin_evac"))
                    ins = act.activation(osq[:, 2 * h:2 * h + 2, :], Q[:, 2 * h:2 * h + 2, :], ACT.Square)
                ins.then_inc(sems["sq_ready"], 1)
                n.up("sq_ready")

            act.wait_ge(sems["c_landed"], 16)
            step(act.activation(cvec[:, :, :], cvec[:, :, :], ACT.Silu))
            act.activation(c_hl[:, :, 0:2], cvec[:, :, :], ACT.Copy).then_inc(sems["c_ready"], 1)
            n.up("c_ready")
            split_to(SLOTS)
            act.wait_ge(sems["x_landed"], 2 * 16)

            def first_modulation():
                for u in FIRST_UNITS:
                    unit(0, u)
                act.wait_ge(sems["params"], PARAMS)
                act.activation(wglr_hi[:, :], wglr[:, :], ACT.Copy).then_inc(sems["glr_split"], 1)
            for turn, (l, s) in enumerate(PASSES):
                    full = whole(l, s)
                    x = X[:, :, s * S:(s + 1) * S]
                    if turn == 0:
                        modulated(l, s, 0, first_modulation)
                    else:
                        high_parts(lambda c: mod[:, l, c, s:s + 1], early if turn == 3 else Q, "early_ready")
                    norm_left = turn > 0 and whole(*PASSES[turn - 1])
                    pl, ps = PASSES[turn - 1]
                    before = X[:, :, ps * S:(ps + 1) * S]
                    if full:
                        n.up("y_ready", KC)
                        for c in range(KC):
                            o = arrived()
                            moved(act.activation(YP[:, c, PAD:PAD + S], o[:, 0:S], ACT.Copy))
                            o = arrived()
                            buffered(c, "y_ready")
                            moved(act.activation(gate_buf[:, c % 2, :], o[:, 0:S], ACT.Sigmoid))
                            if norm_left and c == 0:
                                squares(Q, M, "xc_ready")
                            if norm_left and c == 1:
                                root(aux[1])
                            if norm_left and c == 2:
                                shifted(pl, before, "ln2_b", Q)
                    warm()
                    if not full:
                        squares(Q, M, "xc_ready")
                    heads = [K[:, c, s * S:(s + 1) * S] for c in range(KVH)] + [Q[:, c, :] for c in range(HEADS) if full]
                    for c, t in enumerate(heads):
                        moved(act.activation(t, arrived()[:, 0:S], ACT.Copy))
                        act.wait_ge(sems["lin_evac"], at.now("lin_evac"))
                        ins = act.activation(hsq[:, c, :], t, ACT.Square)
                    ins.then_inc(sems["sq_ready"], 1)
                    n.up("sq_ready")
                    for tt in range(QT):
                        o = arrived()
                        moved(act.activation(V[:, s * QT + tt, :], o[:, 0:KVH * DH], ACT.Copy))
                    if not full:
                        root(aux[1])
                        unit(l, ("glr", 0))
                        shifted(pl, before, "ln2_b", Q)
                    root(aux[0], ROWS)
                    for c in range(GH if full else 2):
                        unit(l, ("kg", c))
                    for c in range(GH if full else 0):
                        unit(l, ("qg", c))
                    if full:
                        if s == CTX:
                            items = [(QT, s_hi[:, h, :], None, (0, P)) for h in range(HEADS)]
                        else:
                            items = [(1, s_hi[:, h, qt * P:(qt + 1) * P], None, (0, P)) for h in range(HEADS) for qt in range(QT)]
                        attention(items, float(DH) ** -0.5, probs, probsT, True, returned(spread(attention_fill(l, s), len(items))),
                                  lambda u: unit(l, u))
                        n.up("m_ready", KC)
                        act.wait_ge(sems["y_ready"], n.at("y_ready"))
                        for c in range(KC):
                            o = arrived()
                            buffered(c, "m_ready")
                            moved(act.activation(gate_buf[:, c % 2, :], o[:, 0:S], ACT.Sigmoid))
                            o = arrived()
                            moved(act.activation(y_buf[:, c % 2, :], o[:, 0:S], ACT.Copy))
                            if c < 4:
                                squares(CV, osq, "xc_ready", [2 * c])
                            if c == 4:
                                root(aux[1])
                        for c in range(KC):
                            act.wait_ge(sems["t_ready"], at.up("t_ready"))
                            act.activation(osq[:, c, :], CV[:, c, :], ACT.Sigmoid, bias=v1(l, "conv_ln_b", c)
                                           ).then_inc(sems["sigmoid_ready"], 1)
                            n.up("sigmoid_ready")
                            moved(act.activation(Q[:, c, :], arrived()[:, 0:S], ACT.Sigmoid))
                        n.up("s_ready", KC)
                    gla(l, s, full)
                    if not full:
                        continue
                    root(aux[0], ROWS)
                    if s == CTX:
                        for c in range(KC):
                            unit(l, ("r", c))
                    act.wait_ge(sems["lin_evac"], n.at("lin_evac"))
                    act.activation(rbuf[:, :, :], rbuf[:, :, :], ACT.Silu).then_inc(sems["silu_ready"], 1)
                    for c in range(KC):
                        moved(act.activation(gbuf[:, c, :], arrived()[:, 0:S], ACT.Sigmoid))
                    n.up("s_ready", KC)
                    n.up("m_ready", KC)
                    for c in range(KC):
                        o = arrived()
                        buffered(c, "m_ready")
                        moved(act.activation(y_buf[:, c % 2, :], o[:, 0:S], ACT.Copy))
                    act.wait_ge(sems["m_ready"], n.at("m_ready"))
                    residual(lambda c: mod[:, l, 16 + c, s:s + 1], turn < 2, out_fill(l, s))
                    if l == DEPTH - 1:
                        act.wait_ge(sems["r_ready"], n.at("r_ready"))
                        act.dma_start(const2, const2_in).then_inc(sems["b2_landed"], 16)
                        act.dma_start(small2, small2_in).then_inc(sems["b2_landed"], 16)
                    beside = norm_fill(l, s)
                    post(l, x, "ln1_b", beside)
                    modulated(l, s, 24, lambda: unit(l, ("adt", beside[1][1])))
                    feed_forward(lambda c: mod[:, l, 40 + c, s:s + 1])
                    if turn == 3:
                        post(l, x, "ln2_b", squared=True)

            x = X[:, :, S:2 * S]

            def rms():
                warm()
                root(aux[1])

            act.wait_ge(sems["b2_landed"], 32)
            for l in range(DEPTH):
                rms()
                high_parts()

                def move(dst, rows=(0, P), scale=1.0, tiles=KC):
                    o = arrived(tiles)
                    src = o[rows[0]:rows[1], 0:dst.free_size()]
                    if len(dst.shape) == 3:
                        src = src.rearrange("p (a b) -> p a b", a=dst.shape[1])
                    moved(act.activation(dst, src, ACT.Copy, scale=scale))
                for c in range(2):
                    move(w2["cq"][:, c, :])
                move(w2["ckv"][:, 0, :])
                move(w2["kr"][NOPE:QK, 0, :], (NOPE, QK))
                act.wait_ge(sems["lin_evac"], n.at("lin_evac"))
                act.wait_ge(sems["r_ready"], n.at("r_ready"))
                act.activation(gate_buf[:, :, :], w2["cq"][:, :, :], ACT.Square).then_inc(sems["sq_ready"], 1)
                n.up("sq_ready")
                act.activation(y_buf[:, 0, :], w2["ckv"][:, 0, :], ACT.Square).then_inc(sems["sq_ready"], 1)
                n.up("sq_ready")
                move(w2["vf"])
                for name in ("uc", "gc", "gb"):
                    for c in range(2):
                        move(w2[name][:, c, :])
                    if name == "uc":
                        move(w2["up"][:, 0, 16:])
                        root(aux[0], slot=0)
                        root(aux[1], slot=1)
                        move(w2["up"][:, 1, 16:])
                for c in range(2):
                    move(w2["qs"][:, c, :])
                move(w2["ks"][:, 0, :])
                for h in range(MH):
                    move(w2["qh"][0:QK, h, :], (0, QK), tiles=0)
                for h in range(MH):
                    move(w2["kh"][0:NOPE, h, :], (0, NOPE), tiles=0)
                move(w2["vm"][:, :, :], tiles=0)
                move(w2["vs"][:, :, :], tiles=0)
                for c in range(2):
                    move(w2["mx"][:, 4 + c, :], scale=v2(l, "pool_scale", c), tiles=0)
                act.wait_ge(sems["yb_ready"], l + 1)
                act.wait_ge(sems["lin_evac"], n.at("lin_evac"))
                squares(w2["mx"], M, pieces=(2, 4))
                items = []
                for h in range(MH):
                    r = 64 * (h % 2)
                    items.append((QT, w2["mx"][r:r + 64, h // 2, :], None, (r, r + 64)))
                for h in range(SH):
                    r = 64 * (h % 2)
                    items.append((QT, w2["mx"][r:r + 64, 6 + h // 2, :], v2(l, "sinks", h), (r, r + 64)))
                attention(items, None, w2["probs"], w2["probsT"], False, [[]] * len(items), None)
                act.wait_ge(sems["yb_ready"], l + 1)
                act.wait_ge(sems["o_ready"], n.at("o_ready"))
                squares(w2["mx"], M, pieces=(0, 6))
                root(aux[0], ROWS)
                high_parts(src=w2["mx"], dst=s_hi)
                n.up("s_ready", KC)
                residual(None, squared=x)
                rms()
                high_parts()
                feed_forward(None, squared=x)
            rms()
            at.tile_done = LOADS * TILES
            split_to(LOADS)

        @block.vector
        def _(dve):
            at = Place()
            n = at.n

            def step(ins):
                ins.then_inc(sems["dve_step"], 1)
                dve.wait_ge(sems["dve_step"], at.up("dve_step"))

            def over(t, k):
                return t.unsqueeze(1).broadcast_to([t.shape[0], k, t.shape[1]])

            def inverse(b, rows=P, slot=0, name="dve_step"):
                dve.wait_ge(sems["std_ready"], at.up("std_ready"))
                r, t, v = rstd[0:rows, :], tmp[0:rows, :], b[0:rows, 0:S]
                step(dve.reciprocal(r, std[0:rows, slot, :]))
                step(dve.scalar_tensor_tensor(t, v, EPS, r, ALU.add, ALU.mult))
                step(dve.scalar_tensor_tensor(t, t, -0.5, r, ALU.mult, ALU.mult))
                dve.scalar_tensor_tensor(r, t, 1.5, r, ALU.add, ALU.mult).then_inc(sems[name], 1)
                n.up(name)
                dve.wait_ge(sems[name], at.now(name))

            def centre(src, dst):
                dve.wait_ge(sems["mean_done"], at.up("mean_done"))
                for p in range(0, KC, 2):
                    dve.tensor_tensor(dst[:, p:p + 2, :], src[:, p:p + 2, :], over(aux[0][:, 0:S], 2), ALU.subtract).then_inc(sems["xc_ready"], 1)
                    n.up("xc_ready")

            def scale_chunk(src, g, c, dst=W, name="t_ready"):
                dve.scalar_tensor_tensor(dst[:, c, :], src[:, c, :], g(c), rstd[:, :], ALU.mult, ALU.mult).then_inc(sems[name], 1)
                n.up(name)

            def low_part(c, shift, src=W, high=h_hi, lo=h_lo, name="h_ready"):
                dve.wait_ge(sems["hi_part"], at.up("hi_part"))
                hi = high[:, c, :].bitcast(F32)
                if shift:
                    dve.scalar_tensor_tensor(lo[:, c, :], src[:, c, :], shift(c), hi, ALU.add, ALU.subtract).then_inc(sems[name], 1)
                    n.up(name)
                else:
                    dve.tensor_tensor(lo[:, c, :], src[:, c, :], hi, ALU.subtract).then_inc(sems[name], 1)
                    n.up(name)

            def to_h(src, g, shift):
                for c in range(KC):
                    scale_chunk(src, g, c)
                    if c >= 1:
                        low_part(c - 1, shift)
                low_part(KC - 1, shift)

            def modulated(l, x, s, shift, scale, before=None):
                centre(x, W)
                inverse(aux[1])
                if before:
                    before()
                dve.wait_ge(sems["xc_ready"], at.now("xc_ready"))
                to_h(W, lambda c: mod[:, l, scale + c, s:s + 1], lambda c: mod[:, l, shift + c, s:s + 1])

            def scaled(buf, g, name="t_ready", inverted=False):
                if not inverted:
                    inverse(aux[1])
                dve.wait_ge(sems["xc_ready"], at.now("xc_ready"))
                for c in range(KC):
                    scale_chunk(buf, g, c, buf, name)

            def post(l, x, g, beside=None):
                centre(x, W)
                if beside:
                    beside()
                    dve.wait_ge(sems["early_ready"], at.now("early_ready"))
                scaled(W, lambda c: v1(l, g, c))
                dve.wait_ge(sems["x_ready"], at.up("x_ready", KC))

            def both_parts(hi, lo, y, name):
                step(dve.tensor_copy(hi, y))
                dve.tensor_tensor(lo, y, hi.bitcast(F32), ALU.subtract).then_inc(sems[name], 1)
                n.up(name)

            def merge_chunk(c, gate, first=False):
                if first:
                    dve.tensor_tensor(M[:, c, :], gate, y_buf[:, c % 2, :], ALU.mult).then_inc(sems["m_ready"], 1)
                    n.up("m_ready")
                else:
                    step(dve.tensor_tensor(y_buf[:, c % 2, :], gate, y_buf[:, c % 2, :], ALU.mult))
                    dve.tensor_tensor(M[:, c, :], M[:, c, :], y_buf[:, c % 2, :], ALU.add).then_inc(sems["m_ready"], 1)
                    n.up("m_ready")

            def residual(x, alpha, means, early=None):
                for c in range(KC):
                    dve.wait_ge(sems["lin_evac"], at.up("lin_evac"))
                    dve.scalar_tensor_tensor(x[:, c, :], x[:, c, :], alpha, gate_buf[:, c % 2, :], ALU.mult, ALU.add
                                             ).then_inc(sems["r_ready"], 1)
                    n.up("r_ready")
                    if means and c >= 1:
                        dve.wait_ge(sems["r_ready"], at.now("r_ready"))
                        ins = dve.tensor_tensor(std[:, 1, :], std[:, 1, :] if c > 1 else x[:, 0, :], x[:, c, :], ALU.add)
                        if c < KC - 1:
                            step(ins)
                        else:
                            ins.then_inc(sems["sum_ready"], 1)
                            n.up("sum_ready")
                    if early:
                        early(c)

            def feed_forward(x, scaled):
                a, _ = CONST1["alpha"]
                with dve.Fori(0, 2) as i:
                    at.enter(i, dve_step=2 * HALF + (KC - 2) * scaled)
                    for c in range(HALF):
                        dve.wait_ge(sems["lin_evac"], at.up("lin_evac", 2))
                        y = y_buf[:, c % 2, :]
                        step(dve.tensor_tensor(y, gate_buf[:, c % 2, :], y, ALU.mult))
                        both_parts(s_hi[:, c, :], s_lo[:, c, :], y, "s_ready")
                    dve.wait_ge(sems["r_ready"], at.now("r_ready"))
                    residual(x, const1[:, bass.ds(i + a, 1)] if scaled else 1.0, scaled)
                    at.leave()
                dve.wait_ge(sems["r_ready"], at.now("r_ready"))

            PARTS = 6
            CONV_PIECES, PIECE = KC // 2 * PARTS, (TAPS - 1) // PARTS

            def convolve(l, piece, y0):
                q, part = divmod(piece, PARTS)
                if part == 0:
                    dve.wait_ge(sems["y_ready"], y0 + 2 * q + 2)
                    for c in (2 * q, 2 * q + 1):
                        dve.tensor_scalar(CV[:, c, :], YP[:, c, 0:S], v1(l, "conv_w", c * TAPS), v1(l, "conv_b", c),
                                          ALU.mult, ALU.add).then_inc(sems["dve_step"], 1)
                        n.up("dve_step")
                for tap in range(1 + part * PIECE, 1 + (part + 1) * PIECE):
                    for c in (2 * q, 2 * q + 1):
                        dve.wait_ge(sems["dve_step"], n.at("dve_step") - 1)
                        dve.scalar_tensor_tensor(CV[:, c, :], YP[:, c, tap:tap + S], v1(l, "conv_w", c * TAPS + tap), CV[:, c, :],
                                                 ALU.mult, ALU.add).then_inc(sems["dve_step"], 1)
                        n.up("dve_step")

            def attention(items, scale, p_tile, high, fill, run):
                def top(j):
                    groups, bias, sink, qk_scale, _ = items[j]
                    dve.wait_ge(sems["s_done"], at.up("s_done"))
                    st = small[:, j % 2, :]
                    src = aux[j % 2][:, :]
                    if scale is None:
                        src = w2["scores"][:, j % 2, :]
                        step(dve.scalar_tensor_tensor(src, aux[j % 2][:, :], qk_scale, bias, ALU.mult, ALU.add))
                    step(dve.reduce_max(st[:, 0:groups], src.rearrange("p (g k) -> p g k", g=groups), AXX))
                    if sink is not None:
                        dve.tensor_scalar(st[:, 2:2 + groups], st[:, 0:groups], sink, -1.0, ALU.max, ALU.mult).then_inc(sems["nb_ready"], 1)
                        n.up("nb_ready")
                    else:
                        dve.tensor_scalar(st[:, 2:2 + groups], st[:, 0:groups], -1.0 if scale is None else -scale, None, ALU.mult).then_inc(sems["nb_ready"], 1)
                        n.up("nb_ready")

                def normalise(j):
                    groups, _, sink, _, _ = items[j]
                    dve.wait_ge(sems["p_ready"], at.up("p_ready"))
                    w = 2 * S // groups
                    st = small[:, j % 2, :]
                    if sink is not None:
                        step(dve.tensor_tensor(st[:, 4:4 + groups], st[:, 4:4 + groups], st[:, 8:8 + groups], ALU.add))
                    step(dve.reciprocal(st[:, 6:6 + groups], st[:, 4:4 + groups]))
                    for g in range(groups):
                        p = p_tile[:, j % 2, g * w:(g + 1) * w]
                        ins = dve.tensor_scalar(p, p, st[:, 6 + g:7 + g], None, ALU.mult)
                    ins.then_inc(sems["pn_ready"], 1)
                    n.up("pn_ready")

                def low(j):
                    groups, _, _, _, (hi, lo) = items[j]
                    dve.wait_ge(sems["o_hi"], at.up("o_hi"))
                    dve.tensor_tensor(lo, aux[3][:, 0:groups * P], hi.bitcast(F32), ALU.subtract).then_inc(sems["o_ready"], 1)
                    n.up("o_ready")
                for j in range(len(items) + 3):
                    if j < len(items):
                        top(j)
                    if 1 <= j < len(items) + 1:
                        normalise(j - 1)
                    if high and j >= 3:
                        low(j - 3)
                    if j < len(items):
                        for u in fill[j]:
                            run(u)

            pending = []

            def modulation():
                for l, g, chunk in pending:
                    dve.wait_ge(sems["lin_evac"], chunk)
                    c = ADA_CHUNKS * g
                    m = mod[:, l, c:c + ADA_CHUNKS, :]
                    b = vec1[:, l, VEC1["b_ada"][0] + c:VEC1["b_ada"][0] + c + ADA_CHUNKS].unsqueeze(2).broadcast_to([P, ADA_CHUNKS, 2])
                    one = 1.0 if c // KC in (1, 4) else 0.0
                    step(dve.scalar_tensor_tensor(m, m, one, b, ALU.add, ALU.add))
                pending.clear()

            def unit(l, u, y0=None):
                kind, c = u
                if kind == "conv":
                    convolve(l, c, y0)
                elif kind == "cy":
                    dve.wait_ge(sems["lin_evac"], at.up("lin_evac"))
                    merge_chunk(c, Q[:, c, :])
                else:
                    n.up("lin_evac", 2 if kind == "vg" else 1)
                    if kind == "adt":
                        pending.append((c[0], c[1], n.at("lin_evac")))

            def hat_differences(s, d):
                if s == CTX:
                    a = S - 1 if d == 0 else 0
                    b = B[:, d * GH:(d + 1) * GH, :]
                    ins = dve.tensor_tensor(HAT[:, :, d, :], b[:, :, a:a + 1].broadcast_to([P, GH, S]), b, ALU.subtract)
                else:
                    ins = dve.tensor_copy(small[:, 0, 13 + d:14 + d], B[:, 0, 0:1])
                ins.then_inc(sems["hat_diff"], 1)
                n.up("hat_diff")

            def hat_product(s, d):
                dve.wait_ge(sems["hat_exp"], at.up("hat_exp"))
                dve.tensor_tensor(HAT[:, :, d, :], HAT[:, :, d, :], KG if s == CTX else QG, ALU.mult).then_inc(sems["hat_ready"], 1)
                n.up("hat_ready")

            def gla(l, s, full):
                fill = gla_steps(l, s)
                dve.wait_ge(sems["lin_evac"], at.up("lin_evac", 4))
                for u in fill[0][:2]:
                    unit(l, u)
                for d in range(2):
                    dve.wait_ge(sems["ln_ready"], at.up("ln_ready"))
                    zd = Z[:, d * GH:(d + 1) * GH, :]
                    step(dve.scalar_tensor_tensor(zd, zd, 0.0, B[:, d * GH:(d + 1) * GH, :], ALU.min, ALU.subtract))
                    for h in range(GH):
                        src, dst = Z[:, d * GH + h, :], B[:, d * GH + h, :]
                        if d == 1:
                            src, dst = src[:, ::-1], dst[:, ::-1]
                        ins = dve.tensor_tensor_scan(dst, src, src, 0.0, ALU.add, ALU.bypass)
                step(ins)
                if full:
                    g0 = n.at("gram_done")

                    def halves(t, half):
                        v = t.rearrange("p h (b two e) -> p (h b) two e", two=2, e=half)
                        return v[:, :, 0, :], v[:, :, 1, :]

                    def differences(j):
                        half, d = LEVELS[j // 2], j % 2
                        if j >= 2:
                            dve.wait_ge(sems["gram_done"], g0 + j - 1)
                        left, right = halves(B[:, d * GH:(d + 1) * GH, :], half)
                        dl, dr = halves(DL[:, j % 2], half)
                        blocks = left.shape[1]
                        if d == 0:
                            mid = left[:, :, half - 1:half].broadcast_to([P, blocks, half])
                            dve.tensor_tensor(dr, right, mid, ALU.subtract)
                            dve.tensor_tensor(dl, mid, left, ALU.subtract).then_inc(sems["diff_ready"], 1)
                            n.up("diff_ready")
                        else:
                            mid = right[:, :, 0:1].broadcast_to([P, blocks, half])
                            dve.tensor_tensor(dl, left, mid, ALU.subtract)
                            dve.tensor_tensor(dr, mid, right, ALU.subtract).then_inc(sems["diff_ready"], 1)
                            n.up("diff_ready")

                    def decay(j):
                        half, d = LEVELS[j // 2], j % 2
                        dve.wait_ge(sems["lev_exp"], at.up("lev_exp"))
                        dl, dr = halves(DL[:, j % 2], half)
                        ql, qr = halves(QG, half)
                        kl, kr = halves(KG, half)
                        dve.tensor_tensor(dl, dl, kl if d == 0 else ql, ALU.mult)
                        dve.tensor_tensor(dr, dr, qr if d == 0 else kr, ALU.mult).then_inc(sems["lev_ready"], 1)
                        n.up("lev_ready")

                    def place(j):
                        pair = [aux[2 * (j % 2)], aux[2 * (j % 2) + 1]]
                        dve.wait_ge(sems["gram_done"], g0 + j + 1)
                        if j < 2:
                            kt, qs = (0, P) if j == 0 else (1, 0)
                            dve.tensor_copy(A[:, :, kt, qs:qs + P], pair[0][:, :].rearrange("p (h q) -> p h q", h=GH)).then_inc(sems["a_copied"], 1)
                            n.up("a_copied")
                            return
                        dve.wait_ge(sems["a_copied"], at.now("a_copied"))
                        for kt in range(QT):
                            ins = dve.copy_predicated(A[:, :, kt, kt * P:(kt + 1) * P], over(masks[:, j - 2, :], GH),
                                                      pair[kt][:, :].rearrange("p (h q) -> p h q", h=GH))
                        ins.then_inc(sems["a_copied"], 1)
                        n.up("a_copied")
                    for j in range(STEPS):
                        if j >= 1:
                            decay(j - 1)
                        if j < STEPS - 1:
                            differences(j)
                        if j >= 2:
                            place(j - 2)
                        for u in fill[j] if j else fill[0][2:]:
                            unit(l, u)
                        if j in (HAT_STEP, HAT_STEP + 1):
                            hat_differences(s, j - HAT_STEP)
                        if j in (HAT_STEP + 2, HAT_STEP + 3):
                            hat_product(s, j - HAT_STEP - 2)
                    for u in fill[STEPS]:
                        unit(l, u)
                    place(STEPS - 2)
                    place(STEPS - 1)
                    n.up("gram_done", STEPS)
                else:
                    for u in fill[0][2:]:
                        unit(l, u)
                    dve.wait_ge(sems["x_ready"], n.at("x_ready"))
                    for d in range(2):
                        hat_differences(s, d)
                    for d in range(2):
                        hat_product(s, d)
                    centre(X[:, :, S:2 * S], early)
                    scaled(early, lambda k: mod[:, l, 8 + k, LAT:LAT + 1], "early_ready")
                modulation()
                n.up("lin_evac", GH if full else len(STATE_UNITS))

            dve.wait_ge(sems["c_ready"], at.up("c_ready"))
            dve.tensor_tensor(c_hl[:, :, 2:4], cvec[:, :, :], c_hl[:, :, 0:2].bitcast(F32), ALU.subtract).then_inc(sems["c_ready"], 1)
            n.up("c_ready")

            def first_modulation():
                dve.wait_ge(sems["params"], PARAMS)
                step(dve.tensor_copy(masks[:, :, :], view(arena2, pt_at, N_MASK, P)))
                for u in FIRST_UNITS:
                    unit(0, u)
                modulation()
                dve.wait_ge(sems["glr_split"], at.up("glr_split"))
                dve.tensor_tensor(wglr_lo[:, :], wglr[:, :], wglr_hi[:, :].bitcast(F32), ALU.subtract).then_inc(sems["glr_split"], 1)
            for turn, (l, s) in enumerate(PASSES):
                    full = whole(l, s)
                    x = X[:, :, s * S:(s + 1) * S]
                    if turn == 0:
                        modulated(l, x, s, 0, 8, first_modulation)
                    else:
                        for c in range(KC):
                            low_part(c, lambda c: mod[:, l, c, s:s + 1], early if turn == 3 else Q)
                    norm_left = turn > 0 and whole(*PASSES[turn - 1])
                    pl, ps = PASSES[turn - 1]
                    before = X[:, :, ps * S:(ps + 1) * S]
                    if not full:
                        centre(before, Q)
                        scaled(Q, lambda c: v1(pl, "ln2_g", c))
                        n.up("x_ready", KC)
                    if full:
                        dve.memset(YP[:, :, 0:PAD], 0.0)
                        step(dve.memset(YP[:, :, PAD + S:2 * PAD + S], 0.0))
                        y0, piece = n.at("y_ready"), 0
                        for c in range(KC):
                            dve.wait_ge(sems["lin_evac"], at.up("lin_evac", 2))
                            y = YP[:, c, PAD:PAD + S]
                            dve.tensor_tensor(y, y, gate_buf[:, c % 2, :], ALU.mult).then_inc(sems["y_ready"], 1)
                            n.up("y_ready")
                            if norm_left and c == 0:
                                centre(before, Q)
                            if norm_left and c == 2:
                                scaled(Q, lambda c: v1(pl, "ln2_g", c))
                                n.up("x_ready", KC)
                            for _ in range(1 + c % 2 if c else 0):
                                convolve(l, piece, y0)
                                piece += 1
                        for _ in range(6):
                            convolve(l, piece, y0)
                            piece += 1
                    n.up("lin_evac", KVH + QT + (HEADS if full else 1))
                    inverse(aux[0], ROWS, name="row_ready")
                    heads = [(K[:, c, s * S:(s + 1) * S], "k_norm") for c in range(KVH)]
                    heads += [(Q[:, c, :], "q_norm") for c in range(HEADS) if full]
                    base = n.at("qk_normed")

                    def normed(j):
                        t, name = heads[j]
                        dve.wait_ge(sems["spread_done"], at.up("spread_done"))
                        dve.scalar_tensor_tensor(t, t, v1(l, name), aux[1 + j % 2][:, 0:S], ALU.mult, ALU.mult).then_inc(sems["qk_normed"], 1)
                        n.up("qk_normed")

                    def rotated(j):
                        t, _ = heads[j]
                        dve.wait_ge(sems["rot_done"], at.up("rot_done"))
                        dve.wait_ge(sems["qk_normed"], base + j + 1)
                        step(dve.tensor_tensor(t, t, c1("cos"), ALU.mult))
                        step(dve.tensor_tensor(tmp[:, :], aux[3 * (j % 2)][:, 0:S], c1("sin"), ALU.mult))
                        dve.tensor_tensor(t, t, tmp[:, :], ALU.add).then_inc(sems["qk_ready"], 1)
                        n.up("qk_ready")
                        dve.wait_ge(sems["qk_ready"], at.now("qk_ready"))
                    for j in range(len(heads)):
                        normed(j)
                        if s == LAT and j >= 1:
                            rotated(j - 1)
                    if s == LAT:
                        rotated(len(heads) - 1)
                    n.up("lin_evac", 2 * GH if full else 2)
                    if full:
                        if s == CTX:
                            items = [(QT, None, None, None, (s_hi[:, h, :], s_lo[:, h, :])) for h in range(HEADS)]
                        else:
                            items = [(1, None, None, None, (s_hi[:, h, qt * P:(qt + 1) * P], s_lo[:, h, qt * P:(qt + 1) * P]))
                                     for h in range(HEADS) for qt in range(QT)]
                        fill = returned(spread(attention_fill(l, s), len(items)))
                        pieces = spread([("conv", p) for p in range(piece, CONV_PIECES)], len(items))
                        attention(items, float(DH) ** -0.5, probs, True, [f + p for f, p in zip(fill, pieces)], lambda u: unit(l, u, y0))
                        dve.wait_ge(sems["dve_step"], at.now("dve_step"))
                        dve.tensor_copy(small[:, 0, 15:16], CV[:, 0, 0:1]).then_inc(sems["conv_done"], 1)
                        modulation()
                        centre(CV, CV)
                        for c in range(KC):
                            dve.wait_ge(sems["lin_evac"], at.up("lin_evac", 2))
                            merge_chunk(c, gate_buf[:, c % 2, :], first=True)
                            if c == 4:
                                inverse(aux[1])
                                dve.wait_ge(sems["xc_ready"], at.now("xc_ready"))
                                for k in range(KC):
                                    scale_chunk(CV, lambda k: v1(l, "conv_ln_g", k), k)
                        n.up("lin_evac", KC)
                        for c in range(KC):
                            dve.wait_ge(sems["sigmoid_ready"], at.up("sigmoid_ready"))
                            y = CV[:, c, :]
                            step(dve.scalar_tensor_tensor(y, y, v1(l, "conv_ln_b", c), osq[:, c, :], ALU.add, ALU.mult))
                            both_parts(s_hi[:, c, :], s_lo[:, c, :], y, "s_ready")
                    gla(l, s, full)
                    if not full:
                        continue
                    inverse(aux[0], ROWS, name="row_ready")
                    dve.wait_ge(sems["spread_done"], at.up("spread_done", 2))
                    if s == CTX:
                        n.up("lin_evac", KC)
                    for c in range(KC):
                        h, y = c // 2, Q[:, c, :]
                        if c == 0:
                            silu_at = at.up("silu_ready")
                        step(dve.scalar_tensor_tensor(y, y, v1(l, "gla_norm", c % 2), aux[1 + h // 2][:, h % 2 * S:h % 2 * S + S],
                                                      ALU.mult, ALU.mult))
                        if c == 0:
                            dve.wait_ge(sems["silu_ready"], silu_at)
                        step(dve.tensor_tensor(y, y, rbuf[:, c, :], ALU.mult))
                        both_parts(s_hi[:, c, :], s_lo[:, c, :], y, "s_ready")
                    n.up("lin_evac", KC)
                    for c in range(KC):
                        dve.wait_ge(sems["lin_evac"], at.up("lin_evac"))
                        merge_chunk(c, gbuf[:, c, :])
                        dve.wait_ge(sems["m_ready"], at.now("m_ready"))
                        both_parts(h_hi[:, c, :], h_lo[:, c, :], M[:, c, :], "h_ready")
                    if turn < 2:
                        nl, ns = PASSES[turn + 1]

                        def early_norm(c):
                            if c in out_fill(l, s):
                                unit(l, out_fill(l, s)[c])
                            if c == 1:
                                centre(X[:, :, ns * S:(ns + 1) * S], Q)
                            if c == 5:
                                inverse(aux[1])
                        residual(x, ALPHA, True, early_norm)
                        post(l, x, "ln1_g", lambda: scaled(Q, lambda k: mod[:, nl, 8 + k, ns:ns + 1], "early_ready", True))
                    else:
                        residual(x, ALPHA, True)
                        post(l, x, "ln1_g")
                    modulated(l, x, s, 24, 32)
                    for u in returned([norm_fill(l, s)])[0]:
                        unit(l, u)
                    modulation()
                    feed_forward(x, True)
                    if turn == 3:
                        post(l, x, "ln2_g")

            x = X[:, :, S:2 * S]
            dve.wait_ge(sems["b2_landed"], 32)

            def rms(g):
                inverse(aux[1])
                to_h(x, g, None)
            for l in range(DEPTH):
                rms(lambda c: v2(l, "attn_norm", c))
                dve.memset(w2["zp"][:, :, 0:2], 0.0)
                step(dve.memset(w2["up"][:, :, 0:16], 0.0))
                inverse(aux[0], slot=0)
                for c in range(2):
                    ins = dve.scalar_tensor_tensor(w2["cq"][:, c, :], w2["cq"][:, c, :], v2(l, "q_norm", c), rstd[:, :], ALU.mult, ALU.mult)
                ins.then_inc(sems["qk_normed"], 1)
                n.up("qk_normed")
                dve.wait_ge(sems["qk_normed"], at.now("qk_normed"))
                inverse(aux[1], slot=1)
                dve.scalar_tensor_tensor(w2["ckv"][:, 0, :], w2["ckv"][:, 0, :], v2(l, "kv_norm"), rstd[:, :], ALU.mult, ALU.mult).then_inc(sems["qk_normed"], 1)
                n.up("qk_normed")
                dve.wait_ge(sems["lin_evac"], at.up("lin_evac", 9))
                prev, e = w2["up"], 16 + S
                for i, window in enumerate(POOLS):
                    cur = w2[f"p{window}"]
                    lo, sh = window - 1, window // 2
                    step(dve.tensor_tensor(cur[:, :, lo:e], prev[:, :, lo:e], prev[:, :, lo - sh:e - sh], ALU.add))
                    prev = cur
                ic = c2("inv_count").rearrange("p (c t) -> p c t", c=2)
                for i, window in enumerate(POOLS):
                    c, r = i // 2, 64 * (i % 2)
                    ins = dve.tensor_tensor(w2["pooled"][r:r + 64, c, :], w2[f"p{window}"][r:r + 64, c, 16:], ic[r:r + 64, c, :], ALU.mult)
                step(ins)
                dve.tensor_tensor(w2["pooled"][:, :, :], w2["pooled"][:, :, :], w2["up"][:, :, 16:], ALU.subtract).then_inc(sems["pooled_ready"], 1)
                n.up("pooled_ready")
                dve.wait_ge(sems["lin_evac"], at.up("lin_evac", 4))
                step(dve.tensor_tensor(w2["zp"][:, :, 2:], w2["gc"][:, :, :], w2["uc"][:, :, :], ALU.mult))
                for c in range(2):
                    y = w2["uc"][:, c, :]
                    step(dve.tensor_scalar(y, w2["zp"][:, c, 0:S], v2(l, "conv_w", c), None, ALU.mult))
                    for t in (1, 2):
                        step(dve.scalar_tensor_tensor(y, w2["zp"][:, c, t:t + S], v2(l, "conv_w", 2 * t + c), y, ALU.mult, ALU.add))
                dve.tensor_tensor(w2["mx"][:, 2:4, :], w2["uc"][:, :, :], w2["gb"][:, :, :], ALU.mult).then_inc(sems["yb_ready"], 1)
                n.up("yb_ready")
                cos, sin = c2("cos"), c2("sin")
                dve.wait_ge(sems["lin_evac"], at.up("lin_evac", 3 + 2 * MH + 2))
                dve.wait_ge(sems["rot_done"], at.up("rot_done"))
                kr = w2["kr"][NOPE:QK, 0, :]
                step(dve.tensor_tensor(kr, kr, cos[NOPE:QK, :], ALU.mult))
                step(dve.tensor_tensor(tmp[NOPE:QK, :], aux[2][NOPE:QK, 0:S], sin[NOPE:QK, :], ALU.mult))
                dve.tensor_tensor(w2["kh"][NOPE:QK, :, :], over(kr, MH), over(tmp[NOPE:QK, :], MH), ALU.add).then_inc(sems["qk_ready"], 1)
                n.up("qk_ready")
                dve.wait_ge(sems["qk_ready"], at.now("qk_ready"))
                for h in range(MH):
                    dve.wait_ge(sems["rot_done"], at.up("rot_done"))
                    q, t = w2["qh"][0:QK, h, :], tmp[0:QK, :]
                    step(dve.tensor_tensor(q, q, cos[0:QK, :], ALU.mult))
                    step(dve.tensor_tensor(t, aux[2 + (h + 1) % 2][0:QK, 0:S], sin[0:QK, :], ALU.mult))
                    dve.tensor_tensor(q, q, t, ALU.add).then_inc(sems["qk_ready"], 1)
                    n.up("qk_ready")
                    dve.wait_ge(sems["qk_ready"], at.now("qk_ready"))
                n.up("lin_evac", 2)
                items = []
                causal = c2("causal")
                window = c2("window").rearrange("p (h k) -> p h k", h=SH)
                for h in range(MH):
                    items.append((QT, causal, None, float(QK) ** -0.5, None))
                for h in range(SH):
                    items.append((QT, window[:, h, :], v2(l, "sinks", h), float(SHD) ** -0.5, None))
                attention(items, None, w2["probs"], False, [[]] * len(items), None)
                dve.wait_ge(sems["yb_ready"], at.now("yb_ready"))
                inverse(aux[0], ROWS, name="row_ready")
                dve.wait_ge(sems["spread_done"], at.up("spread_done", 2))
                for c in range(KC):
                    g, y = c // 2, w2["mx"][:, c, :]
                    dve.scalar_tensor_tensor(y, y, v2(l, "mix_norm", c), aux[1 + g // 2][:, g % 2 * S:g % 2 * S + S],
                                             ALU.mult, ALU.mult).then_inc(sems["t_ready"], 1)
                    n.up("t_ready")
                    if c >= 1:
                        low_part(c - 1, None, w2["mx"], s_hi, s_lo, "s_ready")
                low_part(KC - 1, None, w2["mx"], s_hi, s_lo, "s_ready")
                residual(x, 1.0, False)
                dve.wait_ge(sems["r_ready"], at.now("r_ready"))
                rms(lambda c: v2(l, "ffn_norm", c))
                feed_forward(x, False)
            inverse(aux[1])
            for c in range(KC):
                g = vec2[:, DEPTH * N_VEC2 + c:DEPTH * N_VEC2 + c + 1]
                ins = dve.scalar_tensor_tensor(W[:, c, :], x[:, c, :], g, rstd[:, :], ALU.mult, ALU.mult)
            ins.then_inc(sems["fin_ready"], 1)
            n.up("fin_ready")


def tiles(w):
    k, m = w.shape
    return w.reshape(k // P, P, m // P, P).transpose(2, 0, 1, 3)


def token_tiles(w):
    k, m = w.shape
    return w.reshape(k // P, P, m // P, P).transpose(0, 2, 1, 3).reshape(-1, P, P)


def paired(a, b):
    return np.stack([tiles(a), tiles(b)], 1)


def wide_tiles(w):
    return [token_tiles(w[:, g * ADA_COLS:(g + 1) * ADA_COLS]) for g in range(ADA_GROUPS)]


def half_tiles(gate, up, down):
    both, parts, cut = paired(gate, up), [], HALF * P
    for i in range(2):
        parts += [both[i * HALF:(i + 1) * HALF], tiles(down[i * cut:(i + 1) * cut])]
    return parts


def first_stack_tiles(layers):
    ada = [wide_tiles(w["w_ada"]) for w in layers]
    parts = ada[0][:ADA_FIRST]
    none = np.zeros((2 * GH, 0, P, P), np.float32)
    for l, w in enumerate(layers):
        k, v, kg, vg, _, q, qg, r, ca, cg, g_att, g_gla, g_conv = np.split(
            w["w_in"], np.cumsum([256, 256, 512, 1024, 32, 1024, 512, 1024, 1024, 1024, 1024, 1024]), axis=1)
        chunks = {"cy": tiles(w["w_conv_o"]), "r": tiles(r), "glr": none, "kt": none, "st": none,
                  "vg": [token_tiles(vg[:, j * 2 * P:(j + 1) * 2 * P]) for j in range(GH)]}

        def unit(kind, c):
            return none[0] if kind == "adt" else ada[c[0]][c[1]] if kind == "ada" else chunks[kind][c]
        for s in (CTX, LAT):
            if l == DEPTH - 1 and s == CTX:
                parts += [tiles(k), token_tiles(v), tiles(kg)] + chunks["vg"]
                continue
            parts += [paired(ca, cg), tiles(k), tiles(q), token_tiles(v), tiles(kg), tiles(qg)]
            parts += [unit(*u) for u in attention_fill(l, s)]
            parts += [paired(g_att, w["w_att_o"]), tiles(g_conv)]
            parts += [unit(*u) for step in gla_steps(l, s) for u in step]
            parts += [tiles(r)] * (s == CTX) + [tiles(g_gla), tiles(w["w_gla_o"])]
            beside = out_fill(l, s)
            for c, chunk in enumerate(tiles(w["w_out"])):
                parts += [chunk, unit(*beside[c]) if c in beside else none[0]]
            parts += [unit(*u) for u in norm_fill(l, s)]
            parts += half_tiles(w["w_ff_gate"], w["w_ff_up"], w["w_ff_down"])
    return [p.reshape(-1, P, P) for p in parts]


def second_stack_tiles(w):
    cq, ckv, kr, gb, gc, uc, up, qs, ks, vs = np.split(
        w["w_in"], np.cumsum([256, 128, 32, 256, 256, 256, 256, 256, 128]), axis=1)
    kr = np.pad(kr, ((0, 0), (NOPE, P - QK)))
    qs = qs.reshape(D, 2, 2, SHD).transpose(0, 2, 1, 3).reshape(D, SH * SHD)
    gate, upw = np.split(w["w_gate_up"], 2, axis=1)
    parts = [tiles(x) for x in (cq, ckv, kr, vs, uc, up, gc, gb, qs, ks, w["w_o"])] + half_tiles(gate, upw, w["w_down"])
    return [p.reshape(-1, P, P) for p in parts]


def columns(*vectors):
    return np.concatenate([v.reshape(-1, P).T for v in vectors], 1)


def constants():
    eye = np.eye(P, dtype=np.float32)
    c = {"ident": eye}
    for m in (1024, 256, 128):
        c[f"mean{m}"] = np.full((P, P), 1.0 / m, np.float32)
    rot = np.zeros((P, P), np.float32)
    rot[np.arange(1, P, 2), np.arange(0, P, 2)] = -1.0
    rot[np.arange(0, P, 2), np.arange(1, P, 2)] = 1.0
    c["rot"] = rot
    c["head128"] = np.concatenate([np.tile(np.eye(ROWS)[h], (P, 1)) / 128 for h in range(KVH + HEADS)], 1)
    c["head256"] = np.concatenate([np.tile(np.eye(ROWS)[h], (P, 1)) / 256 for h in range(4)], 1)
    c["pair"] = np.zeros((P, 2))
    c["pair"][[0, 2], 0] = c["pair"][[1, 3], 1] = 1.0
    c["alpha"] = np.tile([ALPHA, 1.0], (P, 1))
    t = np.arange(S)
    half = DH // 2
    inv = np.float32(10000.0) ** (-np.arange(0, half, 2, dtype=np.float32) / np.float32(half))
    ang = np.concatenate([(t // 64).astype(np.float32)[:, None] * inv, (t % 64).astype(np.float32)[:, None] * inv], -1)
    ang = np.repeat(ang.T, 2, 0).astype(np.float64)
    c["cos"], c["sin"] = np.cos(ang), np.sin(ang)
    const1 = np.concatenate([c[k] for k in CONST1], 1).astype(np.float32)

    d = {}
    rot = np.zeros((P, P), np.float32)
    h = ROPE // 2
    rot[NOPE + h + np.arange(h), NOPE + np.arange(h)] = -1.0
    rot[NOPE + np.arange(h), NOPE + h + np.arange(h)] = 1.0
    d["rot"] = rot
    inv = np.float32(1.0) / (np.float32(10000.0) ** (np.arange(0, ROPE, 2, dtype=np.float32) / np.float32(ROPE)))
    ang = (t.astype(np.float32)[:, None] * inv).astype(np.float64).T
    cos, sin = np.ones((P, S)), np.zeros((P, S))
    cos[NOPE:QK], sin[NOPE:QK] = np.concatenate([np.cos(ang)] * 2), np.concatenate([np.sin(ang)] * 2)
    d["cos"], d["sin"] = cos, sin
    count = np.ones((P, 2, S))
    for g, wdw in enumerate(POOLS):
        count[64 * (g % 2):64 * (g % 2) + 64, g // 2] = 1.0 / np.minimum(t + 1, wdw)
    d["inv_count"] = count.reshape(P, -1)
    q, k = t[:, None], t[None, :]
    d["causal"] = np.where(k <= q, 0.0, NEG).reshape(QT, P, S).transpose(1, 0, 2).reshape(P, -1)
    dist = q - k
    ok = (dist >= 0) & (dist < WINDOW)
    slopes = [2.0 ** (-8.0 * (i + 1) / SH) for i in range(SH)]
    d["window"] = np.stack([np.where(ok, -s * dist, NEG) for s in slopes]).reshape(SH, QT, P, S).transpose(2, 0, 1, 3).reshape(P, -1)
    const2 = np.concatenate([d[k] for k in CONST2], 1).astype(np.float32)

    j, i = np.arange(P)[:, None], np.arange(P)[None, :]
    masks = []
    for half in LEVELS[1:]:
        same = j // (2 * half) == i // (2 * half)
        left, right = j % (2 * half) < half, i % (2 * half) >= half
        masks += [same & left & right, (same & left & right).T]
    masks.append(i == j)
    return const1, const2, np.stack(masks, 1).astype(np.float32)


def kernel(**x):
    from concourse import bacc
    from concourse.bass_utils import run_bass_kernel_spmd

    x = {k: np.asarray(v) for k, v in x.items()}
    const1, const2, masks = constants()
    layers = [{k: x[k][l] for k in ("w_ada", "w_in", "w_conv_o", "w_att_o", "w_gla_o", "w_out", "w_ff_gate", "w_ff_up", "w_ff_down")}
              for l in range(DEPTH)]
    stream, glrs, vec1, a2 = first_stack_tiles(layers), [], [], np.zeros((GLR, DEPTH, GH * GDK), np.float32)
    for l in range(DEPTH):
        glr = np.zeros((D, GLR), np.float32)
        for d in range(2):
            col = 256 + 256 + 512 + 1024 + d * RANK
            glr[:, 32 * d:32 * d + RANK] = x["w_in"][l][:, col:col + RANK]
            a2[32 * d:32 * d + RANK, l] = x["gla_w_a2"][l, d]
        glrs.append(glr.reshape(KC, P, GLR).transpose(1, 0, 2).reshape(P, -1))
        conv_w = x["conv_w_dw"][l].reshape(TAPS, KC, P).transpose(2, 1, 0).reshape(P, -1)
        vec1.append(np.concatenate([columns(x["b_ada"][l], x["q_norm"][l], x["k_norm"][l], x["gla_b_a"][l], x["gla_norm"][l],
                                            x["conv_b_dw"][l], x["conv_ln_g"][l], x["conv_ln_b"][l], x["ln1_g"][l], x["ln1_b"][l],
                                            x["ln2_g"][l], x["ln2_b"][l]), conv_w], 1))
    vec2, small2 = [], []
    for l in range(DEPTH):
        stream += second_stack_tiles({"w_in": x["w_in_2"][l], "w_o": x["w_o_2"][l], "w_gate_up": x["w_gate_up_2"][l], "w_down": x["w_down_2"][l]})
        vec2 += [columns(x["attn_norm_2"][l], x["mla_q_norm_2"][l], x["mla_kv_norm_2"][l], x["conv_w_2"][l], x["pool_scale_2"][l],
                         x["mix_norm_2"][l], x["ffn_norm_2"][l]), np.broadcast_to(x["swa_sinks_2"][l], (P, SH))]
        pool = np.zeros((P, 2, P), np.float32)
        for g in range(4):
            r = 64 * (g % 2)
            pool[r:r + 64, g // 2, r:r + 64] = x["pool_w_2"][l, g]
        small2.append(np.concatenate([x["w_uq_2"][l].reshape(2, P, -1).transpose(1, 0, 2).reshape(P, -1), x["w_ukv_2"][l],
                                      pool.reshape(P, -1)], 1))
    vec2.append(columns(x["final_norm_2"]))
    stream.append(np.zeros(((LOADS - USED) * TILES, P, P), np.float32))
    both = np.concatenate([x["ctx"][0], x["x"][0]], 0)
    arrays = {
        "stream": np.concatenate(stream).reshape(LOADS, TILES, P, P).transpose(0, 2, 1, 3).reshape(LOADS, P, TILES * P),
        "tokens": both.T.reshape(KC, P, 2 * S).transpose(1, 0, 2),
        "cvec": np.stack([x["c_ctx"], x["c"][0]], 1).reshape(KC, P, 2).transpose(1, 0, 2),
        "vec1": np.stack(vec1, 1),
        "vec2": np.concatenate(vec2, 1),
        "w_glr": np.concatenate(glrs, 1),
        "w_a2": a2,
        "const1": const1, "const2": const2,
        "small2": np.stack(small2, 1),
        "masks": masks,
    }
    arrays = {k: np.ascontiguousarray(a) for k, a in arrays.items()}
    nc = bacc.Bacc("TRN2", target_bir_lowering=False, num_devices=1)
    args = [nc.dram_tensor(f"in_{k}", a.shape, mybir.dt.from_np(a.dtype), kind="ExternalInput").ap() for k, a in arrays.items()]
    out = nc.dram_tensor("out", (P, KC, S), mybir.dt.float32, kind="ExternalOutput").ap()
    program(nc, *args, out)
    r = run_bass_kernel_spmd(nc, [{f"in_{k}": a for k, a in arrays.items()}], core_ids=[0])
    got = np.asarray(r.results[0]["out"])
    return np.ascontiguousarray(got.transpose(2, 1, 0).reshape(1, S, D))
```
